# Optimizing a Trainium2 kernel written in Bass

```python
import math
import jax, jax.numpy as jnp
from jax import lax
import numpy as np

D_MODEL = 4096
BATCH = 1
SEQ = 256
DEPTH = 1
DEC_BATCH = 8
DEC_SEQ = 8
PAST_LEN = 2048
PAGE_SIZE = 128

W_A = D_MODEL // 4
W_B = D_MODEL // 2
W_C = D_MODEL // 4
MIX = W_A + W_B + W_C
CONV_A = 3
CONV_B = 4
LRU_HEADS = 16
LRU_HD = W_B // LRU_HEADS
LRU_C = 8.0
S5_GROUP = 16
S5_G = W_C // S5_GROUP
S5_P = 64
EPS = 1e-6
SPLITS = (W_A, W_A, W_A, W_A, W_B, W_B, W_C, W_C)
IN_COLS = 4 * W_A + 2 * W_B + 2 * W_C

kernel_name = "hybrid_conv_rglru_s5_decoder_step"

def _split_cols(z):
    out = []
    start = 0
    for w in SPLITS:
        out.append(z[..., start:start + w])
        start += w
    return out

def _rmsnorm(x, g):
    xf = x.astype(jnp.float32)
    y = xf * lax.rsqrt(jnp.mean(xf * xf, axis=-1, keepdims=True) + EPS)
    return (y * g.astype(jnp.float32)).astype(x.dtype)

def _causal_dwconv(buf, v, w, b):
    k_width = w.shape[0]
    t_len = v.shape[1]
    padded = jnp.concatenate([buf.astype(v.dtype), v], axis=1)
    y = b + sum(w[k] * padded[:, k:k + t_len] for k in range(k_width))
    return y, padded[:, t_len:]

def _real_combine(e1, e2):
    a1, b1 = e1
    a2, b2 = e2
    return a1 * a2, a2 * b1 + b2

def _complex_combine(e1, e2):
    ar1, ai1, br1, bi1 = e1
    ar2, ai2, br2, bi2 = e2
    return (ar2 * ar1 - ai2 * ai1,
            ar2 * ai1 + ai2 * ar1,
            ar2 * br1 - ai2 * bi1 + br2,
            ar2 * bi1 + ai2 * br1 + bi2)

def _layer(x, c, conv_a, conv_b, lru_h, s5_re, s5_im,
           g_norm, w_ada, b_ada, w_in, w_conv_a, b_conv_a, w_conv_b, b_conv_b,
           w_rg, b_rg, w_ig, b_ig, lru_lambda, s5_lambda_re, s5_lambda_im, s5_log_dt,
           s5_b_re, s5_b_im, s5_c_re, s5_c_im, s5_d, w_glu, b_glu, w_out):
    f32 = jnp.float32
    bn, t_len, _ = x.shape
    mod = c @ w_ada + b_ada
    shift, scale, gate = jnp.split(mod, 3, axis=-1)
    h = _rmsnorm(x, g_norm) * (1.0 + scale[:, None]) + shift[:, None]
    proj = h @ w_in
    a_b, a_c, a_x, a_g, b_x, b_g, c_u, c_g = _split_cols(proj)

    conv_in = a_c * a_x
    conv_out, conv_a_new = _causal_dwconv(conv_a, conv_in, w_conv_a, b_conv_a)
    out_a = a_b * conv_out * jax.nn.silu(a_g)

    xb, conv_b_new = _causal_dwconv(conv_b, b_x, w_conv_b, b_conv_b)
    xh = xb.reshape(bn, t_len, LRU_HEADS, LRU_HD)
    r = jax.nn.sigmoid(jnp.einsum('bthi,hij->bthj', xh, w_rg) + b_rg).reshape(bn, t_len, W_B)
    ig = jax.nn.sigmoid(jnp.einsum('bthi,hij->bthj', xh, w_ig) + b_ig).reshape(bn, t_len, W_B)
    log_a = -LRU_C * r.astype(f32) * jax.nn.softplus(-lru_lambda.astype(f32))
    a = jnp.exp(log_a)
    beta = jnp.sqrt(-jnp.expm1(2.0 * log_a))
    bt = beta * ig.astype(f32) * xb.astype(f32)
    bt = bt.at[:, 0].add(a[:, 0] * lru_h.astype(f32))
    _, hs = lax.associative_scan(_real_combine, (a, bt), axis=1)
    lru_h_new = hs[:, -1]
    out_b = hs.astype(x.dtype) * jax.nn.silu(b_g)

    dt = jnp.exp(s5_log_dt.astype(f32))[:, None]
    lre = s5_lambda_re.astype(f32)
    lim = s5_lambda_im.astype(f32)
    mag = jnp.exp(lre * dt)
    ab_re = mag * jnp.cos(lim * dt)
    ab_im = mag * jnp.sin(lim * dt)
    nr = ab_re - 1.0
    den = lre * lre + lim * lim
    fr = (nr * lre + ab_im * lim) / den
    fi = (ab_im * lre - nr * lim) / den
    bre = s5_b_re.astype(f32)
    bim = s5_b_im.astype(f32)
    bb_re = fr[..., None] * bre - fi[..., None] * bim
    bb_im = fr[..., None] * bim + fi[..., None] * bre
    u = c_u.reshape(bn, t_len, S5_G, S5_GROUP).astype(f32)
    bu_re = jnp.einsum('gpi,btgi->btgp', bb_re, u)
    bu_im = jnp.einsum('gpi,btgi->btgp', bb_im, u)
    h0r = s5_re.astype(f32)
    h0i = s5_im.astype(f32)
    bu_re = bu_re.at[:, 0].add(ab_re * h0r - ab_im * h0i)
    bu_im = bu_im.at[:, 0].add(ab_re * h0i + ab_im * h0r)
    ar = jnp.broadcast_to(ab_re, bu_re.shape)
    ai = jnp.broadcast_to(ab_im, bu_im.shape)
    _, _, hr, hi = lax.associative_scan(_complex_combine, (ar, ai, bu_re, bu_im), axis=1)
    s5_re_new = hr[:, -1]
    s5_im_new = hi[:, -1]
    y = (jnp.einsum('gip,btgp->btgi', s5_c_re.astype(f32), hr)
         - jnp.einsum('gip,btgp->btgi', s5_c_im.astype(f32), hi)
         + s5_d.astype(f32) * u).reshape(bn, t_len, W_C).astype(x.dtype)
    y = jax.nn.gelu(y)
    y = y * jax.nn.sigmoid(y @ w_glu + b_glu)
    out_c = y * jax.nn.silu(c_g)

    mixed = jnp.concatenate([out_a, out_b, out_c], axis=-1) @ w_out
    x = x + gate[:, None] * mixed
    return (x, conv_a_new, conv_b_new, lru_h_new.astype(x.dtype),
            s5_re_new.astype(x.dtype), s5_im_new.astype(x.dtype))

def setup_inputs(seed: int = 0) -> dict:
    key = jax.random.key(seed)
    ks = iter(jax.random.split(key, 40))
    f32 = jnp.float32
    nrm = lambda shape, s: jax.random.normal(next(ks), shape, f32) * s
    u_lru = jax.random.uniform(next(ks), (DEPTH, W_B), f32, 0.9, 0.999)
    log_dt = jax.random.uniform(next(ks), (DEPTH, S5_G), f32,
                                math.log(0.001), math.log(0.1))
    lam_im = jnp.broadcast_to(jnp.pi * jnp.arange(S5_P, dtype=f32), (DEPTH, S5_G, S5_P))
    return {
        "x_prompt": nrm((BATCH, SEQ, D_MODEL), 1.0),
        "x_sample": nrm((DEC_BATCH, DEC_SEQ, D_MODEL), 1.0),
        "c_prompt": nrm((BATCH, D_MODEL), 1.0),
        "c_sample": nrm((DEC_BATCH, D_MODEL), 1.0),
        "state_conv_a": nrm((DEPTH, DEC_BATCH, CONV_A - 1, W_A), 1.0),
        "state_conv_b": nrm((DEPTH, DEC_BATCH, CONV_B - 1, W_B), 1.0),
        "state_lru_h": nrm((DEPTH, DEC_BATCH, W_B), 0.5),
        "state_s5_re": nrm((DEPTH, DEC_BATCH, S5_G, S5_P), 0.5),
        "state_s5_im": nrm((DEPTH, DEC_BATCH, S5_G, S5_P), 0.5),
        "g_norm": 1.0 + nrm((DEPTH, D_MODEL), 0.02),
        "w_ada": nrm((DEPTH, D_MODEL, 3 * D_MODEL), 0.5 * D_MODEL ** -0.5),
        "b_ada": nrm((DEPTH, 3 * D_MODEL), 0.02),
        "w_in": nrm((DEPTH, D_MODEL, IN_COLS), D_MODEL ** -0.5),
        "w_conv_a": nrm((DEPTH, CONV_A, W_A), CONV_A ** -0.5),
        "b_conv_a": nrm((DEPTH, W_A), 0.02),
        "w_conv_b": nrm((DEPTH, CONV_B, W_B), CONV_B ** -0.5),
        "b_conv_b": nrm((DEPTH, W_B), 0.02),
        "w_rg": nrm((DEPTH, LRU_HEADS, LRU_HD, LRU_HD), LRU_HD ** -0.5),
        "b_rg": nrm((DEPTH, LRU_HEADS, LRU_HD), 0.02),
        "w_ig": nrm((DEPTH, LRU_HEADS, LRU_HD, LRU_HD), LRU_HD ** -0.5),
        "b_ig": nrm((DEPTH, LRU_HEADS, LRU_HD), 0.02),
        "lru_lambda": jnp.log(u_lru) - jnp.log1p(-u_lru),
        "s5_lambda_re": -0.5 + nrm((DEPTH, S5_G, S5_P), 0.01),
        "s5_lambda_im": lam_im + nrm((DEPTH, S5_G, S5_P), 0.01),
        "s5_log_dt": log_dt,
        "s5_b_re": nrm((DEPTH, S5_G, S5_P, S5_GROUP), (2.0 * S5_GROUP) ** -0.5),
        "s5_b_im": nrm((DEPTH, S5_G, S5_P, S5_GROUP), (2.0 * S5_GROUP) ** -0.5),
        "s5_c_re": nrm((DEPTH, S5_G, S5_GROUP, S5_P), (2.0 * S5_P) ** -0.5),
        "s5_c_im": nrm((DEPTH, S5_G, S5_GROUP, S5_P), (2.0 * S5_P) ** -0.5),
        "s5_d": nrm((DEPTH, S5_G, S5_GROUP), 1.0),
        "w_glu": nrm((DEPTH, W_C, W_C), W_C ** -0.5),
        "b_glu": nrm((DEPTH, W_C), 0.02),
        "w_out": nrm((DEPTH, MIX, D_MODEL), MIX ** -0.5),
        "g_final": 1.0 + nrm((D_MODEL,), 0.02),
    }

def reference(x_prompt, x_sample, c_prompt, c_sample,
              state_conv_a, state_conv_b, state_lru_h, state_s5_re, state_s5_im,
              g_norm, w_ada, b_ada, w_in, w_conv_a, b_conv_a, w_conv_b, b_conv_b,
              w_rg, b_rg, w_ig, b_ig, lru_lambda, s5_lambda_re, s5_lambda_im, s5_log_dt,
              s5_b_re, s5_b_im, s5_c_re, s5_c_im, s5_d, w_glu, b_glu, w_out, g_final):
    dt_p = x_prompt.dtype
    bp = x_prompt.shape[0]
    xp = x_prompt
    xs = x_sample
    p_ca, p_cb, p_h, p_re, p_im = [], [], [], [], []
    s_ca, s_cb, s_h, s_re, s_im = [], [], [], [], []
    for l in range(DEPTH):
        w_l = (g_norm[l], w_ada[l], b_ada[l], w_in[l], w_conv_a[l], b_conv_a[l],
               w_conv_b[l], b_conv_b[l], w_rg[l], b_rg[l], w_ig[l], b_ig[l],
               lru_lambda[l], s5_lambda_re[l], s5_lambda_im[l], s5_log_dt[l],
               s5_b_re[l], s5_b_im[l], s5_c_re[l], s5_c_im[l], s5_d[l],
               w_glu[l], b_glu[l], w_out[l])
        zp = (jnp.zeros((bp, CONV_A - 1, W_A), dt_p), jnp.zeros((bp, CONV_B - 1, W_B), dt_p),
              jnp.zeros((bp, W_B), dt_p), jnp.zeros((bp, S5_G, S5_P), dt_p),
              jnp.zeros((bp, S5_G, S5_P), dt_p))
        xp, ca, cb, hh, sr, si = _layer(xp, c_prompt, *zp, *w_l)
        p_ca.append(ca); p_cb.append(cb); p_h.append(hh); p_re.append(sr); p_im.append(si)
        xs, ca, cb, hh, sr, si = _layer(xs, c_sample, state_conv_a[l], state_conv_b[l],
                                        state_lru_h[l], state_s5_re[l], state_s5_im[l], *w_l)
        s_ca.append(ca); s_cb.append(cb); s_h.append(hh); s_re.append(sr); s_im.append(si)
    y_prompt = _rmsnorm(xp, g_final)
    y_sample = _rmsnorm(xs, g_final)
    return (y_prompt, y_sample,
            jnp.stack(p_ca), jnp.stack(p_cb), jnp.stack(p_h), jnp.stack(p_re), jnp.stack(p_im),
            jnp.stack(s_ca), jnp.stack(s_cb), jnp.stack(s_h), jnp.stack(s_re), jnp.stack(s_im))


_drawn_inputs = setup_inputs


def setup_inputs(seed=0):
    import zlib

    import numpy as np

    out = dict(_drawn_inputs(seed))
    spreads = {}
    factors = {'b_conv_a': 8.0,
     'b_rg': 8.0,
     'b_ig': 7.474,
     's5_lambda_re': 13.129,
     'b_glu': 64.0,
     'g_final': 7.939,
     's5_c_re': 2.771,
     's5_c_im': 2.7}
    for name, (base, spread) in spreads.items():
        noise = np.random.default_rng([zlib.crc32(name.encode()), seed]).standard_normal(out[name].shape)
        drawn = base * np.exp(spread * noise) if base else spread * noise
        out[name] = __import__('jax').numpy.asarray(drawn.astype(out[name].dtype))
    for name, factor in factors.items():
        out[name] = (out[name] * factor).astype(out[name].dtype)
    return out
```

```python
from contextlib import ExitStack

import concourse.bass as bass
import numpy as np
from concourse import mybir

F32 = mybir.dt.float32
F32R = mybir.dt.float32r
ALU = mybir.AluOpType
ACT = mybir.ActivationFunctionType

P = 128
D = 4096
KT = D // P
TP, DB, DS = 256, 8, 8
T = TP + DB * DS
W_A, W_B, W_C = D // 4, D // 2, D // 4
S5_P, S5_I = 64, 16
EPS = 1e-6

COLS = 512
SLAB = 2 * COLS
BLK = COLS // P
SPG = KT // 2
AHEAD = 3
RING = 4
N_U, N_A, N_G, N_B, N_O = 4, 8, 2, 8, 8
SLAB_U = 0
SLAB_A = SLAB_U + N_U * SPG
SLAB_G = SLAB_A + N_A * SPG
SPGG = W_C // P // 2
SLAB_B = SLAB_G + N_G * SPGG
SLAB_O = SLAB_B + N_B * SPG
SLABS = SLAB_O + N_O * SPG
ADA_J = 8

SW = TP + DB * (DS + 1)
PA = 2 + TP + DB * (DS + 2)
PB = 3 + TP + DB * (DS + 3)
XW = PB - 3

C_BADA, C_G, C_WCA, C_BCA, C_WCB, C_BCB = 0, 96, 128, 152, 160, 224
C_BRG, C_BIG, C_LAM, C_BGLU, C_S5D, C_GF = 240, 256, 272, 288, 296, 304
N_PAR = 336
NST = 32
REP = 8 * P + NST + 8

TWO_PI = 6.283185307179586
PI_1 = 6.28125
PI_2 = 2029.0 / 2**20
PI_3 = TWO_PI - PI_1 - PI_2
ROUND = 12582912.0
NEAR_PI = 3.1415925


class Tally:

    def __init__(self, sem):
        self.sem, self.base, self.local = sem, 0, 0

    def up(self, ins):
        ins.then_inc(self.sem, 1)
        self.local += 1
        return ins

    def now(self):
        return self.base + self.local

    def enter(self, i, per):
        self.start, self.per = self.now(), per
        self.base, self.local = self.start + i * per, 0

    def leave(self, n):
        assert self.local == self.per, (self.sem.name, self.local, self.per)
        self.base, self.local = self.start + n * self.per, 0


def build(nc, a):
    ctx = ExitStack()
    with ctx:
        def sem(name):
            return ctx.enter_context(nc.semaphore(name))

        ORIGIN, WORDS = 16512, 53208

        def at(name, off, *shape, dt=F32):
            n = int(np.prod(shape))
            assert off + n <= WORDS, name
            t = nc.alloc_sbuf_tensor_at(name, [P, *shape], dt, offset=ORIGIN + 4 * off)
            return t

        o = 0

        def take(n):
            nonlocal o
            start = o
            o += -(-n // 8) * 8
            return start

        NC_ = 8 * SW
        o_act = take(NC_ + 24 * T)
        o_h = take(2 * KT * T)
        o_raw = take(RING * SLAB)
        o_w = take(2 * RING * SLAB)
        X = at("x", o_act, KT, T)
        ACTS = at("acts", o_act, NC_ + 24 * T)
        H_HI = at("h_hi", o_h, KT, T, dt=F32R)
        H_LO = at("h_lo", o_h + KT * T, KT, T, dt=F32R)
        RAW = at("w_raw", o_raw, RING, SLAB)
        W_HI = at("w_hi", o_w, RING, 2, COLS, dt=F32R)
        W_LO = at("w_lo", o_w + RING * SLAB, RING, 2, COLS, dt=F32R)
        ADA = at("ada_ring", o_w, 2 * RING, 2, COLS)
        CT = at("c_T", take(KT * 32), KT, 32)
        PAR = at("par", take(N_PAR), N_PAR)
        SELONES = at("sel_ones", take(9 + P), 9 + P)
        SEL, ONES = SELONES[:, 0:9], SELONES[:, 9:9 + P]
        o_s5h0 = take(512)
        S5H0 = at("s5_h0", o_s5h0, NST, 2, DB)
        CBST = at("convb_state", take(384), 16, DB, 3)
        LRU0 = at("lru_h0", take(128), 16, DB)
        CAST = at("conva_state", take(128), 8, DB, 2)
        MOD = at("mod", take(108), 3, BLK, 9)
        MAGF = at("s5_mag_turn", take(80), 2, NST + 8)
        TURN = at("s5_turn", take(1), 1)
        EPSC = at("eps", take(1), 1)
        NEG8SP = at("neg8softplus", take(16), 16)
        STG_A = at("stage_a", take(72), BLK, 9, 2)
        STG_B = at("stage_b", take(108), BLK, 9, 3)
        STG_H = at("stage_h", take(36), BLK, 9)
        STG_S = at("stage_s", take(72), BLK, 2, 9)
        s = o
        T0 = [at(f"s5t{i}", o_h + REP * i, REP) for i in range(14)]
        SPT = at("softplus_tmp", s + 2048, 4, 16)
        SQ = at("x_sq", o_h + 14 * REP, 2, 4 * T)
        SQA = at("x_sqa", o_h + 14 * REP + 8 * T, 4 * T)
        BB = at("s5_bb", s, 8, 2, P)
        CC = at("s5_cc", s + 2048, 2, BLK, 32)
        BBU = at("s5_bb_unit", s + 2304, 2, P)
        MASK = at("s5_mask", s + 2560, SW)
        STEP = at("s5_step", s + 2888, SW)
        RSTD = at("rstd", s + 3216, T)
        HT = at("h_tmp", s + 3536, BLK, T)
        ACCS = at("ada_acc", s + 4816, COLS)
        COEF = at("s5_coef", s + 3216, SW)
        TMPD = at("s5_tmpd", s + 3544, SW)
        TMPP = at("s5_tmpp", s + 3872, SW)
        HRI = at("s5_h", s + 4200, 2, SW)
        o_b = o_act + NC_ + 8 * T
        o_s5 = o_b + NC_
        SG = at("silu_c", o_b, 8, SW)
        UU = at("s5_u_unit", s + 5184, SW)
        TCOS = [at("cos0", o_s5, SW), at("cos1", o_s5 + SW, SW)]
        TSIN = [at("sin0", o_s5 + 2 * SW, SW), at("sin1", s + 4856, SW)]
        Q = [at("q0", o_s5 + 3 * SW, 2, SW), at("q1", o_s5 + 5 * SW, 2, SW)]
        assert 7 * SW + NC_ <= 16 * T
        o_pad = (WORDS - 4 * PA) // 8 * 8
        assert o_pad >= s + 5184 + SW
        PADA = at("pad_a", o_pad, BLK, PA)
        TMPA = at("tmp_a", o_pad, BLK, T)
        Y_HI = at("y_hi", s, 8, SW, dt=F32R)
        Y_LO = at("y_lo", s + NC_, 8, SW, dt=F32R)
        ZG = at("z_glu", o_pad, BLK, SW)
        WG = at("w_gates", s, BLK, 2, P)
        PADB = at("pad_b", s + 1024, BLK, PB)
        SGB = at("silu_b", s + 1024, BLK, T)
        XB = at("xb", s + 2416, BLK, XW)
        R = at("lru_r", s + 3792, 2, XW)
        IG = at("lru_i", s + 4480, 2, XW)
        AA = at("lru_a", s + 5168, 2, XW)
        TH = at("lru_t", s + 5856, 2, XW)
        ADA2 = at("gate_ring", s, RING, 2, COLS)
        OT = at("out_tmp", s + 4096, BLK, T)
        SQO = at("y_sq", s + 5376, 2, T)
        SQS = at("y_sqs", s + 6016, T)
        RST2 = at("rstd2", s + 6336, T)
        ACC2 = at("gate_acc", o_s5h0, COLS)

        CST = ACTS[:, 0:NC_].rearrange("p (n w) -> p n w", w=SW)
        CSTS = CST[:, :, TP:SW].rearrange("p n (s w) -> p n s w", w=DS + 1)
        AROW = ACTS[:, NC_:NC_ + 8 * T].rearrange("p (n w) -> p n w", w=T)
        AROWS = AROW[:, :, TP:T].rearrange("p n (s w) -> p n s w", w=DS)
        BROW = ACTS[:, NC_ + 8 * T:NC_ + 24 * T].rearrange("p (n w) -> p n w", w=T)
        BROWS = BROW[:, :, TP:T].rearrange("p n (s w) -> p n s w", w=DS)
        SGS = SG[:, :, TP:SW].rearrange("p n (s w) -> p n s w", w=DS + 1)
        PADAS = PADA[:, :, 2 + TP:PA].rearrange("p n (s w) -> p n s w", w=DS + 2)
        PADBS = PADB[:, :, 3 + TP:PB].rearrange("p n (s w) -> p n s w", w=DS + 3)
        XS = X[:, :, TP:T].rearrange("p n (s w) -> p n s w", w=DS)
        HTS = HT[:, :, TP:T].rearrange("p n (s w) -> p n s w", w=DS)
        OTS = OT[:, :, TP:T].rearrange("p n (s w) -> p n s w", w=DS)

        M = ctx.enter_context(nc.psum_tensor("m", [P, BLK, 512], F32))
        A0 = [ctx.enter_context(nc.psum_tensor(f"aux{i}", [P, 512], F32)) for i in range(4)]
        MS = M[:, :, TP:T].rearrange("p n (s w) -> p n s w", w=DS)

        small_in, x_in, s5_in = sem("small_in"), sem("x_in"), sem("s5_in")
        w_landed = [sem(f"w_landed{i}") for i in range(RING)]
        ada_landed = [sem(f"ada_landed{i}") for i in range(2 * RING)]
        gate_landed = [sem(f"gate_landed{i}") for i in range(RING)]
        ada_used, gate_used = sem("ada_used"), sem("gate_used")
        w_hi_done, w_lo_done, slab_done, bank_done, bank_free = map(
            sem, ["w_hi_done", "w_lo_done", "slab_done", "bank_done", "bank_free"])
        sq_done, sqa_done, sum_done, root_done, rstd_done = map(
            sem, ["sq_done", "sqa_done", "sum_done", "root_done", "rstd_done"])
        acc_done, acc_out, sel_done, ht_done, h_hi_done, h_lo_done = map(
            sem, ["acc_done", "acc_out", "sel_done", "ht_done", "h_hi_done", "h_lo_done"])
        s5_act, s5_dve, bb_ready, strips_ready = map(sem, ["s5_act", "s5_dve", "bb_ready", "strips_ready"])
        frac_done, table_done, coef_done, bbu_ready, cc_in, cc_ready = map(
            sem, ["frac_done", "table_done", "coef_done", "bbu_ready", "cc_in", "cc_ready"])
        bu_done, bu_used, q_done, hs5_done, y_done, y_sum, staged_s, out_s = map(
            sem, ["bu_done", "bu_used", "q_done", "hs5_done", "y_done", "y_sum", "staged_s", "out_s"])
        pada_ready, conva_done, ab_done, ag_done, out_a = map(
            sem, ["pada_ready", "conva_done", "ab_done", "ag_done", "out_a"])
        gelu_done, y_hi_done, y_lo_done, z_used = map(sem, ["gelu_done", "y_hi_done", "y_lo_done", "z_used"])
        wg_in, padb_ready, xb_ready, gates_done, gates_used, root_in, roots, hs_done, hs_out, lru_staged = map(
            sem, ["wg_in", "padb_ready", "xb_ready", "gates_done", "gates_used", "root_in", "roots", "hs_done",
                  "hs_out", "lru_staged"])
        out_b, bg_done, convb_staged = sem("out_b"), sem("bg_done"), sem("convb_staged")
        mix_hi_done, mix_lo_done, x_back, gacc_done, gacc_out, gsel_done, gmod_done = map(
            sem, ["mix_hi_done", "mix_lo_done", "x_back", "gacc_done", "gacc_out", "gsel_done", "gmod_done"])
        y_done2, ysq_done, ysum_done, yroot, rstd2_done, fin_dve, fin_pool, out_y = map(
            sem, ["res_done", "ysq_done", "ysum_done", "yroot", "rstd2_done", "fin_dve", "fin_pool", "out_y"])
        ysq_used, lru_act, staged_a, c_done, fin_act = map(sem, ["ysq_used", "lru_act", "staged_a", "c_done", "fin_act"])
        pe_tail, pool_passed, act_passed = sem("pe_tail"), sem("pool_passed"), sem("act_passed")
        act_step, dve_step, pool_step = Tally(sem("act_step")), Tally(sem("dve_step")), Tally(sem("pool_step"))

        from_one = [ht_done, h_hi_done, h_lo_done, sel_done, slab_done, bu_used, y_sum, gates_used,
                    hs_out, lru_staged, gates_done, bg_done, ag_done, y_done, q_done, bu_done,
                    y_done2, ysq_used, gmod_done]

        block = ctx.enter_context(nc.Block())
        FIN_DVE = 6

        @block.sync
        def _(sp):
            for one in from_one:
                sp.sem_inc(one, 1)
            for n in range(2 * RING):
                sp.dma_start(ADA[:, n], a["ada"][n]).then_inc(ada_landed[n], 16)
            with sp.Fori(1, 2 * ADA_J * SPG // (2 * RING)) as r:
                for n in range(2 * RING):
                    sp.wait_ge(ada_used, r * 2 * RING + n + 1 - 2 * RING)
                    sp.dma_start(ADA[:, n], a["ada"][r * 2 * RING + n]).then_inc(ada_landed[n], 16)
            for n in range(RING):
                sp.dma_start(RAW[:, n], a["w"][n]).then_inc(w_landed[n], 16)
            with sp.Fori(1, SLAB_O // RING + 1) as r:
                for n in range(RING):
                    sp.wait_ge(w_lo_done, r * RING + n + 1 - RING)
                    sp.dma_start(RAW[:, n], a["w"][r * RING + n]).then_inc(w_landed[n], 16)
            sp.wait_ge(bg_done, 4 + 1)
            sp.wait_ge(lru_staged, 8 + 1)
            sp.wait_ge(convb_staged, 4)
            for n in range(RING):
                sp.dma_start(ADA2[:, n], a["ada"][2 * ADA_J * SPG + n]).then_inc(gate_landed[n], 16)
            with sp.Fori(0, N_O * SPG // RING - 1) as r:
                for n in range(RING):
                    sp.wait_ge(w_lo_done, SLAB_O + r * RING + n + 1)
                    sp.dma_start(RAW[:, n], a["w"][SLAB_O + (r + 1) * RING + n]).then_inc(w_landed[n], 16)
                    sp.wait_ge(gate_used, r * RING + n + 1)
                    sp.dma_start(ADA2[:, n], a["ada"][2 * ADA_J * SPG + (r + 1) * RING + n]).then_inc(
                        gate_landed[n], 16)
            for g in range(FIN_DVE):
                sp.wait_ge(fin_dve, g + 1)
                sp.dma_start(a["y"][g], X[:, 4 * g:4 * g + 4]).then_inc(out_y, 16)
            for g in range(FIN_DVE, ADA_J):
                sp.wait_ge(fin_act, g + 1 - FIN_DVE)
                sp.dma_start(a["y"][g], X[:, 4 * g:4 * g + 4]).then_inc(out_y, 16)
            sp.wait_ge(out_y, 16 * ADA_J)
            sp.wait_ge(out_s, 16 * 8)
            sp.wait_ge(out_a, 16 * 2)
            sp.wait_ge(out_b, 32 * 4)

        @block.tensor
        def _(pe):
            mm = nc.tensor.matmul

            def slab(nb, c, nk, q, hi, lo, width):
                pe.wait_ge(w_lo_done, nb + c + 1)
                s_ = c % RING
                for b in range(BLK):
                    if c == 0:
                        pe.wait_ge(bank_free, 4 * q + b + 1)
                    for kk in range(2):
                        k = 2 * c + kk
                        w_hi = W_HI[:, s_, kk, b * P:(b + 1) * P]
                        w_lo = W_LO[:, s_, kk, b * P:(b + 1) * P]
                        out = M[:, b, 0:width]
                        mm(out, w_hi, hi[:, k, :], start=k == 0, stop=False)
                        mm(out, w_hi, lo[:, k, :], start=False, stop=False)
                        last = mm(out, w_lo, hi[:, k, :], start=False, stop=k == nk - 1)
                    if k == nk - 1 and b < BLK - 1:
                        last.then_inc(bank_done, 1)
                last.then_inc(slab_done, 1)

            pe.wait_ge(small_in, 16 * 7)
            pe.wait_ge(sqa_done, 8)
            for i in range(4):
                last = mm(A0[3][:, 0:T], ONES, SQA[:, i * T:(i + 1) * T], start=i == 0, stop=i == 3)
            last.then_inc(sum_done, 1)
            with pe.Fori(0, ADA_J) as j:
                for part in range(2):
                    for sl in range(SPG):
                        pe.wait_ge(ada_landed[sl % 8], 64 * j + 32 * part + 16 * (sl // 8 + 1))
                        for kk in range(2):
                            k = 2 * sl + kk
                            r = 32 * (k % 4)
                            last = mm(A0[part][r:r + 32, :], CT[:, k, :], ADA[:, sl % 8, kk, :], start=k < 4,
                                      stop=k >= KT - 4)
                        last.then_inc(ada_used, 1)
                    pe.wait_ge(acc_out, 2 * j + part + 1)
                    pe.wait_ge(ht_done, j + 1)
                    if part == 0:
                        pe.wait_ge(rstd_done, 1)
                    for b in range(BLK):
                        last = mm(A0[2 + part][:, 9 * b:9 * b + 9], ACCS[:, b * P:(b + 1) * P], SEL, start=True,
                                  stop=True)
                    last.then_inc(sel_done, 1)

            with pe.Fori(0, N_U) as g:
                for c in range(SPG):
                    if c % 2 == 0:
                        pe.wait_ge(h_lo_done, c // 2 + 1 + 1)
                    slab(SLAB_U + g * SPG, c, KT, g, H_HI, H_LO, T)

            with pe.Fori(0, N_A) as u:
                for c in range(SPG):
                    slab(SLAB_A + u * SPG, c, KT, N_U + u, H_HI, H_LO, T)
                    if c in (0, 3, 6, 9):
                        j = c // 3
                        if j == 0:
                            pe.wait_ge(bbu_ready, u + 1)
                        pe.wait_ge(bu_used, 4 * u + j + 1)
                        r = slice(32 * j, 32 * j + 32)
                        mm(A0[0][:, 0:SW], BBU[r, 0, :], UU[r, :], start=True, stop=True)
                        mm(A0[1][:, 0:SW], BBU[r, 1, :], UU[r, :], start=True, stop=True).then_inc(bu_done, 1)
                    if c in (6, 9, 12, 15):
                        j = c // 3 - 2
                        if j == 0:
                            pe.wait_ge(cc_ready, u + 1)
                            pe.wait_ge(y_sum, u + 1)
                        pe.wait_ge(hs5_done, 4 * u + j + 1)
                        r = slice(32 * j, 32 * j + 32)
                        mm(A0[2][r, 0:SW], CC[:, 0, j, :], HRI[:, 0, :], start=True, stop=False)
                        mm(A0[2][r, 0:SW], CC[:, 1, j, :], HRI[:, 1, :], start=False, stop=True).then_inc(y_done, 1)

            with pe.Fori(0, N_G) as g:
                for c in range(SPGG):
                    pe.wait_ge(y_lo_done, c + 1)
                    slab(SLAB_G + g * SPGG, c, 8, N_U + N_A + g, Y_HI, Y_LO, SW)

            with pe.Fori(0, N_B // 2) as i:
                for g in range(2):
                    for c in range(SPG):
                        slab(SLAB_B + (2 * i + g) * SPG, c, KT, N_U + N_A + N_G + 2 * i + g, H_HI, H_LO, T)
                        if g == 1 and c in (5, 11):
                            pr = c // 6
                            if pr == 0:
                                pe.wait_ge(wg_in, 16 * (i + 1))
                            pe.wait_ge(xb_ready, 2 * i + pr + 1)
                            pe.wait_ge(gates_used, 2 * i + pr + 1)
                            for hd in range(2):
                                for w in range(2):
                                    last = mm(A0[2 * w + hd][:, 0:XW], WG[:, 2 * pr + hd, w, :],
                                              XB[:, 2 * pr + hd, :], start=True, stop=True)
                            last.then_inc(gates_done, 1)

            per = [2] * 4 + [1] * 8 + [0] * 4
            with pe.Fori(0, N_O) as j:
                n = 0
                for c in range(SPG):
                    if c % 2 == 0:
                        pe.wait_ge(mix_lo_done, c // 2 + 1)
                    slab(SLAB_O + j * SPG, c, KT, N_U + N_A + N_G + N_B + j, H_HI, H_LO, T)
                    for _ in range(per[c]):
                        pe.wait_ge(gate_landed[n % RING], 64 * j + 16 * (n // RING + 1))
                        for kk in range(2):
                            k = 2 * n + kk
                            r = 32 * (k % 4)
                            last = mm(A0[0][r:r + 32, :], CT[:, k, :], ADA2[:, n % RING, kk, :], start=k < 4,
                                      stop=k >= KT - 4)
                        last.then_inc(gate_used, 1)
                        n += 1
                    if c == 13:
                        pe.wait_ge(gacc_out, j + 1)
                        pe.wait_ge(gmod_done, j + 1)
                        for b in range(BLK):
                            last = mm(A0[1][:, 9 * b:9 * b + 9], ACC2[:, b * P:(b + 1) * P], SEL, start=True,
                                      stop=True)
                        last.then_inc(gsel_done, 1)
            pe.wait_ge(ysq_used, 32 + 1)
            mm(A0[2][:, 0:T], ONES, SQS[:], start=True, stop=True).then_inc(pe_tail, 1)

        @block.scalar
        def _(act):
            fn = nc.scalar.activation
            st = act_step

            def then(ins):
                st.up(ins)
                act.wait_ge(st.sem, st.now())

            def hi(nb, c, first=False):
                act.wait_ge(w_landed[c % RING], 4 * nb + 16 * (c // RING + 1))
                if not first:
                    act.wait_ge(slab_done, nb + c + 1 - RING + 1)
                fn(W_HI[:, c % RING], RAW[:, c % RING].rearrange("p (k n) -> p k n", k=2), ACT.Copy).then_inc(
                    w_hi_done, 1)

            def bank_ready(q, b, nb_next):
                if b < BLK - 1:
                    act.wait_ge(bank_done, 3 * q + b + 1)
                else:
                    act.wait_ge(slab_done, nb_next + 1)

            act.dma_start(X[:], a["x"]).then_inc(x_in, 16)
            for dst, name in ((CT, "c"), (PAR, "par"), (SELONES, "sel_ones"), (S5H0, "s5h0"), (CBST, "cb"),
                              (LRU0, "lru"), (CAST, "ca")):
                act.dma_start(dst[:], a[name]).then_inc(small_in, 16)
            for i in range(3):
                act.dma_start(T0[i][:], a["rep"][:, i, :]).then_inc(s5_in, 16)
            for i in range(2):
                act.dma_start(T0[3 + i][:, 0:8 * P], a["s5b"][:, i, :]).then_inc(s5_in, 16)
            act.dma_start(MASK[:], a["mask"]).then_inc(s5_in, 16)
            act.dma_start(STEP[:], a["step"]).then_inc(s5_in, 16)

            act.wait_ge(x_in, 16)
            for i in range(8):
                if i >= 2:
                    act.wait_ge(sqa_done, i - 1)
                fn(SQ[:, i % 2, :], X[:, 4 * i:4 * i + 4, :].rearrange("p k t -> p (k t)"),
                   ACT.Square).then_inc(sq_done, 1)
            act.wait_ge(sum_done, 1)
            act.wait_ge(s5_dve, 1)
            fn(RSTD[:], A0[3][:, 0:T], ACT.Sqrt, scale=1.0 / D, bias=EPSC[:]).then_inc(root_done, 1)

            act.wait_ge(s5_in, 16 * 7)
            fn(T0[2][:], T0[2][:], ACT.Exp).then_inc(s5_act, 1)
            act.wait_ge(s5_dve, 2)
            fn(T0[6][:], T0[6][:], ACT.Exp).then_inc(s5_act, 1)
            act.wait_ge(small_in, 16 * 7)
            act.wait_ge(s5_dve, 3)
            fn(NEG8SP[:], NEG8SP[:], ACT.Exp).then_inc(s5_act, 1)
            act.wait_ge(s5_dve, 4)
            fn(T0[7][:], T0[5][:], ACT.Sin).then_inc(s5_act, 1)
            fn(T0[8][:], T0[5][:], ACT.Sin, scale=0.5).then_inc(s5_act, 1)

            with act.Fori(0, ADA_J) as j:
                for part in range(2):
                    act.wait_ge(ada_used, 32 * j + 16 * (part + 1))
                    act.wait_ge(sel_done, 2 * j + part + 1)
                    fn(ACCS[:], A0[part][:], ACT.Copy).then_inc(acc_out, 1)
                act.wait_ge(bb_ready, 1)
                act.wait_ge(ht_done, j + 1 + 1)
                fn(H_HI[:, bass.ds(4 * j, 4), :], HT[:], ACT.Copy).then_inc(h_hi_done, 1)

            act.wait_ge(ada_used, 2 * ADA_J * SPG)
            for c in range(AHEAD):
                hi(0, c, first=True)
            with act.Fori(0, 2) as g:
                nb = SLAB_U + g * SPG
                for c in range(AHEAD, AHEAD + SPG):
                    hi(nb, c)
                for b in range(BLK):
                    bank_ready(g, b, nb + SPG)
                    if b == 0:
                        act.wait_ge(strips_ready, 1)
                    fn(CST[:, 4 * g + b, 0:TP], M[:, b, 0:TP], ACT.Copy)
                    fn(CSTS[:, 4 * g + b, :, 1:], MS[:, b], ACT.Copy).then_inc(bank_free, 1)
            with act.Fori(0, 2) as g:
                nb = SLAB_U + (2 + g) * SPG
                for c in range(AHEAD, AHEAD + SPG):
                    hi(nb, c)
                for b in range(BLK):
                    bank_ready(2 + g, b, nb + SPG)
                    fn(SG[:, 4 * g + b, 0:TP], M[:, b, 0:TP], ACT.Silu)
                    fn(SGS[:, 4 * g + b, :, 1:], MS[:, b], ACT.Silu).then_inc(bank_free, 1)

            def tables(par, tile):
                act.wait_ge(frac_done, tile + 1)
                then(fn(TCOS[par][:], TSIN[par][:], ACT.Sin, scale=TWO_PI / 2))
                then(fn(TCOS[par][:], TCOS[par][:], ACT.Square))
                fn(TCOS[par][:], TCOS[par][:], ACT.Copy, scale=-2.0, bias=1.0)
                fn(TSIN[par][:], TSIN[par][:], ACT.Sin, scale=TWO_PI).then_inc(table_done, 1)

            tables(0, 0)
            with act.Fori(0, 2) as h:
                st.enter(h, 32)
                for m in range(4):
                    u = 4 * h + m
                    nb = SLAB_A + u * SPG
                    q = N_U + u
                    for c in range(AHEAD, AHEAD + SPG):
                        hi(nb, c)
                        if c == 3:
                            act.wait_ge(bu_done, 4 * u + 1)
                            fn(UU[:], CST[:, u, :], ACT.Copy)
                            fn(BBU[:], BB[:, u], ACT.Copy).then_inc(bbu_ready, 1)
                        if c == 5:
                            act.wait_ge(cc_in, 16 * (u + 1))
                            fn(CC[:, 1], CC[:, 1], ACT.Copy, scale=-1.0).then_inc(cc_ready, 1)
                        if c in (3, 6, 9, 12):
                            j = c // 3 - 1
                            act.wait_ge(q_done, 4 * u + j + 1)
                            fn(COEF[:], MASK[:], ACT.Copy, scale=MAGF[:, 0, bass.ds(4 * u + j, 1)]).then_inc(
                                coef_done, 1)
                        if c in (6, 9, 12, 15):
                            j = c // 3 - 2
                            tables((j + 1) % 2, 4 * u + j + 1)
                    for b in range(BLK):
                        if b == 0 and m == 0:
                            act.wait_ge(pada_ready, h + 1)
                        if b == 0 and m == 2:
                            act.wait_ge(conva_done, h + 1)
                            act.wait_ge(staged_a, h + 1)
                        if b == 0 and m == 3:
                            act.wait_ge(ab_done, h + 1)
                        bank_ready(q, b, nb + SPG)
                        if m == 0:
                            fn(PADA[:, b, 2:2 + TP], M[:, b, 0:TP], ACT.Copy)
                            fn(PADAS[:, b, :, 2:], MS[:, b], ACT.Copy).then_inc(bank_free, 1)
                        elif m == 1:
                            fn(AROW[:, 4 * h + b, :], M[:, b, 0:T], ACT.Copy).then_inc(bank_free, 1)
                        else:
                            fn(TMPA[:, b, :], M[:, b, 0:T], ACT.Copy if m == 2 else ACT.Silu).then_inc(bank_free, 1)
                    act.wait_ge(y_sum, u + 1 + 1)
                    act.sem_inc(act_passed, 1)
                    fn(CST[:, u, :], CST[:, u, :], ACT.Gelu_apprx_tanh).then_inc(gelu_done, 1)
            st.leave(2)

            act.wait_ge(gelu_done, 8)
            act.wait_ge(y_done, 32 + 1)
            act.wait_ge(staged_s, 8)
            act.wait_ge(frac_done, 34)
            for i in range(4):
                fn(Y_HI[:, 2 * i:2 * i + 2, :], CST[:, 2 * i:2 * i + 2, :], ACT.Copy).then_inc(y_hi_done, 1)
            for c in range(AHEAD, AHEAD + 2 * SPGG):
                hi(SLAB_G, c)
                if c in (6, 10):
                    g = (c - 6) // 4
                    for b in range(BLK):
                        if b == 0 and g == 0:
                            act.wait_ge(ag_done, 2 + 1)
                        if b == 0 and g == 1:
                            act.wait_ge(z_used, 1)
                        bank_ready(N_U + N_A + g, b, SLAB_G + 4 * (g + 1))
                        n = 4 * g + b
                        fn(ZG[:, b, :], M[:, b, 0:SW], ACT.Sigmoid, bias=PAR[:, C_BGLU + n:C_BGLU + n + 1]).then_inc(
                            bank_free, 1)

            def rows_out(i, pr):
                act.wait_ge(hs_done, 2 * i + pr + 1)
                for hd in range(2):
                    n = 4 * i + 2 * pr + hd
                    fn(BROW[:, n, 0:TP], R[:, hd, 0:TP], ACT.Copy)
                    last = fn(BROWS[:, n], R[:, hd, TP:XW].rearrange("p (s w) -> p s w", w=DS + 3)[:, :, 3:], ACT.Copy)
                last.then_inc(hs_out, 1)

            with act.Fori(0, 4) as i:
                for g in range(2):
                    nb = SLAB_B + (2 * i + g) * SPG
                    q = N_U + N_A + N_G + 2 * i + g
                    for c in range(AHEAD, AHEAD + SPG):
                        hi(nb, c)
                        if g == 1 and c in (9, 15):
                            pr = c // 15
                            act.wait_ge(gates_done, 2 * i + pr + 1 + 1)
                            act.wait_ge(hs_out, 2 * i + pr + 1)
                            act.wait_ge(lru_staged, 2 * i + pr + 1)
                            for w, buf, col in ((0, R, C_BRG), (1, IG, C_BIG)):
                                for hd in range(2):
                                    last = fn(buf[:, hd, :], A0[2 * w + hd][:, 0:XW], ACT.Sigmoid,
                                              bias=PAR[:, bass.ds(col + 4 * i + 2 * pr + hd, 1)])
                            last.then_inc(gates_used, 1)
                            act.wait_ge(gates_used, 2 * i + pr + 1 + 1)
                            for hd in range(2):
                                n8 = NEG8SP[:, bass.ds(4 * i + 2 * pr + hd, 1)]
                                fn(AA[:, hd, :], R[:, hd, :], ACT.Exp, scale=n8)
                                last = fn(TH[:, hd, :], R[:, hd, :], ACT.Tanh, scale=n8)
                            last.then_inc(lru_act, 1)
                            act.wait_ge(lru_act, 4 * i + 2 * pr + 1)
                            fn(R[:], AA[:], ACT.Square).then_inc(lru_act, 1)
                        if g == 1 and c in (12, 17):
                            pr = c // 17
                            act.wait_ge(root_in, 2 * i + pr + 1)
                            fn(TH[:], TH[:], ACT.Sqrt, scale=-1.0).then_inc(roots, 1)
                        if g == 1 and c == 14:
                            rows_out(i, 0)
                    for b in range(BLK):
                        if b == 0 and g == 0:
                            act.wait_ge(padb_ready, i + 1)
                        if b == 0 and g == 1:
                            act.wait_ge(convb_staged, i + 1)
                            act.wait_ge(xb_ready, 2 * i + 2)
                        bank_ready(q, b, nb + SPG)
                        if g == 0:
                            fn(PADB[:, b, 3:3 + TP], M[:, b, 0:TP], ACT.Copy)
                            fn(PADBS[:, b, :, 3:], MS[:, b], ACT.Copy).then_inc(bank_free, 1)
                        else:
                            fn(SGB[:, b, :], M[:, b, 0:T], ACT.Silu).then_inc(bank_free, 1)
                rows_out(i, 1)

            act.wait_ge(slab_done, SLAB_O + 1)
            for i in range(8):
                if i == 4:
                    act.wait_ge(bg_done, 4 + 1)
                if i == 0:
                    act.wait_ge(c_done, 1)
                dst = H_HI[:, 4 * i:4 * i + 4, :]
                if i < 2:
                    fn(dst[:, :, 0:TP], CST[:, 4 * i:4 * i + 4, 0:TP], ACT.Copy)
                    fn(dst[:, :, TP:T].rearrange("p n (s w) -> p n s w", w=DS), CSTS[:, 4 * i:4 * i + 4, :, 1:],
                       ACT.Copy).then_inc(mix_hi_done, 1)
                else:
                    src = AROW[:, 4 * i - 8:4 * i - 4, :] if i < 4 else BROW[:, 4 * i - 16:4 * i - 12, :]
                    fn(dst, src, ACT.Copy).then_inc(mix_hi_done, 1)

            def group_o(j, last_group):
                nb = SLAB_O + j * SPG
                for c in range(AHEAD, SPG if last_group else AHEAD + SPG):
                    hi(nb, c)
                    if c == 15:
                        act.wait_ge(gate_used, 16 * (j + 1))
                        fn(ACC2[:], A0[0][:], ACT.Copy).then_inc(gacc_out, 1)
                for b in range(BLK):
                    if b == 0:
                        act.wait_ge(y_done2, j + 1)
                    bank_ready(N_U + N_A + N_G + N_B + j, b, nb + SPG)
                    fn(OT[:, b, :], M[:, b, 0:T], ACT.Copy).then_inc(bank_free, 1)
                act.wait_ge(y_done2, j + 1 + 1)
                for b in range(BLK):
                    act.wait_ge(ysq_used, 4 * j + max(b - 1, 0) + 1)
                    fn(SQO[:, b % 2, :], X[:, 4 * j + b, :], ACT.Square).then_inc(ysq_done, 1)

            with act.Fori(0, N_O - 1) as j:
                group_o(j, False)
            group_o(N_O - 1, True)
            act.wait_ge(pe_tail, 1)
            fn(RST2[:], A0[2][:, 0:T], ACT.Sqrt, scale=1.0 / D, bias=EPSC[:]).then_inc(yroot, 1)
            for g in range(FIN_DVE, ADA_J):
                for b in range(BLK):
                    k = 4 * g + b
                    act.wait_ge(fin_pool, k - 4 * FIN_DVE + 1)
                    last = fn(X[:, k, :], X[:, k, :], ACT.Copy, scale=PAR[:, C_GF + k:C_GF + k + 1])
                last.then_inc(fin_act, 1)

        @block.vector
        def _(dve):
            tt, ts, stt = nc.vector.tensor_tensor, nc.vector.tensor_scalar, nc.vector.scalar_tensor_tensor
            st = dve_step
            MUL, ADD, SUB = ALU.mult, ALU.add, ALU.subtract

            def then(ins):
                st.up(ins)
                dve.wait_ge(st.sem, st.now())

            def lo(nb, c):
                dve.wait_ge(w_hi_done, nb + c + 1)
                tt(W_LO[:, c % RING], RAW[:, c % RING].rearrange("p (k n) -> p k n", k=2),
                   W_HI[:, c % RING].bitcast(F32), SUB).then_inc(w_lo_done, 1)

            def col(c):
                return PAR[:, bass.ds(c, 1)] if not isinstance(c, int) else PAR[:, c:c + 1]

            def bias9(c):
                return PAR[:, bass.ds(c, BLK)].unsqueeze(2).to_broadcast([P, BLK, 9])

            nc.vector.memset(EPSC[:], EPS).then_inc(s5_dve, 1)
            for b in range(BLK):
                nc.vector.memset(M[:, b, :], 0.0).then_inc(bank_free, 1)
            for i in range(8):
                dve.wait_ge(sq_done, i + 1)
                if i == 0:
                    ins = nc.vector.tensor_copy(SQA[:], SQ[:, 0, :])
                else:
                    dve.wait_ge(sqa_done, i)
                    ins = tt(SQA[:], SQA[:], SQ[:, i % 2, :], ADD)
                ins.then_inc(sqa_done, 1)

            RE, IM, DT, B_RE, B_IM, ANG, MAG, SIN, COS, U1, U2, U3, FR, FI = T0
            w = slice(0, 8 * P)
            dve.wait_ge(s5_act, 1)
            tt(ANG[:], IM[:], DT[:], MUL)
            tt(MAG[:], RE[:], DT[:], MUL).then_inc(s5_dve, 1)
            dve.wait_ge(small_in, 16 * 7)
            lam = PAR[:, C_LAM:C_LAM + 16]
            then(ts(SPT[:, 0], lam, -1.0, None, MUL))
            then(tt(SPT[:, 1], SPT[:, 0], lam, ALU.max))
            ts(NEG8SP[:], SPT[:, 1], -1.0, None, MUL).then_inc(s5_dve, 1)
            then(ts(U1[:], ANG[:], 1.0 / TWO_PI, ROUND, MUL, ADD))
            then(ts(U1[:], U1[:], -ROUND, None, ADD))
            for part in (PI_1, PI_2, PI_3):
                then(stt(ANG[:], U1[:], -part, ANG[:], MUL, ADD))
            ts(ANG[:], ANG[:], NEAR_PI, -NEAR_PI, ALU.min, ALU.max).then_inc(s5_dve, 1)
            dve.wait_ge(s5_act, 3)
            then(ts(SPT[:, 1], NEG8SP[:], 2.0, None, ADD))
            then(nc.vector.reciprocal(SPT[:, 1], SPT[:, 1]))
            then(tt(SPT[:, 1], SPT[:, 1], NEG8SP[:], MUL))
            then(tt(SPT[:, 2], SPT[:, 1], SPT[:, 1], MUL))
            then(ts(SPT[:, 3], SPT[:, 2], 1.0 / 17, None, MUL))
            for n in (15, 13, 11, 9, 7, 5, 3):
                then(stt(SPT[:, 3], SPT[:, 3], 1.0 / n, SPT[:, 2], ADD, MUL))
            then(stt(SPT[:, 3], SPT[:, 3], 1.0, SPT[:, 1], ADD, MUL))
            then(ts(SPT[:, 0], SPT[:, 0], 0.0, -8.0, ALU.max, MUL))
            then(stt(NEG8SP[:], SPT[:, 3], -16.0, SPT[:, 0], MUL, ADD))
            dve.wait_ge(root_done, 1)
            nc.vector.reciprocal(RSTD[:], RSTD[:]).then_inc(rstd_done, 1)
            ts(MAGF[:, 1, :], ANG[:, 8 * P:REP], 1.0 / TWO_PI, None, MUL)
            ts(MAGF[:, 0, :], MAG[:, 8 * P:REP], 1.0, None, MUL)
            dve.wait_ge(s5_act, 5)
            then(tt(COS[:, w], COS[:, w], COS[:, w], MUL))
            then(ts(COS[:, w], COS[:, w], -2.0, 1.0, MUL, ADD))
            tt(SIN[:, w], SIN[:, w], MAG[:, w], MUL)
            then(tt(COS[:, w], COS[:, w], MAG[:, w], MUL))
            tt(U1[:, w], RE[:, w], RE[:, w], MUL)
            tt(U2[:, w], IM[:, w], IM[:, w], MUL)
            then(ts(COS[:, w], COS[:, w], -1.0, None, ADD))
            then(tt(U1[:, w], U1[:, w], U2[:, w], ADD))
            nc.vector.reciprocal(U1[:, w], U1[:, w])
            tt(FR[:, w], COS[:, w], RE[:, w], MUL)
            then(tt(U2[:, w], SIN[:, w], IM[:, w], MUL))
            then(tt(FR[:, w], FR[:, w], U2[:, w], ADD))
            tt(FI[:, w], SIN[:, w], RE[:, w], MUL)
            then(tt(U2[:, w], COS[:, w], IM[:, w], MUL))
            then(tt(FI[:, w], FI[:, w], U2[:, w], SUB))
            tt(FR[:, w], FR[:, w], U1[:, w], MUL)
            then(tt(FI[:, w], FI[:, w], U1[:, w], MUL))

            def by_unit(t):
                return t[:, w].rearrange("p (u n) -> p u n", n=P)

            tt(U1[:, w], FR[:, w], B_RE[:, w], MUL)
            then(tt(U2[:, w], FI[:, w], B_IM[:, w], MUL))
            tt(BB[:, :, 0, :], by_unit(U1), by_unit(U2), SUB)
            tt(U3[:, w], FR[:, w], B_IM[:, w], MUL)
            then(tt(MAG[:, w], FI[:, w], B_RE[:, w], MUL))
            tt(BB[:, :, 1, :], by_unit(U3), by_unit(MAG), ADD).then_inc(bb_ready, 1)
            dve.wait_ge(bb_ready, 1)
            dve.wait_ge(rstd_done, 1)

            with dve.Fori(0, ADA_J) as j:
                st.enter(j, 3)
                dve.wait_ge(h_lo_done, j + 1)
                dve.wait_ge(sel_done, 2 * j + 1 + 1)
                tt(MOD[:, 0], A0[2][:, 0:36].rearrange("p (b n) -> p b n", n=9), bias9(C_BADA + 4 * j), ADD)
                dve.wait_ge(h_hi_done, j + 1)
                for kk in range(BLK):
                    ins = stt(HT[:, kk, :], X[:, 4 * j + kk, :], col(C_G + 4 * j + kk), RSTD[:], MUL, MUL)
                then(ins)
                dve.wait_ge(sel_done, 2 * j + 2 + 1)
                then(stt(MOD[:, 1], A0[3][:, 0:36].rearrange("p (b n) -> p b n", n=9), 1.0,
                         bias9(C_BADA + 32 + 4 * j), ADD, ADD))
                for kk in range(BLK):
                    ts(HT[:, kk, 0:TP], HT[:, kk, 0:TP], MOD[:, 1, kk, 0:1], MOD[:, 0, kk, 0:1], MUL, ADD)
                then(tt(HTS[:], HTS[:], MOD[:, 1, :, 1:9].unsqueeze(3).to_broadcast([P, BLK, DB, DS]), MUL))
                tt(HTS[:], HTS[:], MOD[:, 0, :, 1:9].unsqueeze(3).to_broadcast([P, BLK, DB, DS]), ADD).then_inc(
                    ht_done, 1)
                dve.wait_ge(h_hi_done, j + 1 + 1)
                tt(H_LO[:, bass.ds(4 * j, BLK), :], HT[:], H_HI[:, bass.ds(4 * j, BLK), :].bitcast(F32),
                   SUB).then_inc(h_lo_done, 1)
            st.leave(ADA_J)

            for c in range(AHEAD):
                lo(0, c)
            with dve.Fori(0, N_U) as g:
                for c in range(AHEAD, AHEAD + SPG):
                    lo(SLAB_U + g * SPG, c)

            def freed(q, b):
                return 4 * q + b + 1 + BLK

            def turn(t, par):
                qr, qi = Q[par][:, 0, :], Q[par][:, 1, :]
                bu_re, bu_im = A0[0][:, 0:SW], A0[1][:, 0:SW]
                dve.wait_ge(bu_done, t + 1 + 1)
                dve.wait_ge(table_done, t + 1)
                tt(qr, bu_re, TCOS[par][:], MUL)
                tt(qi, bu_im, TCOS[par][:], MUL)
                then(tt(TMPD[:], bu_im, TSIN[par][:], MUL))
                then(tt(qr, qr, TMPD[:], ADD))
                tt(TMPD[:], bu_re, TSIN[par][:], MUL).then_inc(bu_used, 1)
                dve.wait_ge(bu_used, t + 1 + 1)
                then(tt(qi, qi, TMPD[:], SUB))
                then(nc.vector.tensor_copy(Q[par][:, :, TP:SW:DS + 1], S5H0[:, t, :, :]))
                dve.wait_ge(coef_done, t + 1)
                nc.vector.tensor_tensor_scan(qr, COEF[:], qr, 0.0, MUL, ADD)
                nc.vector.tensor_tensor_scan(qi, COEF[:], qi, 0.0, MUL, ADD).then_inc(q_done, 1)

            def conv_a(h, b):
                n = 4 * h + b
                dve.wait_ge(bank_free, freed(N_U + 4 * h + 1, b))
                tt(PADA[:, b, 2:2 + TP], PADA[:, b, 2:2 + TP], AROW[:, n, 0:TP], MUL)
                then(tt(PADAS[:, b, :, 2:], PADAS[:, b, :, 2:], AROWS[:, n], MUL))
                ts(AROW[:, n, 0:TP], PADA[:, b, 0:TP], col(C_WCA + n), col(C_BCA + n), MUL, ADD)
                then(ts(AROWS[:, n], PADAS[:, b, :, 0:DS], col(C_WCA + n), col(C_BCA + n), MUL, ADD))
                for k in (1, 2):
                    stt(AROW[:, n, 0:TP], PADA[:, b, k:k + TP], col(C_WCA + 8 * k + n), AROW[:, n, 0:TP], MUL, ADD)
                    ins = stt(AROWS[:, n], PADAS[:, b, :, k:k + DS], col(C_WCA + 8 * k + n), AROWS[:, n], MUL, ADD)
                    if k == 1:
                        then(ins)
                if b == BLK - 1:
                    ins.then_inc(conva_done, 1)
                else:
                    then(ins)

            with dve.Fori(0, 2) as h:
                st.enter(h, 16 * 4 + 4 * 4 - 1)
                dve.wait_ge(pada_ready, h + 1)
                for m in range(4):
                    u = 4 * h + m
                    nb = SLAB_A + u * SPG
                    for c in range(AHEAD, AHEAD + SPG):
                        lo(nb, c)
                        if c in (4, 7, 10, 13):
                            turn(4 * u + c // 3 - 1, (c // 3 - 1) % 2)
                        if m == 2 and c in (5, 8, 11, 14):
                            conv_a(h, c // 3 - 1)
                        if m == 3 and c == 5:
                            dve.wait_ge(conva_done, h + 1)
                            dve.wait_ge(bank_free, freed(N_U + 4 * h + 2, 3))
                            rows = AROW[:, bass.ds(4 * h, BLK), :]
                            tt(rows, rows, TMPA[:], MUL).then_inc(ab_done, 1)
                    if m == 3:
                        dve.wait_ge(ab_done, h + 1)
                        dve.wait_ge(bank_free, freed(N_U + 4 * h + 3, 3))
                        rows = AROW[:, bass.ds(4 * h, BLK), :]
                        tt(rows, rows, TMPA[:], MUL).then_inc(ag_done, 1)
                    dve.wait_ge(y_done, 4 * u + 4 + 1)
                    stt(CST[:, u, :], CST[:, u, :], col(C_S5D + u), A0[2][:, 0:SW], MUL, ADD).then_inc(y_sum, 1)
            st.leave(2)

            for i in range(4):
                dve.wait_ge(y_hi_done, i + 1)
                tt(Y_LO[:, 2 * i:2 * i + 2, :], CST[:, 2 * i:2 * i + 2, :], Y_HI[:, 2 * i:2 * i + 2, :].bitcast(F32),
                   SUB).then_inc(y_lo_done, 1)
            for c in range(AHEAD, AHEAD + 2 * SPGG):
                lo(SLAB_G, c)
                if c in (6, 10):
                    g = (c - 6) // 4
                    dve.wait_ge(bank_free, freed(N_U + N_A + g, 3))
                    tt(SG[:, 4 * g:4 * g + 4, :], SG[:, 4 * g:4 * g + 4, :], ZG[:], MUL).then_inc(z_used, 1)
            dve.wait_ge(z_used, 2)
            tt(CST[:], CST[:], SG[:], MUL).then_inc(c_done, 1)

            def conv_b(i, hd):
                n = 4 * i + hd
                ins = ts(XB[:, hd, :], PADB[:, hd, 0:XW], col(C_WCB + n), col(C_BCB + n), MUL, ADD)
                for k in (1, 2, 3):
                    then(ins)
                    ins = stt(XB[:, hd, :], PADB[:, hd, k:k + XW], col(C_WCB + 16 * k + n), XB[:, hd, :], MUL, ADD)
                return ins

            def lru(i, pr):
                dve.wait_ge(roots, 2 * i + pr + 1)
                nc.vector.memset(AA[:, :, TP + 2:XW - DS:DS + 3], 0.0)
                then(tt(TH[:], TH[:], IG[:], MUL))
                then(tt(TH[:], TH[:], XB[:, 2 * pr:2 * pr + 2, :], MUL))
                then(nc.vector.tensor_copy(TH[:, :, TP + 2:XW - DS:DS + 3],
                                           LRU0[:, bass.ds(4 * i + 2 * pr, 2), :]))
                for hd in range(2):
                    last = nc.vector.tensor_tensor_scan(R[:, hd, :], AA[:, hd, :], TH[:, hd, :], 0.0, MUL, ADD)
                last.then_inc(hs_done, 1)

            with dve.Fori(0, 4) as i:
                st.enter(i, 3 * 4 + 2 + 2 * 3)
                for g in range(2):
                    nb = SLAB_B + (2 * i + g) * SPG
                    for c in range(AHEAD, AHEAD + SPG):
                        lo(nb, c)
                        if g == 1 and c in (4, 8):
                            pr = c // 8
                            if pr == 0:
                                dve.wait_ge(gates_done, 2 * i + 1)
                                dve.wait_ge(bank_free, freed(N_U + N_A + N_G + 2 * i, 3))
                            then(conv_b(i, 2 * pr))
                            conv_b(i, 2 * pr + 1).then_inc(xb_ready, 1)
                        if g == 1 and c in (11, 17):
                            pr = c // 17
                            dve.wait_ge(lru_act, 4 * i + 2 * pr + 2)
                            stt(TH[:], R[:], 1.0, TH[:], ADD, MUL).then_inc(root_in, 1)
                        if g == 1 and c == 13:
                            lru(i, 0)
                lru(i, 1)
                dve.wait_ge(hs_out, 2 * i + 2 + 1)
                dve.wait_ge(bank_free, freed(N_U + N_A + N_G + 2 * i + 1, 3))
                rows = BROW[:, bass.ds(4 * i, BLK), :]
                tt(rows, rows, SGB[:], MUL).then_inc(bg_done, 1)
            st.leave(4)

            for i in range(8):
                dve.wait_ge(mix_hi_done, i + 1)
                dst, hi_ = H_LO[:, 4 * i:4 * i + 4, :], H_HI[:, 4 * i:4 * i + 4, :].bitcast(F32)
                if i < 2:
                    tt(dst[:, :, 0:TP], CST[:, 4 * i:4 * i + 4, 0:TP], hi_[:, :, 0:TP], SUB)
                    tt(dst[:, :, TP:T].rearrange("p n (s w) -> p n s w", w=DS), CSTS[:, 4 * i:4 * i + 4, :, 1:],
                       hi_[:, :, TP:T].rearrange("p n (s w) -> p n s w", w=DS), SUB).then_inc(mix_lo_done, 1)
                else:
                    src = AROW[:, 4 * i - 8:4 * i - 4, :] if i < 4 else BROW[:, 4 * i - 16:4 * i - 12, :]
                    tt(dst, src, hi_, SUB).then_inc(mix_lo_done, 1)
            then(nc.vector.memset(SQS[:], 0.0))

            def group_o(j, last_group):
                for c in range(AHEAD, SPG + (2 if last_group else AHEAD)):
                    if c < SPG or not last_group:
                        lo(SLAB_O + j * SPG, c)
                    if c == 16:
                        dve.wait_ge(gsel_done, j + 1)
                        tt(MOD[:, 2], A0[1][:, 0:36].rearrange("p (b n) -> p b n", n=9),
                           bias9(C_BADA + 64 + 4 * j), ADD).then_inc(gmod_done, 1)
                dve.wait_ge(gmod_done, j + 1 + 1)
                dve.wait_ge(x_back, 16 * 8)
                dve.wait_ge(bank_free, freed(N_U + N_A + N_G + N_B + j, 3))
                for b in range(BLK):
                    row = X[:, 4 * j + b, 0:TP]
                    stt(row, OT[:, b, 0:TP], MOD[:, 2, b, 0:1], row, MUL, ADD)
                then(tt(OTS[:], OTS[:], MOD[:, 2, :, 1:9].unsqueeze(3).to_broadcast([P, BLK, DB, DS]), MUL))
                rows = XS[:, bass.ds(4 * j, BLK)]
                tt(rows, rows, OTS[:], ADD).then_inc(y_done2, 1)
                for b in range(BLK):
                    dve.wait_ge(ysq_done, 4 * j + b + 1)
                    dve.wait_ge(ysq_used, 4 * j + b + 1)
                    tt(SQS[:], SQS[:], SQO[:, b % 2, :], ADD).then_inc(ysq_used, 1)

            with dve.Fori(0, N_O - 1) as j:
                st.enter(j, 1)
                group_o(j, False)
            st.leave(N_O - 1)
            group_o(N_O - 1, True)
            dve.wait_ge(yroot, 1)
            nc.vector.reciprocal(RST2[:], RST2[:]).then_inc(rstd2_done, 1)
            dve.wait_ge(rstd2_done, 1)
            for g in range(FIN_DVE):
                for b in range(BLK):
                    k = 4 * g + b
                    last = stt(X[:, k, :], X[:, k, :], col(C_GF + k), RST2[:], MUL, MUL)
                last.then_inc(fin_dve, 1)

        @block.gpsimd
        def _(pool):
            tt, ts, copy = nc.gpsimd.tensor_tensor, nc.gpsimd.tensor_scalar, nc.gpsimd.tensor_copy
            st = pool_step
            MUL, ADD, SUB = ALU.mult, ALU.add, ALU.subtract

            def wait(sem_, value):
                pool.wait_ge(sem_, value)
                if not isinstance(value, int):
                    pool.sem_inc(pool_passed, 1)

            def then(ins):
                st.up(ins)
                wait(st.sem, st.now())

            def pad_a(h):
                nc.gpsimd.memset(PADA[:, :, 0:2], 0.0)
                copy(PADAS[:, :, :, 0:2], CAST[:, bass.ds(4 * h, BLK)]).then_inc(pada_ready, 1)

            def frac(t, par):
                sin, cos = TSIN[par][:], TCOS[par][:]
                then(copy(TURN[:], MAGF[:, 1, bass.ds(t, 1)]))
                then(ts(sin, STEP[:], TURN[:], 1.0, MUL, MUL))
                then(ts(cos, sin, 1.0, ROUND, MUL, ADD))
                then(ts(cos, cos, 1.0, -ROUND, MUL, ADD))
                tt(sin, sin, cos, SUB).then_inc(frac_done, 1)

            wait(h_lo_done, ADA_J + 1)
            nc.gpsimd.memset(CST[:, :, TP:SW:DS + 1], 0.0)
            nc.gpsimd.memset(SG[:, :, TP:SW:DS + 1], 0.0).then_inc(strips_ready, 1)
            wait(bb_ready, 1)
            frac(0, 0)
            frac(1, 1)
            with pool.Fori(0, 2) as h:
                st.enter(h, 4 * (4 * 8 - 1))
                wait(ag_done, h + 1)
                pad_a(h)
                for m in range(4):
                    u = 4 * h + m
                    wait(y_done, 4 * u + 1)
                    pool.dma_start(CC[:], a["s5c"][u]).then_inc(cc_in, 16)
                    for j in range(4):
                        t = 4 * u + j
                        par = j % 2
                        qr, qi, cos, sin = Q[par][:, 0, :], Q[par][:, 1, :], TCOS[par][:], TSIN[par][:]
                        wait(q_done, t + 1 + 1)
                        wait(y_done, t + 1)
                        tt(HRI[:, 0, :], qr, cos, MUL)
                        then(tt(TMPP[:], qi, sin, MUL))
                        then(tt(HRI[:, 0, :], HRI[:, 0, :], TMPP[:], SUB))
                        tt(HRI[:, 1, :], qr, sin, MUL)
                        then(tt(TMPP[:], qi, cos, MUL))
                        tt(HRI[:, 1, :], HRI[:, 1, :], TMPP[:], ADD).then_inc(hs5_done, 1)
                        wait(hs5_done, t + 1)
                        ins = copy(STG_S[:, j], HRI[:, :, TP - 1:SW:DS + 1])
                        if j < 3:
                            then(ins)
                        else:
                            ins.then_inc(staged_s, 1)
                        frac(t + 2, par)
                    wait(staged_s, u + 1)
                    pool.dma_start(a["o_s5"][u], STG_S[:]).then_inc(out_s, 16)
                    wait(out_s, 16 * (u + 1))
                    if m == 2:
                        wait(conva_done, h + 1)
                        copy(STG_A[:, :, :, 0], PADA[:, :, TP:PA:DS + 2])
                        copy(STG_A[:, :, :, 1], PADA[:, :, TP + 1:PA:DS + 2]).then_inc(staged_a, 1)
                        wait(staged_a, h + 1)
                        pool.dma_start(a["o_ca"][h], STG_A[:]).then_inc(out_a, 16)
                        wait(out_a, 16 * (h + 1))
            st.leave(2)

            wait(slab_done, SLAB_B + 1)
            with pool.Fori(0, 4) as i:
                wait(bg_done, i + 1)
                nc.gpsimd.memset(PADB[:, :, 0:3], 0.0)
                copy(PADBS[:, :, :, 0:3], CBST[:, bass.ds(4 * i, BLK)]).then_inc(padb_ready, 1)
                wait(gates_done, 2 * i + 1)
                pool.dma_start(WG[:], a["wg"][i]).then_inc(wg_in, 16)
                wait(bank_free, 4 * (N_U + N_A + N_G + 2 * i) + 8)
                copy(STG_B[:, :, :, 0], PADB[:, :, TP:PB:DS + 3])
                copy(STG_B[:, :, :, 1], PADB[:, :, TP + 1:PB:DS + 3])
                copy(STG_B[:, :, :, 2], PADB[:, :, TP + 2:PB:DS + 3]).then_inc(convb_staged, 1)
                wait(convb_staged, i + 1)
                pool.dma_start(a["o_cb"][i], STG_B[:]).then_inc(out_b, 16)
                for pr in range(2):
                    wait(hs_done, 2 * i + pr + 1)
                    copy(STG_H[:, 2 * pr:2 * pr + 2, :], R[:, :, TP - 1:XW:DS + 3]).then_inc(lru_staged, 1)
                wait(lru_staged, 2 * i + 2 + 1)
                pool.dma_start(a["o_lru"][i], STG_H[:]).then_inc(out_b, 16)
                wait(out_b, 32 * (i + 1))

            wait(mix_lo_done, 8)
            for g in range(8):
                pool.dma_start(X[:, 4 * g:4 * g + 4, :], a["x"][:, 4 * g:4 * g + 4, :]).then_inc(x_back, 16)
            wait(rstd2_done, 1)
            for k in range(4 * FIN_DVE, KT):
                tt(X[:, k, :], X[:, k, :], RST2[:], MUL).then_inc(fin_pool, 1)


def layouts():
    a0, b0, c0 = 0, 4 * W_A, 4 * W_A + 2 * W_B
    starts = [c0, c0 + COLS, c0 + W_C, c0 + W_C + COLS]
    for h in range(2):
        starts += [a0 + s * W_A + COLS * h for s in (1, 2, 0, 3)]
    for i in range(4):
        starts += [b0 + COLS * i, b0 + W_B + COLS * i]
    rows = [W_A + W_B + P * n for n in range(8)] + [P * n for n in range(8)] + [W_A + P * n for n in range(16)]
    return starts, rows


def slabs(w, starts, rows):
    out = []
    for s in starts:
        blk = np.stack([w[r:r + P, s:s + COLS] for r in rows])
        out.append(blk.reshape(len(rows) // 2, 2, P, COLS).transpose(0, 2, 1, 3).reshape(-1, P, SLAB))
    return np.concatenate(out)


def channel_major(v):
    v = np.asarray(v)
    v = v.reshape(*v.shape[:-1], v.shape[-1] // P, P)
    return np.moveaxis(v, -1, 0)


_OUTS = {"y": (8, P, 4, T), "o_ca": (2, P, BLK, 9, 2), "o_cb": (4, P, BLK, 9, 3), "o_lru": (4, P, BLK, 9),
         "o_s5": (8, P, BLK, 2, 9)}


def kernel(**inputs):
    import concourse.bacc as bacc
    from concourse.bass_utils import run_bass_kernel_spmd

    x = {k: np.asarray(v) for k, v in inputs.items()}
    f32 = np.float32
    l = {k: v[0] for k, v in x.items() if v.shape[0] == 1 and k not in ("x_prompt", "c_prompt")}
    starts, rows = layouts()
    kt = [P * k for k in range(KT)]
    w = np.concatenate([
        slabs(l["w_in"], starts[:12], kt), slabs(l["w_glu"], [0, COLS], kt[:8]), slabs(l["w_in"], starts[12:], kt),
        slabs(l["w_out"], [COLS * j for j in range(8)], rows)])
    order = [c for j in range(8) for c in (COLS * j, D + COLS * j)] + [2 * D + COLS * j for j in range(8)]
    ada = slabs(l["w_ada"], order, kt)
    tok = np.concatenate([x["x_prompt"][0], x["x_sample"].reshape(DB * DS, D)])
    xT = channel_major(tok).transpose(0, 2, 1)
    cT = np.zeros((P, KT, 32), f32)
    cT[:, :, 0:9] = channel_major(np.concatenate([x["c_prompt"], x["c_sample"]])).transpose(0, 2, 1)
    par = np.concatenate([channel_major(l[k].reshape(-1)) for k in (
        "b_ada", "g_norm", "w_conv_a", "b_conv_a", "w_conv_b", "b_conv_b", "b_rg", "b_ig", "lru_lambda", "b_glu",
        "s5_d")] + [channel_major(x["g_final"])], axis=1)
    assert par.shape[1] == N_PAR
    sel_ones = np.zeros((P, 9 + P), f32)
    for b in range(9):
        sel_ones[b::32, b] = 1
    sel_ones[:, 9:] = 1
    mask, step = np.ones(SW, f32), np.zeros(SW, f32)
    mask[TP::DS + 1] = 0
    step[0:TP] = np.arange(1, TP + 1)
    for b in range(DB):
        step[TP + 9 * b + 1:TP + 9 * b + 9] = np.arange(1, DS + 1)
    mask, step = (np.ascontiguousarray(np.broadcast_to(v, (P, SW))) for v in (mask, step))
    log_dt = np.broadcast_to(l["s5_log_dt"][:, None], (64, S5_P))
    rep = np.zeros((P, 3, REP), f32)
    for n, v in enumerate((l["s5_lambda_re"], l["s5_lambda_im"], log_dt)):
        by = v.reshape(8, 4, P)
        rep[:, n, 0:8 * P] = np.repeat(by.transpose(1, 0, 2).reshape(4, 8 * P), 32, axis=0)
        rep[:, n, 8 * P:8 * P + NST] = v.reshape(NST, P).T
    s5b = np.zeros((4, 2, S5_I, 2, 8, 2, S5_P), f32)
    s5c = np.zeros((8, 2, S5_P, 2, 4, 2, S5_I), f32)
    for n, (b_, c_) in enumerate((("s5_b_re", "s5_c_re"), ("s5_b_im", "s5_c_im"))):
        bv = l[b_].reshape(8, 4, 2, S5_P, S5_I)
        cv = l[c_].reshape(8, 4, 2, S5_I, S5_P)
        for g in range(2):
            s5b[:, g, :, n, :, g, :] = bv[:, :, g].transpose(1, 3, 0, 2)
            s5c[:, g, :, n, :, g, :] = cv[:, :, g].transpose(0, 3, 1, 2)
    s5h0 = np.stack([l["state_s5_re"].reshape(DB, NST, P), l["state_s5_im"].reshape(DB, NST, P)])
    wg = np.stack([l["w_rg"], l["w_ig"]]).reshape(2, 4, BLK, P, P)
    arrays = {
        "w": w, "ada": ada, "x": xT, "c": cT, "par": par, "sel_ones": sel_ones, "mask": mask, "step": step,
        "rep": rep, "s5b": s5b.reshape(P, 2, 8 * P), "s5c": s5c.reshape(8, P, 2, BLK, 32),
        "s5h0": s5h0.transpose(3, 2, 0, 1), "wg": wg.transpose(1, 3, 2, 0, 4),
        "cb": channel_major(l["state_conv_b"]).transpose(0, 3, 1, 2),
        "lru": channel_major(l["state_lru_h"]).transpose(0, 2, 1),
        "ca": channel_major(l["state_conv_a"]).transpose(0, 3, 1, 2),
    }
    arrays = {f"in_{k}": np.ascontiguousarray(v) for k, v in arrays.items()}
    nc = bacc.Bacc("TRN2", target_bir_lowering=False, num_devices=1)
    aps = {k[3:]: nc.dram_tensor(k, v.shape, mybir.dt.from_np(v.dtype), kind="ExternalInput").ap()
           for k, v in arrays.items()}
    for k, shape in _OUTS.items():
        aps[k] = nc.dram_tensor(f"out_{k}", shape, F32, kind="ExternalOutput").ap()
    build(nc, aps)
    r = run_bass_kernel_spmd(nc, [arrays], core_ids=[0]).results[0]
    y, ca, cb, lru, s5 = (np.asarray(r[f"out_{k}"]) for k in _OUTS)
    y = y.transpose(3, 0, 2, 1).reshape(T, D)
    ca = ca.transpose(3, 4, 0, 2, 1).reshape(9, 2, W_A)
    cb = cb.transpose(3, 4, 0, 2, 1).reshape(9, 3, W_B)
    lru = lru.transpose(3, 0, 2, 1).reshape(9, W_B)
    s5 = s5.transpose(3, 4, 0, 2, 1).reshape(2, 9, 64, S5_P)
    both = [ca, cb, lru, s5[0], s5[1]]
    c = np.ascontiguousarray
    return (c(y[None, 0:TP]), c(y[TP:].reshape(DB, DS, D)), *(c(v[None, 0:1]) for v in both),
            *(c(v[None, 1:9]) for v in both))
```

```python
from contextlib import ExitStack

import concourse.bass as bass
import numpy as np
from concourse import mybir

F32 = mybir.dt.float32
F32R = mybir.dt.float32r
ALU = mybir.AluOpType
ACT = mybir.ActivationFunctionType

P = 128
D = 4096
KT = D // P
TP, DB, DS = 256, 8, 8
T = TP + DB * DS
W_A, W_B, W_C = D // 4, D // 2, D // 4
S5_P, S5_I = 64, 16
EPS = 1e-6

COLS = 512
SLAB = 2 * COLS
BLK = COLS // P
SPG = KT // 2
AHEAD = 3
RING = 4
SPH = SPG // 2
SPGG = W_C // P // 2
N_P, N_U, N_A, N_G, N_B, N_O = 8, 4, 8, 2, 8, 8
SLAB_U = N_P * SPH
SLAB_A = SLAB_U + N_U * SPH
SLAB_G = SLAB_A + N_A * SPG
SLAB_B = SLAB_G + N_G * SPGG
SPB = SPH + SPG
SLAB_O = SLAB_B + N_B // 2 * SPB
SLABS = SLAB_O + N_O * SPG
Q_U = N_P
Q_A = Q_U + N_U
Q_G = Q_A + N_A
Q_B = Q_G + N_G
Q_O = Q_B + N_B
ADA_J = 8
ADA_1 = ADA_J // 2

SW = TP + DB * (DS + 1)
PA = 2 + TP + DB * (DS + 2)
PB = 3 + TP + DB * (DS + 3)
XW = PB - 3

C_BADA, C_G, C_WCA, C_BCA, C_WCB, C_BCB = 0, 96, 128, 152, 160, 224
C_BRG, C_BIG, C_LAM, C_BGLU, C_S5D, C_GF = 240, 256, 272, 288, 296, 304
N_PAR = 336
NST = 32
REP = 8 * P + NST + 8

TWO_PI = 6.283185307179586
PI_1 = 6.28125
PI_2 = 2029.0 / 2**20
PI_3 = TWO_PI - PI_1 - PI_2
ROUND = 12582912.0
NEAR_PI = 3.1415925


class Tally:

    def __init__(self, sem):
        self.sem, self.base, self.local = sem, 0, 0

    def up(self, ins):
        ins.then_inc(self.sem, 1)
        self.local += 1
        return ins

    def now(self):
        return self.base + self.local

    def enter(self, i, per):
        self.start, self.per = self.now(), per
        self.base, self.local = self.start + i * per, 0

    def leave(self, n):
        assert self.local == self.per, (self.sem.name, self.local, self.per)
        self.base, self.local = self.start + n * self.per, 0


def build(nc, a):
    ctx = ExitStack()
    with ctx:
        def sem(name):
            return ctx.enter_context(nc.semaphore(name))

        ORIGIN, WORDS = 16512, 53208

        def at(name, off, *shape, dt=F32):
            n = int(np.prod(shape))
            assert off + n <= WORDS, name
            t = nc.alloc_sbuf_tensor_at(name, [P, *shape], dt, offset=ORIGIN + 4 * off)
            return t

        o = 0

        def take(n):
            nonlocal o
            start = o
            o += -(-n // 8) * 8
            return start

        NC_ = 8 * SW
        o_act = take(NC_ + 24 * T)
        o_h = take(2 * KT * T)
        o_raw = take(RING * SLAB)
        o_w = take(2 * RING * SLAB)
        X = at("x", o_act, KT, T)
        ACTS = at("acts", o_act, NC_ + 24 * T)
        H_HI = at("h_hi", o_h, KT, T, dt=F32R)
        H_LO = at("h_lo", o_h + KT * T, KT, T, dt=F32R)
        RAW = at("w_raw", o_raw, RING, SLAB)
        W_HI = at("w_hi", o_w, RING, 2, COLS, dt=F32R)
        W_LO = at("w_lo", o_w + RING * SLAB, RING, 2, COLS, dt=F32R)
        ADA = at("ada_ring", o_w, 2 * RING, 2, COLS)
        ADAX = at("ada_ring_x", o_act, RING, 2, COLS)
        CT = at("c_T", take(KT * 32), KT, 32)
        PAR = at("par", take(N_PAR), N_PAR)
        SELONES = at("sel_ones", take(9 + P), 9 + P)
        SEL, ONES = SELONES[:, 0:9], SELONES[:, 9:9 + P]
        o_s5h0 = take(512)
        S5H0 = at("s5_h0", o_s5h0, NST, 2, DB)
        CBST = at("convb_state", take(384), 16, DB, 3)
        LRU0 = at("lru_h0", take(128), 16, DB)
        CAST = at("conva_state", take(128), 8, DB, 2)
        MOD = at("mod", take(108), 3, BLK, 9)
        MAGF = at("s5_mag_turn", take(80), 2, NST + 8)
        TURN = at("s5_turn", take(1), 1)
        EPSC = at("eps", take(1), 1)
        NEG8SP = at("neg8softplus", take(16), 16)
        STG_A = at("stage_a", take(72), BLK, 9, 2)
        STG_B = at("stage_b", take(108), BLK, 9, 3)
        STG_H = at("stage_h", take(36), BLK, 9)
        STG_S = at("stage_s", take(72), BLK, 2, 9)
        s = o
        T0 = [at(f"s5t{i}", o_h + REP * i, REP) for i in range(14)]
        SPT = at("softplus_tmp", s + 2048, 4, 16)
        SQ = at("x_sq", o_h + 14 * REP, 2, 4 * T)
        SQA = at("x_sqa", o_h + 14 * REP + 8 * T, 4 * T)
        BB = at("s5_bb", s, 8, 2, P)
        CC = at("s5_cc", s + 2048, 2, BLK, 32)
        BBU = at("s5_bb_unit", s + 2304, 2, P)
        MASK = at("s5_mask", s + 2560, SW)
        STEP = at("s5_step", s + 2888, SW)
        RSTD = at("rstd", s + 3216, T)
        HT = at("h_tmp", s + 3536, BLK, T)
        ACCS = at("ada_acc", s + 4816, COLS)
        o_part = (WORDS - 4 * XW) // 8 * 8
        assert o_part >= s + 4816 + COLS
        PART_C = at("part_c", o_part, BLK, SW)
        PART_B = at("part_b", o_part, BLK, XW)
        COEF = at("s5_coef", s + 3216, SW)
        TMPD = at("s5_tmpd", s + 3544, SW)
        TMPP = at("s5_tmpp", s + 3872, SW)
        HRI = at("s5_h", s + 4200, 2, SW)
        o_b = o_act + NC_ + 8 * T
        o_s5 = o_b + NC_
        SG = at("silu_c", o_b, 8, SW)
        UU = at("s5_u_unit", s + 5184, SW)
        TCOS = [at("cos0", o_s5, SW), at("cos1", o_s5 + SW, SW)]
        TSIN = [at("sin0", o_s5 + 2 * SW, SW), at("sin1", s + 4856, SW)]
        Q = [at("q0", o_s5 + 3 * SW, 2, SW), at("q1", o_s5 + 5 * SW, 2, SW)]
        assert 7 * SW + NC_ <= 16 * T
        o_pad = (WORDS - 4 * PA) // 8 * 8
        assert o_pad >= s + 5184 + SW
        PADA = at("pad_a", o_pad, BLK, PA)
        TMPA = at("tmp_a", o_pad, BLK, T)
        Y_HI = at("y_hi", s, 8, SW, dt=F32R)
        Y_LO = at("y_lo", s + NC_, 8, SW, dt=F32R)
        ZG = at("z_glu", o_pad, BLK, SW)
        WG = at("w_gates", s, BLK, 2, P)
        PADB = at("pad_b", s + 1024, BLK, PB)
        SGB = at("silu_b", s + 1024, BLK, T)
        XB = at("xb", s + 2416, BLK, XW)
        R = at("lru_r", s + 3792, 2, XW)
        IG = at("lru_i", s + 4480, 2, XW)
        AA = at("lru_a", s + 5168, 2, XW)
        TH = at("lru_t", s + 5856, 2, XW)
        ADA2 = at("gate_ring", s, RING, 2, COLS)
        OT = at("out_tmp", s + 4096, BLK, T)
        SQO = at("y_sq", s + 5376, 2, T)
        SQS = at("y_sqs", s + 6016, T)
        RST2 = at("rstd2", s + 6336, T)
        ACC2 = at("gate_acc", o_s5h0, COLS)

        CST = ACTS[:, 0:NC_].rearrange("p (n w) -> p n w", w=SW)
        CSTS = CST[:, :, TP:SW].rearrange("p n (s w) -> p n s w", w=DS + 1)
        AROW = ACTS[:, NC_:NC_ + 8 * T].rearrange("p (n w) -> p n w", w=T)
        AROWS = AROW[:, :, TP:T].rearrange("p n (s w) -> p n s w", w=DS)
        BROW = ACTS[:, NC_ + 8 * T:NC_ + 24 * T].rearrange("p (n w) -> p n w", w=T)
        BROWS = BROW[:, :, TP:T].rearrange("p n (s w) -> p n s w", w=DS)
        SGS = SG[:, :, TP:SW].rearrange("p n (s w) -> p n s w", w=DS + 1)
        PADAS = PADA[:, :, 2 + TP:PA].rearrange("p n (s w) -> p n s w", w=DS + 2)
        PADBS = PADB[:, :, 3 + TP:PB].rearrange("p n (s w) -> p n s w", w=DS + 3)
        XS = X[:, :, TP:T].rearrange("p n (s w) -> p n s w", w=DS)
        HTS = HT[:, :, TP:T].rearrange("p n (s w) -> p n s w", w=DS)
        OTS = OT[:, :, TP:T].rearrange("p n (s w) -> p n s w", w=DS)

        M = ctx.enter_context(nc.psum_tensor("m", [P, BLK, 512], F32))
        A0 = [ctx.enter_context(nc.psum_tensor(f"aux{i}", [P, 512], F32)) for i in range(4)]
        PART_CS = PART_C[:, :, TP:SW].rearrange("p n (s w) -> p n s w", w=DS + 1)
        PART_BS = PART_B[:, :, TP:XW].rearrange("p n (s w) -> p n s w", w=DS + 3)
        MS = M[:, :, TP:T].rearrange("p n (s w) -> p n s w", w=DS)

        part_c, part_b = (nc.dram_tensor(k, (4, P, BLK, width), F32, kind="Internal").ap()
                          for k, width in (("part_c", SW), ("part_b", XW)))

        small_in, x_in, s5_in = sem("small_in"), sem("x_in"), sem("s5_in")
        w_landed = [sem(f"w_landed{i}") for i in range(RING)]
        ada_landed = [sem(f"ada_landed{i}") for i in range(2 * RING)]
        adax_landed = [sem(f"adax_landed{i}") for i in range(RING)]
        part_free, part_out, part_c_in, part_b_in = map(sem, ["part_free", "part_out", "part_c_in", "part_b_in"])
        gate_landed = [sem(f"gate_landed{i}") for i in range(RING)]
        ada_used, gate_used = sem("ada_used"), sem("gate_used")
        w_hi_done, w_lo_done, slab_done, bank_done, bank_free = map(
            sem, ["w_hi_done", "w_lo_done", "slab_done", "bank_done", "bank_free"])
        sq_done, sqa_done, sum_done, root_done, rstd_done = map(
            sem, ["sq_done", "sqa_done", "sum_done", "root_done", "rstd_done"])
        acc_done, acc_out, sel_done, ht_done, h_hi_done, h_lo_done = map(
            sem, ["acc_done", "acc_out", "sel_done", "ht_done", "h_hi_done", "h_lo_done"])
        s5_act, s5_dve, bb_ready = map(sem, ["s5_act", "s5_dve", "bb_ready"])
        frac_done, table_done, coef_done, bbu_ready, cc_in, cc_ready = map(
            sem, ["frac_done", "table_done", "coef_done", "bbu_ready", "cc_in", "cc_ready"])
        bu_done, bu_used, q_done, hs5_done, y_done, y_sum, staged_s, out_s = map(
            sem, ["bu_done", "bu_used", "q_done", "hs5_done", "y_done", "y_sum", "staged_s", "out_s"])
        pada_ready, conva_done, ab_done, ag_done, out_a = map(
            sem, ["pada_ready", "conva_done", "ab_done", "ag_done", "out_a"])
        silu_done = sem("silu_done")
        gelu_done, y_hi_done, y_lo_done, z_used = map(sem, ["gelu_done", "y_hi_done", "y_lo_done", "z_used"])
        wg_in, padb_ready, xb_ready, gates_done, gates_used, root_in, roots, hs_done, hs_out, lru_staged = map(
            sem, ["wg_in", "padb_ready", "xb_ready", "gates_done", "gates_used", "root_in", "roots", "hs_done",
                  "hs_out", "lru_staged"])
        out_b, bg_done, convb_staged = sem("out_b"), sem("bg_done"), sem("convb_staged")
        mix_hi_done, mix_lo_done, x_back, gacc_done, gacc_out, gsel_done, gmod_done = map(
            sem, ["mix_hi_done", "mix_lo_done", "x_back", "gacc_done", "gacc_out", "gsel_done", "gmod_done"])
        y_done2, ysq_done, ysum_done, yroot, rstd2_done, fin_dve, fin_pool, out_y = map(
            sem, ["res_done", "ysq_done", "ysum_done", "yroot", "rstd2_done", "fin_dve", "fin_pool", "out_y"])
        ysq_used, lru_act, staged_a, c_done, fin_act = map(sem, ["ysq_used", "lru_act", "staged_a", "c_done", "fin_act"])
        pe_tail, pool_passed, act_passed = sem("pe_tail"), sem("pool_passed"), sem("act_passed")
        act_step, dve_step, pool_step = Tally(sem("act_step")), Tally(sem("dve_step")), Tally(sem("pool_step"))

        from_one = [ht_done, h_hi_done, h_lo_done, sel_done, slab_done, bu_used, y_sum, gates_used,
                    hs_out, lru_staged, gates_done, bg_done, ag_done, y_done, q_done, bu_done,
                    y_done2, ysq_used, gmod_done]

        block = ctx.enter_context(nc.Block())
        FIN_DVE = 6

        @block.sync
        def _(sp):
            for one in from_one:
                sp.sem_inc(one, 1)
            for n in range(2 * RING):
                sp.dma_start(ADA[:, n], a["ada"][n]).then_inc(ada_landed[n], 16)
            with sp.Fori(1, 2 * ADA_1 * SPG // (2 * RING)) as r:
                for n in range(2 * RING):
                    sp.wait_ge(ada_used, r * 2 * RING + n + 1 - 2 * RING)
                    sp.dma_start(ADA[:, n], a["ada"][r * 2 * RING + n]).then_inc(ada_landed[n], 16)
            first = 2 * ADA_1 * SPG
            for n in range(RING):
                sp.dma_start(RAW[:, n], a["w"][n]).then_inc(w_landed[n], 16)
            for n in range(RING):
                if n == 0:
                    sp.wait_ge(ht_done, 3 + 1)
                if n == 3:
                    sp.wait_ge(ht_done, 4 + 1)
                sp.dma_start(ADAX[:, n], a["ada"][first + n]).then_inc(adax_landed[n], 16)
            with sp.Fori(0, first // (2 * RING) - 1) as r:
                for n in range(RING):
                    for m in (2 * n, 2 * n + 1):
                        sp.wait_ge(ada_used, first + r * 2 * RING + m + 1)
                        sp.dma_start(ADAX[:, m % RING], a["ada"][first + RING + r * 2 * RING + m]).then_inc(
                            adax_landed[m % RING], 16)
                    sp.wait_ge(w_lo_done, r * RING + n + 1)
                    sp.dma_start(RAW[:, n], a["w"][(r + 1) * RING + n]).then_inc(w_landed[n], 16)
            for n in range(RING):
                sp.wait_ge(ada_used, 2 * first - 2 * RING + n + 1)
                sp.dma_start(ADAX[:, n], a["ada"][2 * first - RING + n]).then_inc(adax_landed[n], 16)
            with sp.Fori(N_P * SPH // RING, SLAB_O // RING + 1) as r:
                for n in range(RING):
                    sp.wait_ge(w_lo_done, r * RING + n + 1 - RING)
                    sp.dma_start(RAW[:, n], a["w"][r * RING + n]).then_inc(w_landed[n], 16)
            sp.wait_ge(bg_done, 4 + 1)
            sp.wait_ge(lru_staged, 8 + 1)
            sp.wait_ge(convb_staged, 4)
            for n in range(RING):
                sp.dma_start(ADA2[:, n], a["ada"][2 * ADA_J * SPG + n]).then_inc(gate_landed[n], 16)
            with sp.Fori(0, N_O * SPG // RING - 1) as r:
                for n in range(RING):
                    sp.wait_ge(w_lo_done, SLAB_O + r * RING + n + 1)
                    sp.dma_start(RAW[:, n], a["w"][SLAB_O + (r + 1) * RING + n]).then_inc(w_landed[n], 16)
                    sp.wait_ge(gate_used, r * RING + n + 1)
                    sp.dma_start(ADA2[:, n], a["ada"][2 * ADA_J * SPG + (r + 1) * RING + n]).then_inc(
                        gate_landed[n], 16)
            for g in range(FIN_DVE):
                sp.wait_ge(fin_dve, g + 1)
                sp.dma_start(a["y"][g], X[:, 4 * g:4 * g + 4]).then_inc(out_y, 16)
            for g in range(FIN_DVE, ADA_J):
                sp.wait_ge(fin_act, g + 1 - FIN_DVE)
                sp.dma_start(a["y"][g], X[:, 4 * g:4 * g + 4]).then_inc(out_y, 16)
            sp.wait_ge(out_y, 16 * ADA_J)
            sp.wait_ge(part_out, 16 * N_P)
            sp.wait_ge(out_s, 16 * 8)
            sp.wait_ge(out_a, 16 * 2)
            sp.wait_ge(out_b, 32 * 4)

        @block.tensor
        def _(pe):
            mm = nc.tensor.matmul

            def slab(nb, c, nk, q, hi, lo, width, k0=0):
                pe.wait_ge(w_lo_done, nb + c + 1)
                s_ = c % RING
                for b in range(BLK):
                    if c == 0:
                        pe.wait_ge(bank_free, 4 * q + b + 1)
                    for kk in range(2):
                        k = k0 + 2 * c + kk
                        w_hi = W_HI[:, s_, kk, b * P:(b + 1) * P]
                        w_lo = W_LO[:, s_, kk, b * P:(b + 1) * P]
                        out = M[:, b, 0:width]
                        mm(out, w_hi, hi[:, k, :], start=k == k0, stop=False)
                        mm(out, w_hi, lo[:, k, :], start=False, stop=False)
                        last = mm(out, w_lo, hi[:, k, :], start=False, stop=k == k0 + nk - 1)
                    if k == k0 + nk - 1 and b < BLK - 1:
                        last.then_inc(bank_done, 1)
                last.then_inc(slab_done, 1)

            pe.wait_ge(small_in, 16 * 7)
            pe.wait_ge(sqa_done, 8)
            for i in range(4):
                last = mm(A0[3][:, 0:T], ONES, SQA[:, i * T:(i + 1) * T], start=i == 0, stop=i == 3)
            last.then_inc(sum_done, 1)
            def ada_slab(part, sl, slot):
                for kk in range(2):
                    k = 2 * sl + kk
                    r = 32 * (k % 4)
                    last = mm(A0[part][r:r + 32, :], CT[:, k, :], slot[:, kk, :], start=k < 4, stop=k >= KT - 4)
                last.then_inc(ada_used, 1)

            def ada_sum(j, part):
                pe.wait_ge(acc_out, 2 * j + part + 1)
                pe.wait_ge(ht_done, j + 1)
                for b in range(BLK):
                    last = mm(A0[2 + part][:, 9 * b:9 * b + 9], ACCS[:, b * P:(b + 1) * P], SEL, start=True, stop=True)
                last.then_inc(sel_done, 1)

            with pe.Fori(0, ADA_1) as j:
                for part in range(2):
                    for sl in range(SPG):
                        pe.wait_ge(ada_landed[sl % 8], 64 * j + 32 * part + 16 * (sl // 8 + 1))
                        ada_slab(part, sl, ADA[:, sl % 8])
                    if part == 0:
                        pe.wait_ge(rstd_done, 1)
                    ada_sum(j, part)

            with pe.Fori(0, ADA_J - ADA_1) as jj:
                for part in range(2):
                    for c in range(SPH):
                        for sl in (2 * c, 2 * c + 1):
                            pe.wait_ge(adax_landed[sl % RING], 128 * jj + 64 * part + 16 * (sl // RING + 1))
                            ada_slab(part, sl, ADAX[:, sl % RING])
                        if c % 2 == 0:
                            pe.wait_ge(h_lo_done, c // 2 + 1 + 1)
                        slab((2 * jj + part) * SPH, c, KT // 2, 2 * jj + part, H_HI, H_LO, T)
                    ada_sum(jj + ADA_1, part)

            with pe.Fori(0, N_U) as g:
                for c in range(SPH):
                    if c % 2 == 0:
                        pe.wait_ge(h_lo_done, ADA_1 + c // 2 + 1 + 1)
                    slab(SLAB_U + g * SPH, c, KT // 2, Q_U + g, H_HI, H_LO, T, k0=KT // 2)

            with pe.Fori(0, N_A) as u:
                for c in range(SPG):
                    slab(SLAB_A + u * SPG, c, KT, Q_A + u, H_HI, H_LO, T)
                    if c in (0, 3, 6, 9):
                        j = c // 3
                        if j == 0:
                            pe.wait_ge(bbu_ready, u + 1)
                        pe.wait_ge(bu_used, 4 * u + j + 1)
                        r = slice(32 * j, 32 * j + 32)
                        mm(A0[0][:, 0:SW], BBU[r, 0, :], UU[r, :], start=True, stop=True)
                        mm(A0[1][:, 0:SW], BBU[r, 1, :], UU[r, :], start=True, stop=True).then_inc(bu_done, 1)
                    if c in (6, 9, 12, 15):
                        j = c // 3 - 2
                        if j == 0:
                            pe.wait_ge(cc_ready, u + 1)
                            pe.wait_ge(y_sum, u + 1)
                        pe.wait_ge(hs5_done, 4 * u + j + 1)
                        r = slice(32 * j, 32 * j + 32)
                        mm(A0[2][r, 0:SW], CC[:, 0, j, :], HRI[:, 0, :], start=True, stop=False)
                        mm(A0[2][r, 0:SW], CC[:, 1, j, :], HRI[:, 1, :], start=False, stop=True).then_inc(y_done, 1)

            with pe.Fori(0, N_G) as g:
                for c in range(SPGG):
                    pe.wait_ge(y_lo_done, c + 1)
                    slab(SLAB_G + g * SPGG, c, 8, Q_G + g, Y_HI, Y_LO, SW)

            with pe.Fori(0, N_B // 2) as i:
                for c in range(SPH):
                    slab(SLAB_B + i * SPB, c, KT // 2, Q_B + 2 * i, H_HI, H_LO, T, k0=KT // 2)
                for c in range(SPG):
                        slab(SLAB_B + i * SPB + SPH, c, KT, Q_B + 2 * i + 1, H_HI, H_LO, T)
                        if c in (5, 11):
                            pr = c // 6
                            if pr == 0:
                                pe.wait_ge(wg_in, 16 * (i + 1))
                            pe.wait_ge(xb_ready, 2 * i + pr + 1)
                            pe.wait_ge(gates_used, 2 * i + pr + 1)
                            for hd in range(2):
                                for w in range(2):
                                    last = mm(A0[2 * w + hd][:, 0:XW], WG[:, 2 * pr + hd, w, :],
                                              XB[:, 2 * pr + hd, :], start=True, stop=True)
                            last.then_inc(gates_done, 1)

            per = [2] * 4 + [1] * 8 + [0] * 4
            with pe.Fori(0, N_O) as j:
                n = 0
                for c in range(SPG):
                    if c % 2 == 0:
                        pe.wait_ge(mix_lo_done, c // 2 + 1)
                    slab(SLAB_O + j * SPG, c, KT, Q_O + j, H_HI, H_LO, T)
                    for _ in range(per[c]):
                        pe.wait_ge(gate_landed[n % RING], 64 * j + 16 * (n // RING + 1))
                        for kk in range(2):
                            k = 2 * n + kk
                            r = 32 * (k % 4)
                            last = mm(A0[0][r:r + 32, :], CT[:, k, :], ADA2[:, n % RING, kk, :], start=k < 4,
                                      stop=k >= KT - 4)
                        last.then_inc(gate_used, 1)
                        n += 1
                    if c == 13:
                        pe.wait_ge(gacc_out, j + 1)
                        pe.wait_ge(gmod_done, j + 1)
                        for b in range(BLK):
                            last = mm(A0[1][:, 9 * b:9 * b + 9], ACC2[:, b * P:(b + 1) * P], SEL, start=True,
                                      stop=True)
                        last.then_inc(gsel_done, 1)
            pe.wait_ge(ysq_used, 32 + 1)
            mm(A0[2][:, 0:T], ONES, SQS[:], start=True, stop=True).then_inc(pe_tail, 1)

        @block.scalar
        def _(act):
            fn = nc.scalar.activation
            st = act_step

            def then(ins):
                st.up(ins)
                act.wait_ge(st.sem, st.now())

            def hi(nb, c, first=False):
                act.wait_ge(w_landed[c % RING], 4 * nb + 16 * (c // RING + 1))
                if not first:
                    act.wait_ge(slab_done, nb + c + 1 - RING + 1)
                fn(W_HI[:, c % RING], RAW[:, c % RING].rearrange("p (k n) -> p k n", k=2), ACT.Copy).then_inc(
                    w_hi_done, 1)

            def bank_ready(q, b, nb_next):
                if b < BLK - 1:
                    act.wait_ge(bank_done, 3 * q + b + 1)
                else:
                    act.wait_ge(slab_done, nb_next + 1)

            act.dma_start(X[:], a["x"]).then_inc(x_in, 16)
            for dst, name in ((CT, "c"), (PAR, "par"), (SELONES, "sel_ones"), (S5H0, "s5h0"), (CBST, "cb"),
                              (LRU0, "lru"), (CAST, "ca")):
                act.dma_start(dst[:], a[name]).then_inc(small_in, 16)
            for i in range(3):
                act.dma_start(T0[i][:], a["rep"][:, i, :]).then_inc(s5_in, 16)
            for i in range(2):
                act.dma_start(T0[3 + i][:, 0:8 * P], a["s5b"][:, i, :]).then_inc(s5_in, 16)
            act.dma_start(MASK[:], a["mask"]).then_inc(s5_in, 16)
            act.dma_start(STEP[:], a["step"]).then_inc(s5_in, 16)

            act.wait_ge(x_in, 16)
            for i in range(8):
                if i >= 2:
                    act.wait_ge(sqa_done, i - 1)
                fn(SQ[:, i % 2, :], X[:, 4 * i:4 * i + 4, :].rearrange("p k t -> p (k t)"),
                   ACT.Square).then_inc(sq_done, 1)
            act.wait_ge(sum_done, 1)
            act.wait_ge(s5_dve, 1)
            fn(RSTD[:], A0[3][:, 0:T], ACT.Sqrt, scale=1.0 / D, bias=EPSC[:]).then_inc(root_done, 1)

            act.wait_ge(s5_in, 16 * 7)
            fn(T0[2][:], T0[2][:], ACT.Exp).then_inc(s5_act, 1)
            act.wait_ge(s5_dve, 2)
            fn(T0[6][:], T0[6][:], ACT.Exp).then_inc(s5_act, 1)
            act.wait_ge(small_in, 16 * 7)
            act.wait_ge(s5_dve, 3)
            fn(NEG8SP[:], NEG8SP[:], ACT.Exp).then_inc(s5_act, 1)
            act.wait_ge(s5_dve, 4)
            fn(T0[7][:], T0[5][:], ACT.Sin).then_inc(s5_act, 1)
            fn(T0[8][:], T0[5][:], ACT.Sin, scale=0.5).then_inc(s5_act, 1)

            def acc_copy(j, part):
                act.wait_ge(ada_used, 32 * j + 16 * (part + 1))
                act.wait_ge(sel_done, 2 * j + part + 1)
                fn(ACCS[:], A0[part][:], ACT.Copy).then_inc(acc_out, 1)

            def h_hi(j):
                act.wait_ge(ht_done, j + 1 + 1)
                fn(H_HI[:, bass.ds(4 * j, 4), :], HT[:], ACT.Copy).then_inc(h_hi_done, 1)

            with act.Fori(0, ADA_1 - 1) as j:
                for part in range(2):
                    acc_copy(j, part)
                act.wait_ge(bb_ready, 1)
                h_hi(j)
            for part in range(2):
                acc_copy(ADA_1 - 1, part)
            act.wait_ge(ada_used, 2 * ADA_1 * SPG)
            for c in range(AHEAD):
                hi(0, c, first=True)
            h_hi(ADA_1 - 1)

            for start, buf, samples in ((0, PART_C, PART_CS), (2, PART_B, PART_BS[:, :, :, 3:])):
                off = 1 if start == 0 else 0
                with act.Fori(start, start + 2) as jj:
                    for part in range(2):
                        n = 2 * jj + part
                        for c in range(AHEAD, AHEAD + SPH):
                            hi(n * SPH, c)
                        acc_copy(jj + ADA_1, part)
                        act.wait_ge(part_free, n + 1)
                        for b in range(BLK):
                            bank_ready(n, b, n * SPH + SPH)
                            fn(buf[:, b, 0:TP], M[:, b, 0:TP], ACT.Copy)
                            fn(samples[:, b, :, off:] if off else samples[:, b], MS[:, b], ACT.Copy).then_inc(
                                bank_free, 1)
                    h_hi(jj + ADA_1)

            with act.Fori(0, N_U) as g:
                for c in range(AHEAD, AHEAD + SPH):
                    hi(SLAB_U + g * SPH, c)
            act.wait_ge(bank_free, 4 * (Q_U + N_U) + 4)
            fn(SG[:], SG[:], ACT.Silu).then_inc(silu_done, 1)

            def tables(par, tile):
                act.wait_ge(frac_done, tile + 1)
                then(fn(TCOS[par][:], TSIN[par][:], ACT.Sin, scale=TWO_PI / 2))
                then(fn(TCOS[par][:], TCOS[par][:], ACT.Square))
                fn(TCOS[par][:], TCOS[par][:], ACT.Copy, scale=-2.0, bias=1.0)
                fn(TSIN[par][:], TSIN[par][:], ACT.Sin, scale=TWO_PI).then_inc(table_done, 1)

            tables(0, 0)
            with act.Fori(0, 2) as h:
                st.enter(h, 32)
                for m in range(4):
                    u = 4 * h + m
                    nb = SLAB_A + u * SPG
                    q = Q_A + u
                    for c in range(AHEAD, AHEAD + SPG):
                        hi(nb, c)
                        if c == 3:
                            act.wait_ge(bu_done, 4 * u + 1)
                            fn(UU[:], CST[:, u, :], ACT.Copy)
                            fn(BBU[:], BB[:, u], ACT.Copy).then_inc(bbu_ready, 1)
                        if c == 5:
                            act.wait_ge(cc_in, 16 * (u + 1))
                            fn(CC[:, 1], CC[:, 1], ACT.Copy, scale=-1.0).then_inc(cc_ready, 1)
                        if c in (3, 6, 9, 12):
                            j = c // 3 - 1
                            act.wait_ge(q_done, 4 * u + j + 1)
                            fn(COEF[:], MASK[:], ACT.Copy, scale=MAGF[:, 0, bass.ds(4 * u + j, 1)]).then_inc(
                                coef_done, 1)
                        if c in (6, 9, 12, 15):
                            j = c // 3 - 2
                            tables((j + 1) % 2, 4 * u + j + 1)
                    for b in range(BLK):
                        if b == 0 and m == 0:
                            act.wait_ge(pada_ready, h + 1)
                        if b == 0 and m == 2:
                            act.wait_ge(conva_done, h + 1)
                            act.wait_ge(staged_a, h + 1)
                        if b == 0 and m == 3:
                            act.wait_ge(ab_done, h + 1)
                        bank_ready(q, b, nb + SPG)
                        if m == 0:
                            fn(PADA[:, b, 2:2 + TP], M[:, b, 0:TP], ACT.Copy)
                            fn(PADAS[:, b, :, 2:], MS[:, b], ACT.Copy).then_inc(bank_free, 1)
                        elif m == 1:
                            fn(AROW[:, 4 * h + b, :], M[:, b, 0:T], ACT.Copy).then_inc(bank_free, 1)
                        else:
                            fn(TMPA[:, b, :], M[:, b, 0:T], ACT.Copy if m == 2 else ACT.Silu).then_inc(bank_free, 1)
                    act.wait_ge(y_sum, u + 1 + 1)
                    act.sem_inc(act_passed, 1)
                    fn(CST[:, u, :], CST[:, u, :], ACT.Gelu_apprx_tanh).then_inc(gelu_done, 1)
            st.leave(2)

            act.wait_ge(gelu_done, 8)
            act.wait_ge(y_done, 32 + 1)
            act.wait_ge(staged_s, 8)
            act.wait_ge(frac_done, 34)
            for i in range(4):
                fn(Y_HI[:, 2 * i:2 * i + 2, :], CST[:, 2 * i:2 * i + 2, :], ACT.Copy).then_inc(y_hi_done, 1)
            for c in range(AHEAD, AHEAD + 2 * SPGG):
                hi(SLAB_G, c)
                if c in (6, 10):
                    g = (c - 6) // 4
                    for b in range(BLK):
                        if b == 0 and g == 0:
                            act.wait_ge(ag_done, 2 + 1)
                        if b == 0 and g == 1:
                            act.wait_ge(z_used, 1)
                        bank_ready(Q_G + g, b, SLAB_G + 4 * (g + 1))
                        n = 4 * g + b
                        fn(ZG[:, b, :], M[:, b, 0:SW], ACT.Sigmoid, bias=PAR[:, C_BGLU + n:C_BGLU + n + 1]).then_inc(
                            bank_free, 1)

            def rows_out(i, pr):
                act.wait_ge(hs_done, 2 * i + pr + 1)
                for hd in range(2):
                    n = 4 * i + 2 * pr + hd
                    fn(BROW[:, n, 0:TP], R[:, hd, 0:TP], ACT.Copy)
                    last = fn(BROWS[:, n], R[:, hd, TP:XW].rearrange("p (s w) -> p s w", w=DS + 3)[:, :, 3:], ACT.Copy)
                last.then_inc(hs_out, 1)

            with act.Fori(0, 4) as i:
                for g in range(2):
                    nb = SLAB_B + i * SPB + g * SPH
                    q = Q_B + 2 * i + g
                    for c in range(AHEAD, AHEAD + (SPG if g else SPH)):
                        hi(nb, c)
                        if g == 1 and c in (9, 15):
                            pr = c // 15
                            act.wait_ge(gates_done, 2 * i + pr + 1 + 1)
                            act.wait_ge(hs_out, 2 * i + pr + 1)
                            act.wait_ge(lru_staged, 2 * i + pr + 1)
                            for w, buf, col in ((0, R, C_BRG), (1, IG, C_BIG)):
                                for hd in range(2):
                                    last = fn(buf[:, hd, :], A0[2 * w + hd][:, 0:XW], ACT.Sigmoid,
                                              bias=PAR[:, bass.ds(col + 4 * i + 2 * pr + hd, 1)])
                            last.then_inc(gates_used, 1)
                            act.wait_ge(gates_used, 2 * i + pr + 1 + 1)
                            for hd in range(2):
                                n8 = NEG8SP[:, bass.ds(4 * i + 2 * pr + hd, 1)]
                                fn(AA[:, hd, :], R[:, hd, :], ACT.Exp, scale=n8)
                                last = fn(TH[:, hd, :], R[:, hd, :], ACT.Tanh, scale=n8)
                            last.then_inc(lru_act, 1)
                            act.wait_ge(lru_act, 4 * i + 2 * pr + 1)
                            fn(R[:], AA[:], ACT.Square).then_inc(lru_act, 1)
                        if g == 1 and c in (12, 17):
                            pr = c // 17
                            act.wait_ge(root_in, 2 * i + pr + 1)
                            fn(TH[:], TH[:], ACT.Sqrt, scale=-1.0).then_inc(roots, 1)
                        if g == 1 and c == 14:
                            rows_out(i, 0)
                for b in range(BLK):
                    if b == 0:
                        act.wait_ge(convb_staged, i + 1)
                        act.wait_ge(xb_ready, 2 * i + 2)
                    bank_ready(q, b, nb + SPG)
                    fn(SGB[:, b, :], M[:, b, 0:T], ACT.Silu).then_inc(bank_free, 1)
                rows_out(i, 1)

            act.wait_ge(slab_done, SLAB_O + 1)
            for i in range(8):
                if i == 4:
                    act.wait_ge(bg_done, 4 + 1)
                if i == 0:
                    act.wait_ge(c_done, 1)
                dst = H_HI[:, 4 * i:4 * i + 4, :]
                if i < 2:
                    fn(dst[:, :, 0:TP], CST[:, 4 * i:4 * i + 4, 0:TP], ACT.Copy)
                    fn(dst[:, :, TP:T].rearrange("p n (s w) -> p n s w", w=DS), CSTS[:, 4 * i:4 * i + 4, :, 1:],
                       ACT.Copy).then_inc(mix_hi_done, 1)
                else:
                    src = AROW[:, 4 * i - 8:4 * i - 4, :] if i < 4 else BROW[:, 4 * i - 16:4 * i - 12, :]
                    fn(dst, src, ACT.Copy).then_inc(mix_hi_done, 1)

            def group_o(j, last_group):
                nb = SLAB_O + j * SPG
                for c in range(AHEAD, SPG if last_group else AHEAD + SPG):
                    hi(nb, c)
                    if c == 15:
                        act.wait_ge(gate_used, 16 * (j + 1))
                        fn(ACC2[:], A0[0][:], ACT.Copy).then_inc(gacc_out, 1)
                for b in range(BLK):
                    if b == 0:
                        act.wait_ge(y_done2, j + 1)
                    bank_ready(Q_O + j, b, nb + SPG)
                    fn(OT[:, b, :], M[:, b, 0:T], ACT.Copy).then_inc(bank_free, 1)
                act.wait_ge(y_done2, j + 1 + 1)
                for b in range(BLK):
                    act.wait_ge(ysq_used, 4 * j + max(b - 1, 0) + 1)
                    fn(SQO[:, b % 2, :], X[:, 4 * j + b, :], ACT.Square).then_inc(ysq_done, 1)

            with act.Fori(0, N_O - 1) as j:
                group_o(j, False)
            group_o(N_O - 1, True)
            act.wait_ge(pe_tail, 1)
            fn(RST2[:], A0[2][:, 0:T], ACT.Sqrt, scale=1.0 / D, bias=EPSC[:]).then_inc(yroot, 1)
            for g in range(FIN_DVE, ADA_J):
                for b in range(BLK):
                    k = 4 * g + b
                    act.wait_ge(fin_pool, k - 4 * FIN_DVE + 1)
                    last = fn(X[:, k, :], X[:, k, :], ACT.Copy, scale=PAR[:, C_GF + k:C_GF + k + 1])
                last.then_inc(fin_act, 1)

        @block.vector
        def _(dve):
            tt, ts, stt = nc.vector.tensor_tensor, nc.vector.tensor_scalar, nc.vector.scalar_tensor_tensor
            st = dve_step
            MUL, ADD, SUB = ALU.mult, ALU.add, ALU.subtract

            def then(ins):
                st.up(ins)
                dve.wait_ge(st.sem, st.now())

            def lo(nb, c):
                dve.wait_ge(w_hi_done, nb + c + 1)
                tt(W_LO[:, c % RING], RAW[:, c % RING].rearrange("p (k n) -> p k n", k=2),
                   W_HI[:, c % RING].bitcast(F32), SUB).then_inc(w_lo_done, 1)

            def col(c):
                return PAR[:, bass.ds(c, 1)] if not isinstance(c, int) else PAR[:, c:c + 1]

            def bias9(c):
                return PAR[:, bass.ds(c, BLK)].unsqueeze(2).to_broadcast([P, BLK, 9])

            nc.vector.memset(EPSC[:], EPS).then_inc(s5_dve, 1)
            for b in range(BLK):
                nc.vector.memset(M[:, b, :], 0.0).then_inc(bank_free, 1)
            for i in range(8):
                dve.wait_ge(sq_done, i + 1)
                if i == 0:
                    ins = nc.vector.tensor_copy(SQA[:], SQ[:, 0, :])
                else:
                    dve.wait_ge(sqa_done, i)
                    ins = tt(SQA[:], SQA[:], SQ[:, i % 2, :], ADD)
                ins.then_inc(sqa_done, 1)

            RE, IM, DT, B_RE, B_IM, ANG, MAG, SIN, COS, U1, U2, U3, FR, FI = T0
            w = slice(0, 8 * P)
            dve.wait_ge(s5_act, 1)
            tt(ANG[:], IM[:], DT[:], MUL)
            tt(MAG[:], RE[:], DT[:], MUL).then_inc(s5_dve, 1)
            dve.wait_ge(small_in, 16 * 7)
            lam = PAR[:, C_LAM:C_LAM + 16]
            then(ts(SPT[:, 0], lam, -1.0, None, MUL))
            then(tt(SPT[:, 1], SPT[:, 0], lam, ALU.max))
            ts(NEG8SP[:], SPT[:, 1], -1.0, None, MUL).then_inc(s5_dve, 1)
            then(ts(U1[:], ANG[:], 1.0 / TWO_PI, ROUND, MUL, ADD))
            then(ts(U1[:], U1[:], -ROUND, None, ADD))
            for part in (PI_1, PI_2, PI_3):
                then(stt(ANG[:], U1[:], -part, ANG[:], MUL, ADD))
            ts(ANG[:], ANG[:], NEAR_PI, -NEAR_PI, ALU.min, ALU.max).then_inc(s5_dve, 1)
            dve.wait_ge(s5_act, 3)
            then(ts(SPT[:, 1], NEG8SP[:], 2.0, None, ADD))
            then(nc.vector.reciprocal(SPT[:, 1], SPT[:, 1]))
            then(tt(SPT[:, 1], SPT[:, 1], NEG8SP[:], MUL))
            then(tt(SPT[:, 2], SPT[:, 1], SPT[:, 1], MUL))
            then(ts(SPT[:, 3], SPT[:, 2], 1.0 / 17, None, MUL))
            for n in (15, 13, 11, 9, 7, 5, 3):
                then(stt(SPT[:, 3], SPT[:, 3], 1.0 / n, SPT[:, 2], ADD, MUL))
            then(stt(SPT[:, 3], SPT[:, 3], 1.0, SPT[:, 1], ADD, MUL))
            then(ts(SPT[:, 0], SPT[:, 0], 0.0, -8.0, ALU.max, MUL))
            then(stt(NEG8SP[:], SPT[:, 3], -16.0, SPT[:, 0], MUL, ADD))
            dve.wait_ge(root_done, 1)
            nc.vector.reciprocal(RSTD[:], RSTD[:]).then_inc(rstd_done, 1)
            ts(MAGF[:, 1, :], ANG[:, 8 * P:REP], 1.0 / TWO_PI, None, MUL)
            ts(MAGF[:, 0, :], MAG[:, 8 * P:REP], 1.0, None, MUL)
            dve.wait_ge(s5_act, 5)
            then(tt(COS[:, w], COS[:, w], COS[:, w], MUL))
            then(ts(COS[:, w], COS[:, w], -2.0, 1.0, MUL, ADD))
            tt(SIN[:, w], SIN[:, w], MAG[:, w], MUL)
            then(tt(COS[:, w], COS[:, w], MAG[:, w], MUL))
            tt(U1[:, w], RE[:, w], RE[:, w], MUL)
            tt(U2[:, w], IM[:, w], IM[:, w], MUL)
            then(ts(COS[:, w], COS[:, w], -1.0, None, ADD))
            then(tt(U1[:, w], U1[:, w], U2[:, w], ADD))
            nc.vector.reciprocal(U1[:, w], U1[:, w])
            tt(FR[:, w], COS[:, w], RE[:, w], MUL)
            then(tt(U2[:, w], SIN[:, w], IM[:, w], MUL))
            then(tt(FR[:, w], FR[:, w], U2[:, w], ADD))
            tt(FI[:, w], SIN[:, w], RE[:, w], MUL)
            then(tt(U2[:, w], COS[:, w], IM[:, w], MUL))
            then(tt(FI[:, w], FI[:, w], U2[:, w], SUB))
            tt(FR[:, w], FR[:, w], U1[:, w], MUL)
            then(tt(FI[:, w], FI[:, w], U1[:, w], MUL))

            def by_unit(t):
                return t[:, w].rearrange("p (u n) -> p u n", n=P)

            tt(U1[:, w], FR[:, w], B_RE[:, w], MUL)
            then(tt(U2[:, w], FI[:, w], B_IM[:, w], MUL))
            tt(BB[:, :, 0, :], by_unit(U1), by_unit(U2), SUB)
            tt(U3[:, w], FR[:, w], B_IM[:, w], MUL)
            then(tt(MAG[:, w], FI[:, w], B_RE[:, w], MUL))
            tt(BB[:, :, 1, :], by_unit(U3), by_unit(MAG), ADD).then_inc(bb_ready, 1)
            dve.wait_ge(bb_ready, 1)
            dve.wait_ge(rstd_done, 1)

            def h_tmp(j):
                dve.wait_ge(h_lo_done, j + 1)
                dve.wait_ge(sel_done, 2 * j + 1 + 1)
                tt(MOD[:, 0], A0[2][:, 0:36].rearrange("p (b n) -> p b n", n=9), bias9(C_BADA + 4 * j), ADD)
                dve.wait_ge(h_hi_done, j + 1)
                for kk in range(BLK):
                    ins = stt(HT[:, kk, :], X[:, 4 * j + kk, :], col(C_G + 4 * j + kk), RSTD[:], MUL, MUL)
                then(ins)

            def h_rows(j):
                dve.wait_ge(sel_done, 2 * j + 2 + 1)
                then(stt(MOD[:, 1], A0[3][:, 0:36].rearrange("p (b n) -> p b n", n=9), 1.0,
                         bias9(C_BADA + 32 + 4 * j), ADD, ADD))
                for kk in range(BLK):
                    ts(HT[:, kk, 0:TP], HT[:, kk, 0:TP], MOD[:, 1, kk, 0:1], MOD[:, 0, kk, 0:1], MUL, ADD)
                then(tt(HTS[:], HTS[:], MOD[:, 1, :, 1:9].unsqueeze(3).to_broadcast([P, BLK, DB, DS]), MUL))
                tt(HTS[:], HTS[:], MOD[:, 0, :, 1:9].unsqueeze(3).to_broadcast([P, BLK, DB, DS]), ADD).then_inc(
                    ht_done, 1)
                dve.wait_ge(h_hi_done, j + 1 + 1)
                tt(H_LO[:, bass.ds(4 * j, BLK), :], HT[:], H_HI[:, bass.ds(4 * j, BLK), :].bitcast(F32),
                   SUB).then_inc(h_lo_done, 1)

            with dve.Fori(0, ADA_1 - 1) as j:
                st.enter(j, 3)
                h_tmp(j)
                h_rows(j)
            st.leave(ADA_1 - 1)
            h_tmp(ADA_1 - 1)
            for c in range(AHEAD):
                lo(0, c)
            h_rows(ADA_1 - 1)

            with dve.Fori(0, ADA_J - ADA_1) as jj:
                st.enter(jj, 3)
                for c in range(AHEAD, AHEAD + 2 * SPH):
                    lo(2 * jj * SPH, c)
                    if c == AHEAD + SPH + 1:
                        h_tmp(jj + ADA_1)
                h_rows(jj + ADA_1)
            st.leave(ADA_J - ADA_1)

            def bank_ready(q, b, nb_next):
                if b < BLK - 1:
                    dve.wait_ge(bank_done, 3 * q + b + 1)
                else:
                    dve.wait_ge(slab_done, nb_next + 1)

            for part, (strip, samples) in enumerate(((CST, CSTS), (SG, SGS))):
                with dve.Fori(0, 2) as g:
                    nb = SLAB_U + (2 * part + g) * SPH
                    for c in range(AHEAD, AHEAD + SPH):
                        lo(nb, c)
                    for b in range(BLK):
                        if b == 0:
                            dve.wait_ge(part_c_in, 16 * (2 * part + g + 1))
                        bank_ready(Q_U + 2 * part + g, b, nb + SPH)
                        row, few = strip[:, 4 * g + b, 0:TP], samples[:, 4 * g + b, :, 1:]
                        tt(row, row, M[:, b, 0:TP], ADD)
                        tt(few, few, MS[:, b], ADD).then_inc(bank_free, 1)

            def freed(q, b):
                return 4 * q + b + 1 + BLK

            def turn(t, par):
                qr, qi = Q[par][:, 0, :], Q[par][:, 1, :]
                bu_re, bu_im = A0[0][:, 0:SW], A0[1][:, 0:SW]
                dve.wait_ge(bu_done, t + 1 + 1)
                dve.wait_ge(table_done, t + 1)
                tt(qr, bu_re, TCOS[par][:], MUL)
                tt(qi, bu_im, TCOS[par][:], MUL)
                then(tt(TMPD[:], bu_im, TSIN[par][:], MUL))
                then(tt(qr, qr, TMPD[:], ADD))
                tt(TMPD[:], bu_re, TSIN[par][:], MUL).then_inc(bu_used, 1)
                dve.wait_ge(bu_used, t + 1 + 1)
                then(tt(qi, qi, TMPD[:], SUB))
                then(nc.vector.tensor_copy(Q[par][:, :, TP:SW:DS + 1], S5H0[:, t, :, :]))
                dve.wait_ge(coef_done, t + 1)
                nc.vector.tensor_tensor_scan(qr, COEF[:], qr, 0.0, MUL, ADD)
                nc.vector.tensor_tensor_scan(qi, COEF[:], qi, 0.0, MUL, ADD).then_inc(q_done, 1)

            def conv_a(h, b):
                n = 4 * h + b
                dve.wait_ge(bank_free, freed(Q_A + 4 * h + 1, b))
                tt(PADA[:, b, 2:2 + TP], PADA[:, b, 2:2 + TP], AROW[:, n, 0:TP], MUL)
                then(tt(PADAS[:, b, :, 2:], PADAS[:, b, :, 2:], AROWS[:, n], MUL))
                ts(AROW[:, n, 0:TP], PADA[:, b, 0:TP], col(C_WCA + n), col(C_BCA + n), MUL, ADD)
                then(ts(AROWS[:, n], PADAS[:, b, :, 0:DS], col(C_WCA + n), col(C_BCA + n), MUL, ADD))
                for k in (1, 2):
                    stt(AROW[:, n, 0:TP], PADA[:, b, k:k + TP], col(C_WCA + 8 * k + n), AROW[:, n, 0:TP], MUL, ADD)
                    ins = stt(AROWS[:, n], PADAS[:, b, :, k:k + DS], col(C_WCA + 8 * k + n), AROWS[:, n], MUL, ADD)
                    if k == 1:
                        then(ins)
                if b == BLK - 1:
                    ins.then_inc(conva_done, 1)
                else:
                    then(ins)

            with dve.Fori(0, 2) as h:
                st.enter(h, 16 * 4 + 4 * 4 - 1)
                dve.wait_ge(pada_ready, h + 1)
                for m in range(4):
                    u = 4 * h + m
                    nb = SLAB_A + u * SPG
                    for c in range(AHEAD, AHEAD + SPG):
                        lo(nb, c)
                        if c in (4, 7, 10, 13):
                            turn(4 * u + c // 3 - 1, (c // 3 - 1) % 2)
                        if m == 2 and c in (5, 8, 11, 14):
                            conv_a(h, c // 3 - 1)
                        if m == 3 and c == 5:
                            dve.wait_ge(conva_done, h + 1)
                            dve.wait_ge(bank_free, freed(Q_A + 4 * h + 2, 3))
                            rows = AROW[:, bass.ds(4 * h, BLK), :]
                            tt(rows, rows, TMPA[:], MUL).then_inc(ab_done, 1)
                    if m == 3:
                        dve.wait_ge(ab_done, h + 1)
                        dve.wait_ge(bank_free, freed(Q_A + 4 * h + 3, 3))
                        rows = AROW[:, bass.ds(4 * h, BLK), :]
                        tt(rows, rows, TMPA[:], MUL).then_inc(ag_done, 1)
                    dve.wait_ge(y_done, 4 * u + 4 + 1)
                    stt(CST[:, u, :], CST[:, u, :], col(C_S5D + u), A0[2][:, 0:SW], MUL, ADD).then_inc(y_sum, 1)
            st.leave(2)

            for i in range(4):
                dve.wait_ge(y_hi_done, i + 1)
                tt(Y_LO[:, 2 * i:2 * i + 2, :], CST[:, 2 * i:2 * i + 2, :], Y_HI[:, 2 * i:2 * i + 2, :].bitcast(F32),
                   SUB).then_inc(y_lo_done, 1)
            for c in range(AHEAD, AHEAD + 2 * SPGG):
                lo(SLAB_G, c)
                if c in (6, 10):
                    g = (c - 6) // 4
                    dve.wait_ge(bank_free, freed(Q_G + g, 3))
                    tt(SG[:, 4 * g:4 * g + 4, :], SG[:, 4 * g:4 * g + 4, :], ZG[:], MUL).then_inc(z_used, 1)
            dve.wait_ge(z_used, 2)
            tt(CST[:], CST[:], SG[:], MUL).then_inc(c_done, 1)

            def conv_b(i, hd):
                n = 4 * i + hd
                ins = ts(XB[:, hd, :], PADB[:, hd, 0:XW], col(C_WCB + n), col(C_BCB + n), MUL, ADD)
                for k in (1, 2, 3):
                    then(ins)
                    ins = stt(XB[:, hd, :], PADB[:, hd, k:k + XW], col(C_WCB + 16 * k + n), XB[:, hd, :], MUL, ADD)
                return ins

            def lru(i, pr):
                dve.wait_ge(roots, 2 * i + pr + 1)
                nc.vector.memset(AA[:, :, TP + 2:XW - DS:DS + 3], 0.0)
                then(tt(TH[:], TH[:], IG[:], MUL))
                then(tt(TH[:], TH[:], XB[:, 2 * pr:2 * pr + 2, :], MUL))
                then(nc.vector.tensor_copy(TH[:, :, TP + 2:XW - DS:DS + 3],
                                           LRU0[:, bass.ds(4 * i + 2 * pr, 2), :]))
                for hd in range(2):
                    last = nc.vector.tensor_tensor_scan(R[:, hd, :], AA[:, hd, :], TH[:, hd, :], 0.0, MUL, ADD)
                last.then_inc(hs_done, 1)

            with dve.Fori(0, 4) as i:
                st.enter(i, 3 * 4 + 2 + 2 * 3)
                for g in range(2):
                    nb = SLAB_B + i * SPB + g * SPH
                    for c in range(AHEAD, AHEAD + (SPG if g else SPH)):
                        lo(nb, c)
                        if g == 1 and c in (4, 8):
                            pr = c // 8
                            if pr == 0:
                                dve.wait_ge(gates_done, 2 * i + 1)
                                dve.wait_ge(bank_free, freed(Q_B + 2 * i, 3))
                            then(conv_b(i, 2 * pr))
                            conv_b(i, 2 * pr + 1).then_inc(xb_ready, 1)
                        if g == 1 and c in (11, 17):
                            pr = c // 17
                            dve.wait_ge(lru_act, 4 * i + 2 * pr + 2)
                            stt(TH[:], R[:], 1.0, TH[:], ADD, MUL).then_inc(root_in, 1)
                        if g == 1 and c == 13:
                            lru(i, 0)
                    if g == 0:
                        dve.wait_ge(padb_ready, i + 1)
                        for b in range(BLK):
                            bank_ready(Q_B + 2 * i, b, nb + SPH)
                            row, few = PADB[:, b, 3:3 + TP], PADBS[:, b, :, 3:]
                            tt(row, row, M[:, b, 0:TP], ADD)
                            tt(few, few, MS[:, b], ADD).then_inc(bank_free, 1)
                lru(i, 1)
                dve.wait_ge(hs_out, 2 * i + 2 + 1)
                dve.wait_ge(bank_free, freed(Q_B + 2 * i + 1, 3))
                rows = BROW[:, bass.ds(4 * i, BLK), :]
                tt(rows, rows, SGB[:], MUL).then_inc(bg_done, 1)
            st.leave(4)

            for i in range(8):
                dve.wait_ge(mix_hi_done, i + 1)
                dst, hi_ = H_LO[:, 4 * i:4 * i + 4, :], H_HI[:, 4 * i:4 * i + 4, :].bitcast(F32)
                if i < 2:
                    tt(dst[:, :, 0:TP], CST[:, 4 * i:4 * i + 4, 0:TP], hi_[:, :, 0:TP], SUB)
                    tt(dst[:, :, TP:T].rearrange("p n (s w) -> p n s w", w=DS), CSTS[:, 4 * i:4 * i + 4, :, 1:],
                       hi_[:, :, TP:T].rearrange("p n (s w) -> p n s w", w=DS), SUB).then_inc(mix_lo_done, 1)
                else:
                    src = AROW[:, 4 * i - 8:4 * i - 4, :] if i < 4 else BROW[:, 4 * i - 16:4 * i - 12, :]
                    tt(dst, src, hi_, SUB).then_inc(mix_lo_done, 1)
            then(nc.vector.memset(SQS[:], 0.0))

            def group_o(j, last_group):
                for c in range(AHEAD, SPG + (2 if last_group else AHEAD)):
                    if c < SPG or not last_group:
                        lo(SLAB_O + j * SPG, c)
                    if c == 16:
                        dve.wait_ge(gsel_done, j + 1)
                        tt(MOD[:, 2], A0[1][:, 0:36].rearrange("p (b n) -> p b n", n=9),
                           bias9(C_BADA + 64 + 4 * j), ADD).then_inc(gmod_done, 1)
                dve.wait_ge(gmod_done, j + 1 + 1)
                dve.wait_ge(x_back, 16 * 8)
                dve.wait_ge(bank_free, freed(Q_O + j, 3))
                for b in range(BLK):
                    row = X[:, 4 * j + b, 0:TP]
                    stt(row, OT[:, b, 0:TP], MOD[:, 2, b, 0:1], row, MUL, ADD)
                then(tt(OTS[:], OTS[:], MOD[:, 2, :, 1:9].unsqueeze(3).to_broadcast([P, BLK, DB, DS]), MUL))
                rows = XS[:, bass.ds(4 * j, BLK)]
                tt(rows, rows, OTS[:], ADD).then_inc(y_done2, 1)
                for b in range(BLK):
                    dve.wait_ge(ysq_done, 4 * j + b + 1)
                    dve.wait_ge(ysq_used, 4 * j + b + 1)
                    tt(SQS[:], SQS[:], SQO[:, b % 2, :], ADD).then_inc(ysq_used, 1)

            with dve.Fori(0, N_O - 1) as j:
                st.enter(j, 1)
                group_o(j, False)
            st.leave(N_O - 1)
            group_o(N_O - 1, True)
            dve.wait_ge(yroot, 1)
            nc.vector.reciprocal(RST2[:], RST2[:]).then_inc(rstd2_done, 1)
            dve.wait_ge(rstd2_done, 1)
            for g in range(FIN_DVE):
                for b in range(BLK):
                    k = 4 * g + b
                    last = stt(X[:, k, :], X[:, k, :], col(C_GF + k), RST2[:], MUL, MUL)
                last.then_inc(fin_dve, 1)

        @block.gpsimd
        def _(pool):
            tt, ts, copy = nc.gpsimd.tensor_tensor, nc.gpsimd.tensor_scalar, nc.gpsimd.tensor_copy
            st = pool_step
            MUL, ADD, SUB = ALU.mult, ALU.add, ALU.subtract

            def wait(sem_, value):
                pool.wait_ge(sem_, value)
                if not isinstance(value, int):
                    pool.sem_inc(pool_passed, 1)

            def then(ins):
                st.up(ins)
                wait(st.sem, st.now())

            def pad_a(h):
                nc.gpsimd.memset(PADA[:, :, 0:2], 0.0)
                copy(PADAS[:, :, :, 0:2], CAST[:, bass.ds(4 * h, BLK)]).then_inc(pada_ready, 1)

            def frac(t, par):
                sin, cos = TSIN[par][:], TCOS[par][:]
                then(copy(TURN[:], MAGF[:, 1, bass.ds(t, 1)]))
                then(ts(sin, STEP[:], TURN[:], 1.0, MUL, MUL))
                then(ts(cos, sin, 1.0, ROUND, MUL, ADD))
                then(ts(cos, cos, 1.0, -ROUND, MUL, ADD))
                tt(sin, sin, cos, SUB).then_inc(frac_done, 1)

            for start, buf, dst in ((0, PART_C, part_c), (4, PART_B, part_b)):
                with pool.Fori(0, 4) as n:
                    nc.gpsimd.memset(buf[:], 0.0).then_inc(part_free, 1)
                    wait(bank_free, 4 * n + 4 * start + 8)
                    pool.dma_start(dst[n], buf[:]).then_inc(part_out, 16)
                    wait(part_out, 16 * n + 16 * start + 16)
            wait(h_lo_done, ADA_J + 1)
            wait(ada_used, 2 * ADA_J * SPG)
            for g in range(4):
                dst = CST if g < 2 else SG
                pool.dma_start(dst[:, 4 * (g % 2):4 * (g % 2) + 4], part_c[g]).then_inc(part_c_in, 16)
                wait(part_c_in, 16 * (g + 1))
            wait(bb_ready, 1)
            frac(0, 0)
            frac(1, 1)
            with pool.Fori(0, 2) as h:
                st.enter(h, 4 * (4 * 8 - 1))
                wait(ag_done, h + 1)
                pad_a(h)
                for m in range(4):
                    u = 4 * h + m
                    wait(y_done, 4 * u + 1)
                    pool.dma_start(CC[:], a["s5c"][u]).then_inc(cc_in, 16)
                    for j in range(4):
                        t = 4 * u + j
                        par = j % 2
                        qr, qi, cos, sin = Q[par][:, 0, :], Q[par][:, 1, :], TCOS[par][:], TSIN[par][:]
                        wait(q_done, t + 1 + 1)
                        wait(y_done, t + 1)
                        tt(HRI[:, 0, :], qr, cos, MUL)
                        then(tt(TMPP[:], qi, sin, MUL))
                        then(tt(HRI[:, 0, :], HRI[:, 0, :], TMPP[:], SUB))
                        tt(HRI[:, 1, :], qr, sin, MUL)
                        then(tt(TMPP[:], qi, cos, MUL))
                        tt(HRI[:, 1, :], HRI[:, 1, :], TMPP[:], ADD).then_inc(hs5_done, 1)
                        wait(hs5_done, t + 1)
                        ins = copy(STG_S[:, j], HRI[:, :, TP - 1:SW:DS + 1])
                        if j < 3:
                            then(ins)
                        else:
                            ins.then_inc(staged_s, 1)
                        frac(t + 2, par)
                    wait(staged_s, u + 1)
                    pool.dma_start(a["o_s5"][u], STG_S[:]).then_inc(out_s, 16)
                    wait(out_s, 16 * (u + 1))
                    if m == 2:
                        wait(conva_done, h + 1)
                        copy(STG_A[:, :, :, 0], PADA[:, :, TP:PA:DS + 2])
                        copy(STG_A[:, :, :, 1], PADA[:, :, TP + 1:PA:DS + 2]).then_inc(staged_a, 1)
                        wait(staged_a, h + 1)
                        pool.dma_start(a["o_ca"][h], STG_A[:]).then_inc(out_a, 16)
                        wait(out_a, 16 * (h + 1))
            st.leave(2)

            wait(slab_done, SLAB_B + 1)
            with pool.Fori(0, 4) as i:
                wait(bg_done, i + 1)
                pool.dma_start(PADB[:, :, 3:PB], part_b[i]).then_inc(part_b_in, 16)
                wait(part_b_in, 16 * (i + 1))
                nc.gpsimd.memset(PADB[:, :, 0:3], 0.0)
                copy(PADBS[:, :, :, 0:3], CBST[:, bass.ds(4 * i, BLK)]).then_inc(padb_ready, 1)
                wait(gates_done, 2 * i + 1)
                pool.dma_start(WG[:], a["wg"][i]).then_inc(wg_in, 16)
                wait(bank_free, 4 * (Q_B + 2 * i) + 8)
                copy(STG_B[:, :, :, 0], PADB[:, :, TP:PB:DS + 3])
                copy(STG_B[:, :, :, 1], PADB[:, :, TP + 1:PB:DS + 3])
                copy(STG_B[:, :, :, 2], PADB[:, :, TP + 2:PB:DS + 3]).then_inc(convb_staged, 1)
                wait(convb_staged, i + 1)
                pool.dma_start(a["o_cb"][i], STG_B[:]).then_inc(out_b, 16)
                for pr in range(2):
                    wait(hs_done, 2 * i + pr + 1)
                    copy(STG_H[:, 2 * pr:2 * pr + 2, :], R[:, :, TP - 1:XW:DS + 3]).then_inc(lru_staged, 1)
                wait(lru_staged, 2 * i + 2 + 1)
                pool.dma_start(a["o_lru"][i], STG_H[:]).then_inc(out_b, 16)
                wait(out_b, 32 * (i + 1))

            wait(mix_lo_done, 8)
            for g in range(8):
                pool.dma_start(X[:, 4 * g:4 * g + 4, :], a["x"][:, 4 * g:4 * g + 4, :]).then_inc(x_back, 16)
            wait(rstd2_done, 1)
            for k in range(4 * FIN_DVE, KT):
                tt(X[:, k, :], X[:, k, :], RST2[:], MUL).then_inc(fin_pool, 1)


def layouts():
    a0, b0, c0 = 0, 4 * W_A, 4 * W_A + 2 * W_B
    starts = [c0, c0 + COLS, c0 + W_C, c0 + W_C + COLS]
    for h in range(2):
        starts += [a0 + s * W_A + COLS * h for s in (1, 2, 0, 3)]
    for i in range(4):
        starts += [b0 + COLS * i, b0 + W_B + COLS * i]
    rows = [W_A + W_B + P * n for n in range(8)] + [P * n for n in range(8)] + [W_A + P * n for n in range(16)]
    return starts, rows


def slabs(w, starts, rows):
    out = []
    for s in starts:
        blk = np.stack([w[r:r + P, s:s + COLS] for r in rows])
        out.append(blk.reshape(len(rows) // 2, 2, P, COLS).transpose(0, 2, 1, 3).reshape(-1, P, SLAB))
    return np.concatenate(out)


def channel_major(v):
    v = np.asarray(v)
    v = v.reshape(*v.shape[:-1], v.shape[-1] // P, P)
    return np.moveaxis(v, -1, 0)


_OUTS = {"y": (8, P, 4, T), "o_ca": (2, P, BLK, 9, 2), "o_cb": (4, P, BLK, 9, 3), "o_lru": (4, P, BLK, 9),
         "o_s5": (8, P, BLK, 2, 9)}


def kernel(**inputs):
    import concourse.bacc as bacc
    from concourse.bass_utils import run_bass_kernel_spmd

    x = {k: np.asarray(v) for k, v in inputs.items()}
    f32 = np.float32
    l = {k: v[0] for k, v in x.items() if v.shape[0] == 1 and k not in ("x_prompt", "c_prompt")}
    starts, rows = layouts()
    kt = [P * k for k in range(KT)]
    lower, upper = kt[:KT // 2], kt[KT // 2:]
    b_x, b_g = starts[12::2], starts[13::2]
    w = np.concatenate([
        slabs(l["w_in"], starts[:4] + b_x, lower), slabs(l["w_in"], starts[:4], upper),
        slabs(l["w_in"], starts[4:12], kt), slabs(l["w_glu"], [0, COLS], kt[:8]),
        *(part for i in range(4) for part in (slabs(l["w_in"], [b_x[i]], upper), slabs(l["w_in"], [b_g[i]], kt))),
        slabs(l["w_out"], [COLS * j for j in range(8)], rows)])
    assert len(w) == SLABS
    order = [c for j in range(8) for c in (COLS * j, D + COLS * j)] + [2 * D + COLS * j for j in range(8)]
    ada = slabs(l["w_ada"], order, kt)
    tok = np.concatenate([x["x_prompt"][0], x["x_sample"].reshape(DB * DS, D)])
    xT = channel_major(tok).transpose(0, 2, 1)
    cT = np.zeros((P, KT, 32), f32)
    cT[:, :, 0:9] = channel_major(np.concatenate([x["c_prompt"], x["c_sample"]])).transpose(0, 2, 1)
    par = np.concatenate([channel_major(l[k].reshape(-1)) for k in (
        "b_ada", "g_norm", "w_conv_a", "b_conv_a", "w_conv_b", "b_conv_b", "b_rg", "b_ig", "lru_lambda", "b_glu",
        "s5_d")] + [channel_major(x["g_final"])], axis=1)
    assert par.shape[1] == N_PAR
    sel_ones = np.zeros((P, 9 + P), f32)
    for b in range(9):
        sel_ones[b::32, b] = 1
    sel_ones[:, 9:] = 1
    mask, step = np.ones(SW, f32), np.zeros(SW, f32)
    mask[TP::DS + 1] = 0
    step[0:TP] = np.arange(1, TP + 1)
    for b in range(DB):
        step[TP + 9 * b + 1:TP + 9 * b + 9] = np.arange(1, DS + 1)
    mask, step = (np.ascontiguousarray(np.broadcast_to(v, (P, SW))) for v in (mask, step))
    log_dt = np.broadcast_to(l["s5_log_dt"][:, None], (64, S5_P))
    rep = np.zeros((P, 3, REP), f32)
    for n, v in enumerate((l["s5_lambda_re"], l["s5_lambda_im"], log_dt)):
        by = v.reshape(8, 4, P)
        rep[:, n, 0:8 * P] = np.repeat(by.transpose(1, 0, 2).reshape(4, 8 * P), 32, axis=0)
        rep[:, n, 8 * P:8 * P + NST] = v.reshape(NST, P).T
    s5b = np.zeros((4, 2, S5_I, 2, 8, 2, S5_P), f32)
    s5c = np.zeros((8, 2, S5_P, 2, 4, 2, S5_I), f32)
    for n, (b_, c_) in enumerate((("s5_b_re", "s5_c_re"), ("s5_b_im", "s5_c_im"))):
        bv = l[b_].reshape(8, 4, 2, S5_P, S5_I)
        cv = l[c_].reshape(8, 4, 2, S5_I, S5_P)
        for g in range(2):
            s5b[:, g, :, n, :, g, :] = bv[:, :, g].transpose(1, 3, 0, 2)
            s5c[:, g, :, n, :, g, :] = cv[:, :, g].transpose(0, 3, 1, 2)
    s5h0 = np.stack([l["state_s5_re"].reshape(DB, NST, P), l["state_s5_im"].reshape(DB, NST, P)])
    wg = np.stack([l["w_rg"], l["w_ig"]]).reshape(2, 4, BLK, P, P)
    arrays = {
        "w": w, "ada": ada, "x": xT, "c": cT, "par": par, "sel_ones": sel_ones, "mask": mask, "step": step,
        "rep": rep, "s5b": s5b.reshape(P, 2, 8 * P), "s5c": s5c.reshape(8, P, 2, BLK, 32),
        "s5h0": s5h0.transpose(3, 2, 0, 1), "wg": wg.transpose(1, 3, 2, 0, 4),
        "cb": channel_major(l["state_conv_b"]).transpose(0, 3, 1, 2),
        "lru": channel_major(l["state_lru_h"]).transpose(0, 2, 1),
        "ca": channel_major(l["state_conv_a"]).transpose(0, 3, 1, 2),
    }
    arrays = {f"in_{k}": np.ascontiguousarray(v) for k, v in arrays.items()}
    nc = bacc.Bacc("TRN2", target_bir_lowering=False, num_devices=1)
    aps = {k[3:]: nc.dram_tensor(k, v.shape, mybir.dt.from_np(v.dtype), kind="ExternalInput").ap()
           for k, v in arrays.items()}
    for k, shape in _OUTS.items():
        aps[k] = nc.dram_tensor(f"out_{k}", shape, F32, kind="ExternalOutput").ap()
    build(nc, aps)
    r = run_bass_kernel_spmd(nc, [arrays], core_ids=[0]).results[0]
    y, ca, cb, lru, s5 = (np.asarray(r[f"out_{k}"]) for k in _OUTS)
    y = y.transpose(3, 0, 2, 1).reshape(T, D)
    ca = ca.transpose(3, 4, 0, 2, 1).reshape(9, 2, W_A)
    cb = cb.transpose(3, 4, 0, 2, 1).reshape(9, 3, W_B)
    lru = lru.transpose(3, 0, 2, 1).reshape(9, W_B)
    s5 = s5.transpose(3, 4, 0, 2, 1).reshape(2, 9, 64, S5_P)
    both = [ca, cb, lru, s5[0], s5[1]]
    c = np.ascontiguousarray
    return (c(y[None, 0:TP]), c(y[TP:].reshape(DB, DS, D)), *(c(v[None, 0:1]) for v in both),
            *(c(v[None, 1:9]) for v in both))
```

```python
from contextlib import ExitStack

import concourse.bass as bass
import numpy as np
from concourse import mybir

F32 = mybir.dt.float32
F32R = mybir.dt.float32r
ALU = mybir.AluOpType
ACT = mybir.ActivationFunctionType

P = 128
D = 4096
KT = D // P
TP, DB, DS = 256, 8, 8
T = TP + DB * DS
W_A, W_B, W_C = D // 4, D // 2, D // 4
S5_P, S5_I = 64, 16
EPS = 1e-6

COLS = 512
SLAB = 2 * COLS
BLK = COLS // P
SPG = KT // 2
AHEAD = 3
RING = 4
SPH = SPG // 2
SPGG = W_C // P // 2
N_P, N_U, N_A, N_G, N_B, N_O = 8, 4, 8, 2, 8, 8
SLAB_U = N_P * SPH
SLAB_A = SLAB_U + N_U * SPH
SLAB_G = SLAB_A + N_A * SPG
SLAB_B = SLAB_G + N_G * SPGG
SPB = SPH + SPG
SLAB_O = SLAB_B + N_B // 2 * SPB
SLABS = SLAB_O + N_O * SPG
Q_U = N_P
Q_A = Q_U + N_U
Q_G = Q_A + N_A
Q_B = Q_G + N_G
Q_O = Q_B + N_B
ADA_J = 8
ADA_1 = ADA_J // 2

SW = TP + DB * (DS + 1)
PA = 2 + TP + DB * (DS + 2)
PB = 3 + TP + DB * (DS + 3)
XW = PB - 3

C_BADA, C_G, C_WCA, C_BCA, C_WCB, C_BCB = 0, 96, 128, 152, 160, 224
C_BRG, C_BIG, C_LAM, C_BGLU, C_S5D, C_GF = 240, 256, 272, 288, 296, 304
N_PAR = 336
NST = 32
REP = 8 * P + NST + 8

TWO_PI = 6.283185307179586
PI_1 = 6.28125
PI_2 = 2029.0 / 2**20
PI_3 = TWO_PI - PI_1 - PI_2
ROUND = 12582912.0
NEAR_PI = 3.1415925


class Tally:

    def __init__(self, sem):
        self.sem, self.base, self.local = sem, 0, 0

    def up(self, ins):
        ins.then_inc(self.sem, 1)
        self.local += 1
        return ins

    def now(self):
        return self.base + self.local

    def enter(self, i, per):
        self.start, self.per = self.now(), per
        self.base, self.local = self.start + i * per, 0

    def leave(self, n):
        assert self.local == self.per, (self.sem.name, self.local, self.per)
        self.base, self.local = self.start + n * self.per, 0


def build(nc, a):
    ctx = ExitStack()
    with ctx:
        def sem(name):
            return ctx.enter_context(nc.semaphore(name))

        ORIGIN, WORDS = 16512, 53208

        def at(name, off, *shape, dt=F32):
            n = int(np.prod(shape))
            assert off + n <= WORDS, name
            t = nc.alloc_sbuf_tensor_at(name, [P, *shape], dt, offset=ORIGIN + 4 * off)
            return t

        o = 0

        def take(n):
            nonlocal o
            start = o
            o += -(-n // 8) * 8
            return start

        NC_ = 8 * SW
        o_act = take(NC_ + 24 * T)
        o_h = take(2 * KT * T)
        o_raw = take(RING * SLAB)
        o_w = take(2 * RING * SLAB)
        X = at("x", o_act, KT, T)
        ACTS = at("acts", o_act, NC_ + 24 * T)
        H_HI = at("h_hi", o_h, KT, T, dt=F32R)
        H_LO = at("h_lo", o_h + KT * T, KT, T, dt=F32R)
        RAW = at("w_raw", o_raw, RING, SLAB)
        W_HI = at("w_hi", o_w, RING, 2, COLS, dt=F32R)
        W_LO = at("w_lo", o_w + RING * SLAB, RING, 2, COLS, dt=F32R)
        ADA = at("ada_ring", o_w, 2 * RING, 2, COLS)
        ADAX = at("ada_ring_x", o_act, RING, 2, COLS)
        o_ct = take(KT * 32)
        CT = at("c_T", o_ct, KT, 32)
        PAR = at("par", take(N_PAR), N_PAR)
        SELONES = at("sel_ones", take(9 + P), 9 + P)
        SEL, ONES = SELONES[:, 0:9], SELONES[:, 9:9 + P]
        o_s5h0 = take(512)
        S5H0 = at("s5_h0", o_s5h0, NST, 2, DB)
        o_cb = take(384)
        CBST = at("convb_state", o_cb, 16, DB, 3)
        LRU0 = at("lru_h0", take(128), 16, DB)
        CAST = at("conva_state", take(128), 8, DB, 2)
        MOD = at("mod", take(108), 3, BLK, 9)
        MAGF = at("s5_mag_turn", take(80), 2, NST + 8)
        TURN = at("s5_turn", take(1), 1)
        EPSC = at("eps", take(1), 1)
        NEG8SP = at("neg8softplus", take(16), 16)
        STG_A = at("stage_a", take(72), BLK, 9, 2)
        STG_B = at("stage_b", take(108), BLK, 9, 3)
        STG_H = at("stage_h", take(36), BLK, 9)
        STG_S = at("stage_s", take(72), BLK, 2, 9)
        s = o
        T0 = [at(f"s5t{i}", o_h + REP * i, REP) for i in range(14)]
        SPT = at("softplus_tmp", s + 2048, 4, 16)
        SQ = at("x_sq", o_h + 14 * REP, 2, 4 * T)
        SQA = at("x_sqa", o_h + 14 * REP + 8 * T, 4 * T)
        BB = at("s5_bb", s, 8, 2, P)
        CC = at("s5_cc", s + 2048, 2, BLK, 32)
        BBU_HI = at("s5_bb_unit_hi", s + 2304, 2, P, dt=F32R)
        MASK = at("s5_mask", s + 2560, SW)
        STEP = at("s5_step", s + 2888, SW)
        RSTD = at("rstd", s + 3216, T)
        HT = at("h_tmp", s + 3536, BLK, T)
        ACCS = at("ada_acc", s + 4816, COLS)
        o_part = (WORDS - 4 * XW) // 8 * 8
        assert o_part >= s + 4816 + COLS
        PART_C = at("part_c", o_part, BLK, SW)
        PART_B = at("part_b", o_part, BLK, XW)
        COEF = at("s5_coef", s + 3216, SW)
        TMPD = at("s5_tmpd", s + 3544, SW)
        TMPP = at("s5_tmpp", s + 3872, SW)
        HRI = [at("s5_h0_", s + 4200, 2, SW), at("s5_h1_", o_ct, 2, SW)]
        UU_LO = at("s5_u_unit_lo", o_ct + 2 * SW, SW, dt=F32R)
        assert 3 * SW <= KT * 32
        BBU_LO = at("s5_bb_unit_lo", o_cb, 2, P, dt=F32R)
        o_b = o_act + NC_ + 8 * T
        o_s5 = o_b + NC_
        SG = at("silu_c", o_b, 8, SW)
        UU_HI = at("s5_u_unit_hi", s + 5184, SW, dt=F32R)
        TCOS = [at("cos0", o_s5, SW), at("cos1", o_s5 + SW, SW)]
        TSIN = [at("sin0", o_s5 + 2 * SW, SW), at("sin1", s + 4856, SW)]
        Q = [at("q0", o_s5 + 3 * SW, 2, SW), at("q1", o_s5 + 5 * SW, 2, SW)]
        assert 7 * SW + NC_ <= 16 * T
        o_pad = (WORDS - 4 * PA) // 8 * 8
        assert o_pad >= s + 5184 + SW
        PADA = at("pad_a", o_pad, BLK, PA)
        TMPA = at("tmp_a", o_pad, BLK, T)
        Y_HI = at("y_hi", s, 8, SW, dt=F32R)
        Y_LO = at("y_lo", s + NC_, 8, SW, dt=F32R)
        ZG = at("z_glu", o_pad, BLK, SW)
        WG = at("w_gates", s, BLK, 2, P)
        PADB = at("pad_b", s + 1024, BLK, PB)
        SGB = at("silu_b", s + 1024, BLK, T)
        XB = at("xb", s + 2416, BLK, XW)
        R = at("lru_r", s + 3792, 2, XW)
        IG = at("lru_i", s + 4480, 2, XW)
        AA = at("lru_a", s + 5168, 2, XW)
        TH = at("lru_t", s + 5856, 2, XW)
        ADA2 = at("gate_ring", s, RING, 2, COLS)
        OT = at("out_tmp", s + 4096, BLK, T)
        SQO = at("y_sq", s + 5376, 2, T)
        SQS = at("y_sqs", s + 6016, T)
        RST2 = at("rstd2", s + 6336, T)
        ACC2 = at("gate_acc", o_s5h0, COLS)

        CST = ACTS[:, 0:NC_].rearrange("p (n w) -> p n w", w=SW)
        CSTS = CST[:, :, TP:SW].rearrange("p n (s w) -> p n s w", w=DS + 1)
        AROW = ACTS[:, NC_:NC_ + 8 * T].rearrange("p (n w) -> p n w", w=T)
        AROWS = AROW[:, :, TP:T].rearrange("p n (s w) -> p n s w", w=DS)
        BROW = ACTS[:, NC_ + 8 * T:NC_ + 24 * T].rearrange("p (n w) -> p n w", w=T)
        BROWS = BROW[:, :, TP:T].rearrange("p n (s w) -> p n s w", w=DS)
        SGS = SG[:, :, TP:SW].rearrange("p n (s w) -> p n s w", w=DS + 1)
        PADAS = PADA[:, :, 2 + TP:PA].rearrange("p n (s w) -> p n s w", w=DS + 2)
        PADBS = PADB[:, :, 3 + TP:PB].rearrange("p n (s w) -> p n s w", w=DS + 3)
        XS = X[:, :, TP:T].rearrange("p n (s w) -> p n s w", w=DS)
        HTS = HT[:, :, TP:T].rearrange("p n (s w) -> p n s w", w=DS)
        OTS = OT[:, :, TP:T].rearrange("p n (s w) -> p n s w", w=DS)

        M = ctx.enter_context(nc.psum_tensor("m", [P, BLK, 512], F32))
        A0 = [ctx.enter_context(nc.psum_tensor(f"aux{i}", [P, 512], F32)) for i in range(4)]
        PART_CS = PART_C[:, :, TP:SW].rearrange("p n (s w) -> p n s w", w=DS + 1)
        PART_BS = PART_B[:, :, TP:XW].rearrange("p n (s w) -> p n s w", w=DS + 3)
        MS = M[:, :, TP:T].rearrange("p n (s w) -> p n s w", w=DS)

        part_c, part_b = (nc.dram_tensor(k, (n, P, BLK, width), F32, kind="Internal").ap()
                          for k, n, width in (("part_c", 2, SW), ("part_b", 4, XW)))

        small_in, x_in, s5_in = sem("small_in"), sem("x_in"), sem("s5_in")
        w_landed = [sem(f"w_landed{i}") for i in range(RING)]
        ada_landed = [sem(f"ada_landed{i}") for i in range(2 * RING)]
        adax_landed = [sem(f"adax_landed{i}") for i in range(RING)]
        part_free, part_out, part_c_in, part_b_in = map(sem, ["part_free", "part_out", "part_c_in", "part_b_in"])
        gate_landed = [sem(f"gate_landed{i}") for i in range(RING)]
        ada_used, gate_used = sem("ada_used"), sem("gate_used")
        w_hi_done, w_lo_done, slab_done, bank_done, bank_free = map(
            sem, ["w_hi_done", "w_lo_done", "slab_done", "bank_done", "bank_free"])
        sq_done, sqa_done, sum_done, root_done, rstd_done = map(
            sem, ["sq_done", "sqa_done", "sum_done", "root_done", "rstd_done"])
        acc_out, sel_done, ht_done, h_hi_done, h_lo_done = map(
            sem, ["acc_out", "sel_done", "ht_done", "h_hi_done", "h_lo_done"])
        s5_act, s5_dve, bb_ready = map(sem, ["s5_act", "s5_dve", "bb_ready"])
        frac_done, table_done, coef_done, bbu_ready, cc_in, cc_ready = map(
            sem, ["frac_done", "table_done", "coef_done", "bbu_ready", "cc_in", "cc_ready"])
        bu_done, bu_used, q_done, hs5_done, y_done, y_sum, staged_s, out_s = map(
            sem, ["bu_done", "bu_used", "q_done", "hs5_done", "y_done", "y_sum", "staged_s", "out_s"])
        pada_ready, conva_done, ab_done, ag_done, out_a = map(
            sem, ["pada_ready", "conva_done", "ab_done", "ag_done", "out_a"])
        sg_cleared = sem("sg_cleared")
        bbu_hi_done, c_back, cb_in = map(sem, ["bbu_hi_done", "c_back", "cb_in"])
        silu_done, silu_a_done, silu_b_done = map(sem, ["silu_done", "silu_a_done", "silu_b_done"])
        gelu_done, y_hi_done, y_lo_done, z_used = map(sem, ["gelu_done", "y_hi_done", "y_lo_done", "z_used"])
        wg_in, padb_ready, xb_ready, gates_done, gates_used, root_in, roots, hs_done, hs_out, lru_staged = map(
            sem, ["wg_in", "padb_ready", "xb_ready", "gates_done", "gates_used", "root_in", "roots", "hs_done",
                  "hs_out", "lru_staged"])
        out_b, bg_done, convb_staged = sem("out_b"), sem("bg_done"), sem("convb_staged")
        mix_hi_done, mix_lo_done, x_back, gacc_out, gsel_done, gmod_done = map(
            sem, ["mix_hi_done", "mix_lo_done", "x_back", "gacc_out", "gsel_done", "gmod_done"])
        res_done, ysq_done, yroot, rstd2_done, fin_dve, fin_pool, out_y = map(
            sem, ["res_done", "ysq_done", "yroot", "rstd2_done", "fin_dve", "fin_pool", "out_y"])
        ysq_used, lru_act, staged_a, c_done, fin_act = map(
            sem, ["ysq_used", "lru_act", "staged_a", "c_done", "fin_act"])
        pe_tail, pool_passed, act_passed = sem("pe_tail"), sem("pool_passed"), sem("act_passed")
        act_step, dve_step, pool_step = Tally(sem("act_step")), Tally(sem("dve_step")), Tally(sem("pool_step"))

        from_one = [ht_done, h_hi_done, h_lo_done, sel_done, slab_done, bu_used, y_sum, gates_used,
                    hs_out, lru_staged, gates_done, bg_done, ag_done, y_done, q_done, bu_done,
                    res_done, ysq_used, gmod_done]

        block = ctx.enter_context(nc.Block())
        MIX_AT = (6, 8, 11, 13)
        FIN_DVE = 6

        @block.sync
        def _(sp):
            for one in from_one:
                sp.sem_inc(one, 1)
            for n in range(2 * RING):
                sp.dma_start(ADA[:, n], a["ada"][n]).then_inc(ada_landed[n], 16)
            with sp.Fori(1, 2 * ADA_1 * SPG // (2 * RING)) as r:
                for n in range(2 * RING):
                    sp.wait_ge(ada_used, r * 2 * RING + n + 1 - 2 * RING)
                    sp.dma_start(ADA[:, n], a["ada"][r * 2 * RING + n]).then_inc(ada_landed[n], 16)
            first = 2 * ADA_1 * SPG
            for n in range(RING):
                sp.dma_start(RAW[:, n], a["w"][n]).then_inc(w_landed[n], 16)
            for n in range(RING):
                if n == 0:
                    sp.wait_ge(ht_done, 3 + 1)
                if n == 3:
                    sp.wait_ge(ht_done, 4 + 1)
                sp.dma_start(ADAX[:, n], a["ada"][first + n]).then_inc(adax_landed[n], 16)
            with sp.Fori(0, first // (2 * RING) - 1) as r:
                for n in range(RING):
                    for m in (2 * n, 2 * n + 1):
                        sp.wait_ge(ada_used, first + r * 2 * RING + m + 1)
                        sp.dma_start(ADAX[:, m % RING], a["ada"][first + RING + r * 2 * RING + m]).then_inc(
                            adax_landed[m % RING], 16)
                    sp.wait_ge(w_lo_done, r * RING + n + 1)
                    sp.dma_start(RAW[:, n], a["w"][(r + 1) * RING + n]).then_inc(w_landed[n], 16)
            for n in range(RING):
                sp.wait_ge(ada_used, 2 * first - 2 * RING + n + 1)
                sp.dma_start(ADAX[:, n], a["ada"][2 * first - RING + n]).then_inc(adax_landed[n], 16)
            with sp.Fori(N_P * SPH // RING, SLAB_O // RING + 1) as r:
                for n in range(RING):
                    sp.wait_ge(w_lo_done, r * RING + n + 1 - RING)
                    sp.dma_start(RAW[:, n], a["w"][r * RING + n]).then_inc(w_landed[n], 16)
            sp.wait_ge(bg_done, 4 + 1)
            sp.wait_ge(lru_staged, 8 + 1)
            sp.wait_ge(convb_staged, 4)
            for n in range(RING):
                sp.dma_start(ADA2[:, n], a["ada"][2 * ADA_J * SPG + n]).then_inc(gate_landed[n], 16)
            with sp.Fori(0, N_O * SPG // RING - 1) as r:
                for n in range(RING):
                    sp.wait_ge(w_lo_done, SLAB_O + r * RING + n + 1)
                    sp.dma_start(RAW[:, n], a["w"][SLAB_O + (r + 1) * RING + n]).then_inc(w_landed[n], 16)
                    sp.wait_ge(gate_used, r * RING + n + 1)
                    sp.dma_start(ADA2[:, n], a["ada"][2 * ADA_J * SPG + (r + 1) * RING + n]).then_inc(
                        gate_landed[n], 16)
            for half in range(2):
                sp.wait_ge(fin_dve, half + 1)
                sp.dma_start(a["y"][0, :, 2 * half:2 * half + 2], X[:, 2 * half:2 * half + 2]).then_inc(out_y, 16)
            for g in range(1, FIN_DVE):
                sp.wait_ge(fin_dve, g + 2)
                sp.dma_start(a["y"][g], X[:, 4 * g:4 * g + 4]).then_inc(out_y, 16)
            for g in range(FIN_DVE, ADA_J):
                sp.wait_ge(fin_act, g + 1 - FIN_DVE)
                sp.dma_start(a["y"][g], X[:, 4 * g:4 * g + 4]).then_inc(out_y, 16)
            sp.wait_ge(out_y, 16 * (ADA_J + 1))
            sp.wait_ge(part_out, 16 * (4 + 2))
            sp.wait_ge(out_s, 16 * 8)
            sp.wait_ge(out_a, 16 * 2)
            sp.wait_ge(out_b, 32 * 4)

        @block.tensor
        def _(pe):
            mm = nc.tensor.matmul

            def slab(nb, c, nk, q, hi, lo, width, k0=0):
                pe.wait_ge(w_lo_done, nb + c + 1)
                s_ = c % RING
                for b in range(BLK):
                    if c == 0:
                        pe.wait_ge(bank_free, 4 * q + b + 1)
                    for kk in range(2):
                        k = k0 + 2 * c + kk
                        w_hi = W_HI[:, s_, kk, b * P:(b + 1) * P]
                        w_lo = W_LO[:, s_, kk, b * P:(b + 1) * P]
                        out = M[:, b, 0:width]
                        mm(out, w_hi, hi[:, k, :], start=k == k0, stop=False)
                        mm(out, w_hi, lo[:, k, :], start=False, stop=False)
                        last = mm(out, w_lo, hi[:, k, :], start=False, stop=k == k0 + nk - 1)
                    if k == k0 + nk - 1 and b < BLK - 1:
                        last.then_inc(bank_done, 1)
                last.then_inc(slab_done, 1)

            pe.wait_ge(small_in, 16 * 6)
            pe.wait_ge(sqa_done, 8)
            for i in range(4):
                last = mm(A0[3][:, 0:T], ONES, SQA[:, i * T:(i + 1) * T], start=i == 0, stop=i == 3)
            last.then_inc(sum_done, 1)
            def ada_slab(part, sl, slot):
                for kk in range(2):
                    k = 2 * sl + kk
                    r = 32 * (k % 4)
                    last = mm(A0[part][r:r + 32, :], CT[:, k, :], slot[:, kk, :], start=k < 4, stop=k >= KT - 4)
                last.then_inc(ada_used, 1)

            def ada_sum(j, part):
                pe.wait_ge(acc_out, 2 * j + part + 1)
                pe.wait_ge(ht_done, j + 1)
                for b in range(BLK):
                    last = mm(A0[2 + part][:, 9 * b:9 * b + 9], ACCS[:, b * P:(b + 1) * P], SEL, start=True, stop=True)
                last.then_inc(sel_done, 1)

            with pe.Fori(0, ADA_1) as j:
                for part in range(2):
                    for sl in range(SPG):
                        pe.wait_ge(ada_landed[sl % 8], 64 * j + 32 * part + 16 * (sl // 8 + 1))
                        ada_slab(part, sl, ADA[:, sl % 8])
                    if part == 0:
                        pe.wait_ge(rstd_done, 1)
                    ada_sum(j, part)

            with pe.Fori(0, ADA_J - ADA_1) as jj:
                for part in range(2):
                    for c in range(SPH):
                        for sl in (2 * c, 2 * c + 1):
                            pe.wait_ge(adax_landed[sl % RING], 128 * jj + 64 * part + 16 * (sl // RING + 1))
                            ada_slab(part, sl, ADAX[:, sl % RING])
                        if c % 2 == 0:
                            pe.wait_ge(h_lo_done, c // 2 + 1 + 1)
                        slab((2 * jj + part) * SPH, c, KT // 2, 2 * jj + part, H_HI, H_LO, T)
                    ada_sum(jj + ADA_1, part)

            with pe.Fori(0, N_U) as g:
                for c in range(SPH):
                    if c % 2 == 0:
                        pe.wait_ge(h_lo_done, ADA_1 + c // 2 + 1 + 1)
                    slab(SLAB_U + g * SPH, c, KT // 2, Q_U + g, H_HI, H_LO, T, k0=KT // 2)

            with pe.Fori(0, N_A) as u:
                for c in range(SPG):
                    slab(SLAB_A + u * SPG, c, KT, Q_A + u, H_HI, H_LO, T)
                    if c in (1, 3, 6, 9):
                        j = c // 3
                        if j == 0:
                            pe.wait_ge(bbu_ready, u + 1)
                        pe.wait_ge(bu_used, 4 * u + j + 1)
                        r = slice(32 * j, 32 * j + 32)
                        for n in range(2):
                            out = A0[n][:, 0:SW]
                            mm(out, BBU_HI[r, n, :], UU_HI[r, :], start=True, stop=False)
                            mm(out, BBU_HI[r, n, :], UU_LO[r, :], start=False, stop=False)
                            last = mm(out, BBU_LO[r, n, :], UU_HI[r, :], start=False, stop=True)
                        last.then_inc(bu_done, 1)
                    if c in (8, 15):
                        pair = c // 15
                        if pair == 0:
                            pe.wait_ge(cc_ready, u + 1)
                            pe.wait_ge(y_sum, u + 1)
                        pe.wait_ge(hs5_done, 4 * u + 2 * pair + 2)
                        for n in range(2):
                            for par in range(2):
                                j = 2 * pair + par
                                last = mm(A0[2][32 * j:32 * j + 32, 0:SW], CC[:, n, j, :], HRI[par][:, n, :],
                                          start=n == 0, stop=n == 1)
                        last.then_inc(y_done, 1)

            with pe.Fori(0, N_G) as g:
                for c in range(SPGG):
                    pe.wait_ge(y_lo_done, c + 1)
                    slab(SLAB_G + g * SPGG, c, 8, Q_G + g, Y_HI, Y_LO, SW)

            with pe.Fori(0, N_B // 2) as i:
                for c in range(SPH):
                    slab(SLAB_B + i * SPB, c, KT // 2, Q_B + 2 * i, H_HI, H_LO, T, k0=KT // 2)
                for c in range(SPG):
                    slab(SLAB_B + i * SPB + SPH, c, KT, Q_B + 2 * i + 1, H_HI, H_LO, T)
                    if c in (5, 11):
                        pr = c // 6
                        if pr == 0:
                            pe.wait_ge(wg_in, 16 * (i + 1))
                        pe.wait_ge(xb_ready, 2 * i + pr + 1)
                        pe.wait_ge(gates_used, 2 * i + pr + 1)
                        for hd in range(2):
                            for w in range(2):
                                last = mm(A0[2 * w + hd][:, 0:XW], WG[:, 2 * pr + hd, w, :],
                                          XB[:, 2 * pr + hd, :], start=True, stop=True)
                        last.then_inc(gates_done, 1)

            pe.wait_ge(c_back, 16)
            per = [0, 1] + [2, 1] * 5 + [0] * 4
            with pe.Fori(0, N_O) as j:
                n = 0
                for c in range(SPG):
                    if c % 2 == 0:
                        pe.wait_ge(mix_lo_done, c // 2 + 1)
                    slab(SLAB_O + j * SPG, c, KT, Q_O + j, H_HI, H_LO, T)
                    for _ in range(per[c]):
                        pe.wait_ge(gate_landed[n % RING], 64 * j + 16 * (n // RING + 1))
                        for kk in range(2):
                            k = 2 * n + kk
                            r = 32 * (k % 4)
                            last = mm(A0[0][r:r + 32, :], CT[:, k, :], ADA2[:, n % RING, kk, :], start=k < 4,
                                      stop=k >= KT - 4)
                        last.then_inc(gate_used, 1)
                        n += 1
                    if c == 13:
                        pe.wait_ge(gacc_out, j + 1)
                        pe.wait_ge(gmod_done, j + 1)
                        for b in range(BLK):
                            last = mm(A0[1][:, 9 * b:9 * b + 9], ACC2[:, b * P:(b + 1) * P], SEL, start=True,
                                      stop=True)
                        last.then_inc(gsel_done, 1)
            pe.wait_ge(ysq_used, 32 + 1)
            mm(A0[2][:, 0:T], ONES, SQS[:], start=True, stop=True).then_inc(pe_tail, 1)

        @block.scalar
        def _(act):
            fn = nc.scalar.activation
            st = act_step

            def then(ins):
                st.up(ins)
                act.wait_ge(st.sem, st.now())

            def hi(nb, c, first=False):
                act.wait_ge(w_landed[c % RING], 4 * nb + 16 * (c // RING + 1))
                if not first:
                    act.wait_ge(slab_done, nb + c + 1 - RING + 1)
                fn(W_HI[:, c % RING], RAW[:, c % RING].rearrange("p (k n) -> p k n", k=2), ACT.Copy).then_inc(
                    w_hi_done, 1)

            def bank_ready(q, b, nb_next):
                if b < BLK - 1:
                    act.wait_ge(bank_done, 3 * q + b + 1)
                else:
                    act.wait_ge(slab_done, nb_next + 1)

            act.dma_start(X[:], a["x"]).then_inc(x_in, 16)
            for dst, name in ((CT, "c"), (PAR, "par"), (SELONES, "sel_ones"), (S5H0, "s5h0"), (LRU0, "lru"),
                              (CAST, "ca")):
                act.dma_start(dst[:], a[name]).then_inc(small_in, 16)
            for i in range(3):
                act.dma_start(T0[i][:], a["rep"][:, i, :]).then_inc(s5_in, 16)
            for i in range(2):
                act.dma_start(T0[3 + i][:, 0:8 * P], a["s5b"][:, i, :]).then_inc(s5_in, 16)
            act.dma_start(MASK[:], a["mask"]).then_inc(s5_in, 16)
            act.dma_start(STEP[:], a["step"]).then_inc(s5_in, 16)

            act.wait_ge(x_in, 16)
            for i in range(8):
                if i >= 2:
                    act.wait_ge(sqa_done, i - 1)
                fn(SQ[:, i % 2, :], X[:, 4 * i:4 * i + 4, :].rearrange("p k t -> p (k t)"),
                   ACT.Square).then_inc(sq_done, 1)
            act.wait_ge(sum_done, 1)
            act.wait_ge(s5_dve, 1)
            fn(RSTD[:], A0[3][:, 0:T], ACT.Sqrt, scale=1.0 / D, bias=EPSC[:]).then_inc(root_done, 1)

            act.wait_ge(s5_in, 16 * 7)
            fn(T0[2][:], T0[2][:], ACT.Exp).then_inc(s5_act, 1)
            act.wait_ge(s5_dve, 2)
            fn(T0[6][:], T0[6][:], ACT.Exp).then_inc(s5_act, 1)
            act.wait_ge(small_in, 16 * 6)
            act.wait_ge(s5_dve, 3)
            fn(NEG8SP[:], NEG8SP[:], ACT.Exp).then_inc(s5_act, 1)
            act.wait_ge(s5_dve, 4)
            fn(T0[7][:], T0[5][:], ACT.Sin).then_inc(s5_act, 1)
            fn(T0[8][:], T0[5][:], ACT.Sin, scale=0.5).then_inc(s5_act, 1)

            def acc_copy(j, part):
                act.wait_ge(ada_used, 32 * j + 16 * (part + 1))
                act.wait_ge(sel_done, 2 * j + part + 1)
                fn(ACCS[:], A0[part][:], ACT.Copy).then_inc(acc_out, 1)

            def h_hi(j):
                act.wait_ge(ht_done, j + 1 + 1)
                fn(H_HI[:, bass.ds(4 * j, 4), :], HT[:], ACT.Copy).then_inc(h_hi_done, 1)

            with act.Fori(0, ADA_1 - 1) as j:
                for part in range(2):
                    acc_copy(j, part)
                act.wait_ge(bb_ready, 1)
                h_hi(j)
            for part in range(2):
                acc_copy(ADA_1 - 1, part)
            act.wait_ge(ada_used, 2 * ADA_1 * SPG)
            for c in range(AHEAD):
                hi(0, c, first=True)
            h_hi(ADA_1 - 1)

            def first_half(n, part, jj, free, place):
                for c in range(AHEAD, AHEAD + SPH - 1):
                    hi(n * SPH, c)
                acc_copy(jj + ADA_1, part)
                if free is not None:
                    act.wait_ge(part_free, free)
                for b in range(BLK):
                    bank_ready(n, b, n * SPH + SPH)
                    row, few = place(b)
                    fn(row, M[:, b, 0:TP], ACT.Copy)
                    fn(few, MS[:, b], ACT.Copy).then_inc(bank_free, 1)
                hi(n * SPH, AHEAD + SPH - 1)

            with act.Fori(0, 2) as jj:
                for part in range(2):
                    first_half(2 * jj + part, part, jj, 2 * jj + part + 1,
                               lambda b: (PART_B[:, b, 0:TP], PART_BS[:, b, :, 3:]))
                h_hi(jj + ADA_1)
            with act.Fori(2, 4) as jj:
                first_half(2 * jj, 0, jj, jj + 3, lambda b: (PART_C[:, b, 0:TP], PART_CS[:, b, :, 1:]))
                first_half(2 * jj + 1, 1, jj, None,
                           lambda b: (SG[:, 4 * jj - 8 + b, 0:TP], SGS[:, 4 * jj - 8 + b, :, 1:]))
                h_hi(jj + ADA_1)

            with act.Fori(0, N_U) as g:
                for c in range(AHEAD, AHEAD + SPH):
                    hi(SLAB_U + g * SPH, c)
            def tables(par, tile):
                act.wait_ge(frac_done, tile + 1)
                then(fn(TCOS[par][:], TSIN[par][:], ACT.Sin, scale=TWO_PI / 2))
                then(fn(TCOS[par][:], TCOS[par][:], ACT.Square))
                fn(TCOS[par][:], TCOS[par][:], ACT.Copy, scale=-2.0, bias=1.0)
                fn(TSIN[par][:], TSIN[par][:], ACT.Sin, scale=TWO_PI).then_inc(table_done, 1)

            tables(0, 0)
            act.wait_ge(bank_free, 4 * (Q_U + N_U) + 4)
            act.wait_ge(sg_cleared, 1)
            with act.Fori(0, 2) as h:
                st.enter(h, 32)
                for m in range(4):
                    u = 4 * h + m
                    nb = SLAB_A + u * SPG
                    q = Q_A + u
                    for c in range(AHEAD, AHEAD + SPG):
                        if c == 3:
                            act.wait_ge(bu_done, 4 * u + 1)
                            fn(UU_HI[:], CST[:, u, :], ACT.Copy)
                            fn(BBU_HI[:], BB[:, u], ACT.Copy).then_inc(bbu_hi_done, 1)
                        hi(nb, c)
                        if c == 5:
                            act.wait_ge(cc_in, 16 * (u + 1))
                            fn(CC[:, 1], CC[:, 1], ACT.Copy, scale=-1.0).then_inc(cc_ready, 1)
                        if c in (3, 6, 9, 12):
                            j = c // 3 - 1
                            act.wait_ge(q_done, 4 * u + j + 1)
                            fn(COEF[:], MASK[:], ACT.Copy, scale=MAGF[:, 0, bass.ds(4 * u + j, 1)]).then_inc(
                                coef_done, 1)
                        if m == 3 and c == 5:
                            act.wait_ge(y_sum, 4 * h + 3 + 1)
                            act.sem_inc(act_passed, 1)
                            rows = CST[:, bass.ds(4 * h, 3), :]
                            fn(rows, rows, ACT.Gelu_apprx_tanh)
                            rows = SG[:, bass.ds(4 * h, 4), :]
                            fn(rows, rows, ACT.Silu).then_inc(silu_done, 1)
                        if c in (6, 9, 12, 15):
                            j = c // 3 - 2
                            tables((j + 1) % 2, 4 * u + j + 1)
                    for b in range(BLK):
                        if b == 0 and m == 0:
                            act.wait_ge(pada_ready, h + 1)
                        if b == 0 and m == 2:
                            act.wait_ge(conva_done, h + 1)
                            act.wait_ge(staged_a, h + 1)
                        if b == 0 and m == 3:
                            act.wait_ge(ab_done, h + 1)
                        bank_ready(q, b, nb + SPG)
                        if m == 0:
                            fn(PADA[:, b, 2:2 + TP], M[:, b, 0:TP], ACT.Copy)
                            fn(PADAS[:, b, :, 2:], MS[:, b], ACT.Copy).then_inc(bank_free, 1)
                        elif m == 1:
                            fn(AROW[:, 4 * h + b, :], M[:, b, 0:T], ACT.Copy).then_inc(bank_free, 1)
                        else:
                            fn(TMPA[:, b, :], M[:, b, 0:T], ACT.Copy).then_inc(bank_free, 1)
                act.wait_ge(bank_free, 4 * (Q_A + 4 * h + 3) + 8)
                fn(TMPA[:], TMPA[:], ACT.Silu).then_inc(silu_a_done, 1)
            st.leave(2)

            act.wait_ge(silu_done, 2)
            for i in range(4):
                if i in (1, 3):
                    if i == 3:
                        act.wait_ge(y_sum, 8 + 1)
                    r = 2 * i + 1
                    fn(CST[:, r, :], CST[:, r, :], ACT.Gelu_apprx_tanh).then_inc(gelu_done, 1)
                    if i == 3:
                        act.wait_ge(frac_done, 34)
                    act.wait_ge(gelu_done, (i + 1) // 2)
                fn(Y_HI[:, 2 * i:2 * i + 2, :], CST[:, 2 * i:2 * i + 2, :], ACT.Copy).then_inc(y_hi_done, 1)
            for c in range(AHEAD, AHEAD + 2 * SPGG):
                hi(SLAB_G, c)
                if c in (6, 10):
                    g = (c - 6) // 4
                    for b in range(BLK):
                        if b == 0 and g == 0:
                            act.wait_ge(ag_done, 2 + 1)
                        if b == 0 and g == 1:
                            act.wait_ge(z_used, 1)
                        bank_ready(Q_G + g, b, SLAB_G + 4 * (g + 1))
                        n = 4 * g + b
                        fn(ZG[:, b, :], M[:, b, 0:SW], ACT.Sigmoid, bias=PAR[:, C_BGLU + n:C_BGLU + n + 1]).then_inc(
                            bank_free, 1)

            def rows_out(i, pr):
                act.wait_ge(hs_done, 2 * i + pr + 1)
                for hd in range(2):
                    n = 4 * i + 2 * pr + hd
                    fn(BROW[:, n, 0:TP], R[:, hd, 0:TP], ACT.Copy)
                    last = fn(BROWS[:, n], R[:, hd, TP:XW].rearrange("p (s w) -> p s w", w=DS + 3)[:, :, 3:], ACT.Copy)
                last.then_inc(hs_out, 1)

            def mix_hi(i):
                act.wait_ge(slab_done, min(SLAB_O - SPG + 2 * i + 2, SLAB_O) + 1)
                if i == 0:
                    act.wait_ge(c_done, 1)
                if i == 7:
                    act.wait_ge(bg_done, 4 + 1)
                dst = H_HI[:, 4 * i:4 * i + 4, :]
                if i < 2:
                    fn(dst[:, :, 0:TP], CST[:, 4 * i:4 * i + 4, 0:TP], ACT.Copy)
                    fn(dst[:, :, TP:T].rearrange("p n (s w) -> p n s w", w=DS), CSTS[:, 4 * i:4 * i + 4, :, 1:],
                       ACT.Copy).then_inc(mix_hi_done, 1)
                else:
                    src = AROW[:, 4 * i - 8:4 * i - 4, :] if i < 4 else BROW[:, 4 * i - 16:4 * i - 12, :]
                    fn(dst, src, ACT.Copy).then_inc(mix_hi_done, 1)

            def part_b(i, last_group):
                for g in range(2):
                    nb = SLAB_B + i * SPB + g * SPH
                    q = Q_B + 2 * i + g
                    for c in range(AHEAD, AHEAD + (SPG if g else SPH)):
                        hi(nb, c)
                        if last_group and g == 1 and c in MIX_AT:
                            mix_hi(MIX_AT.index(c))
                        if g == 1 and c in (9, 15):
                            pr = c // 15
                            act.wait_ge(gates_done, 2 * i + pr + 1 + 1)
                            act.wait_ge(hs_out, 2 * i + pr + 1)
                            act.wait_ge(lru_staged, 2 * i + pr + 1)
                            for w, buf, col in ((0, R, C_BRG), (1, IG, C_BIG)):
                                for hd in range(2):
                                    last = fn(buf[:, hd, :], A0[2 * w + hd][:, 0:XW], ACT.Sigmoid,
                                              bias=PAR[:, bass.ds(col + 4 * i + 2 * pr + hd, 1)])
                            last.then_inc(gates_used, 1)
                            act.wait_ge(gates_used, 2 * i + pr + 1 + 1)
                            for hd in range(2):
                                n8 = NEG8SP[:, bass.ds(4 * i + 2 * pr + hd, 1)]
                                fn(AA[:, hd, :], R[:, hd, :], ACT.Exp, scale=n8)
                                last = fn(TH[:, hd, :], R[:, hd, :], ACT.Tanh, scale=n8)
                            last.then_inc(lru_act, 1)
                            act.wait_ge(lru_act, 4 * i + 2 * pr + 1)
                            fn(R[:], AA[:], ACT.Square).then_inc(lru_act, 1)
                        if g == 1 and c in (12, 17):
                            pr = c // 17
                            act.wait_ge(root_in, 2 * i + pr + 1)
                            fn(TH[:], TH[:], ACT.Sqrt, scale=-1.0).then_inc(roots, 1)
                        if g == 1 and c == 14:
                            rows_out(i, 0)
                for b in range(BLK):
                    if b == 0:
                        act.wait_ge(convb_staged, i + 1)
                        act.wait_ge(xb_ready, 2 * i + 2)
                    bank_ready(q, b, nb + SPG)
                    fn(SGB[:, b, :], M[:, b, 0:T], ACT.Copy).then_inc(bank_free, 1)
                act.wait_ge(bank_free, 4 * q + 8)
                fn(SGB[:], SGB[:], ACT.Silu).then_inc(silu_b_done, 1)
                rows_out(i, 1)

            with act.Fori(0, 3) as i:
                part_b(i, False)
            part_b(3, True)

            for i in range(4, 8):
                mix_hi(i)

            def group_o(j, last_group):
                nb = SLAB_O + j * SPG
                for c in range(AHEAD, SPG if last_group else AHEAD + SPG):
                    hi(nb, c)
                    if c == 15:
                        act.wait_ge(gate_used, 16 * (j + 1))
                        fn(ACC2[:], A0[0][:], ACT.Copy).then_inc(gacc_out, 1)
                for b in range(BLK):
                    if b == 0:
                        act.wait_ge(res_done, j + 1)
                    bank_ready(Q_O + j, b, nb + SPG)
                    fn(OT[:, b, :], M[:, b, 0:T], ACT.Copy).then_inc(bank_free, 1)
                act.wait_ge(res_done, j + 1 + 1)
                for b in range(BLK):
                    act.wait_ge(ysq_used, 4 * j + max(b - 1, 0) + 1)
                    fn(SQO[:, b % 2, :], X[:, 4 * j + b, :], ACT.Square).then_inc(ysq_done, 1)

            with act.Fori(0, N_O - 1) as j:
                group_o(j, False)
            group_o(N_O - 1, True)
            act.wait_ge(pe_tail, 1)
            fn(RST2[:], A0[2][:, 0:T], ACT.Sqrt, scale=1.0 / D, bias=EPSC[:]).then_inc(yroot, 1)
            for g in range(FIN_DVE, ADA_J):
                for b in range(BLK):
                    k = 4 * g + b
                    act.wait_ge(fin_pool, k - 4 * FIN_DVE + 1)
                    last = fn(X[:, k, :], X[:, k, :], ACT.Copy, scale=PAR[:, C_GF + k:C_GF + k + 1])
                last.then_inc(fin_act, 1)

        @block.vector
        def _(dve):
            tt, ts, stt = nc.vector.tensor_tensor, nc.vector.tensor_scalar, nc.vector.scalar_tensor_tensor
            st = dve_step
            MUL, ADD, SUB = ALU.mult, ALU.add, ALU.subtract

            def then(ins):
                st.up(ins)
                dve.wait_ge(st.sem, st.now())

            def lo(nb, c):
                dve.wait_ge(w_hi_done, nb + c + 1)
                tt(W_LO[:, c % RING], RAW[:, c % RING].rearrange("p (k n) -> p k n", k=2),
                   W_HI[:, c % RING].bitcast(F32), SUB).then_inc(w_lo_done, 1)

            def col(c):
                return PAR[:, bass.ds(c, 1)] if not isinstance(c, int) else PAR[:, c:c + 1]

            def bias9(c):
                return PAR[:, bass.ds(c, BLK)].unsqueeze(2).to_broadcast([P, BLK, 9])

            nc.vector.memset(EPSC[:], EPS).then_inc(s5_dve, 1)
            for b in range(BLK):
                nc.vector.memset(M[:, b, :], 0.0).then_inc(bank_free, 1)
            for i in range(8):
                dve.wait_ge(sq_done, i + 1)
                if i == 0:
                    ins = nc.vector.tensor_copy(SQA[:], SQ[:, 0, :])
                else:
                    dve.wait_ge(sqa_done, i)
                    ins = tt(SQA[:], SQA[:], SQ[:, i % 2, :], ADD)
                ins.then_inc(sqa_done, 1)

            RE, IM, DT, B_RE, B_IM, ANG, MAG, SIN, COS, U1, U2, U3, FR, FI = T0
            w = slice(0, 8 * P)
            dve.wait_ge(s5_act, 1)
            tt(ANG[:], IM[:], DT[:], MUL)
            tt(MAG[:], RE[:], DT[:], MUL).then_inc(s5_dve, 1)
            dve.wait_ge(small_in, 16 * 6)
            lam = PAR[:, C_LAM:C_LAM + 16]
            then(ts(SPT[:, 0], lam, -1.0, None, MUL))
            then(tt(SPT[:, 1], SPT[:, 0], lam, ALU.max))
            ts(NEG8SP[:], SPT[:, 1], -1.0, None, MUL).then_inc(s5_dve, 1)
            then(ts(U1[:], ANG[:], 1.0 / TWO_PI, ROUND, MUL, ADD))
            then(ts(U1[:], U1[:], -ROUND, None, ADD))
            for part in (PI_1, PI_2, PI_3):
                then(stt(ANG[:], U1[:], -part, ANG[:], MUL, ADD))
            ts(ANG[:], ANG[:], NEAR_PI, -NEAR_PI, ALU.min, ALU.max).then_inc(s5_dve, 1)
            dve.wait_ge(s5_act, 3)
            then(ts(SPT[:, 1], NEG8SP[:], 2.0, None, ADD))
            then(nc.vector.reciprocal(SPT[:, 1], SPT[:, 1]))
            then(tt(SPT[:, 1], SPT[:, 1], NEG8SP[:], MUL))
            then(tt(SPT[:, 2], SPT[:, 1], SPT[:, 1], MUL))
            then(ts(SPT[:, 3], SPT[:, 2], 1.0 / 17, None, MUL))
            for n in (15, 13, 11, 9, 7, 5, 3):
                then(stt(SPT[:, 3], SPT[:, 3], 1.0 / n, SPT[:, 2], ADD, MUL))
            then(stt(SPT[:, 3], SPT[:, 3], 1.0, SPT[:, 1], ADD, MUL))
            then(ts(SPT[:, 0], SPT[:, 0], 0.0, -8.0, ALU.max, MUL))
            then(stt(NEG8SP[:], SPT[:, 3], -16.0, SPT[:, 0], MUL, ADD))
            dve.wait_ge(root_done, 1)
            nc.vector.reciprocal(RSTD[:], RSTD[:]).then_inc(rstd_done, 1)
            ts(MAGF[:, 1, :], ANG[:, 8 * P:REP], 1.0 / TWO_PI, None, MUL)
            ts(MAGF[:, 0, :], MAG[:, 8 * P:REP], 1.0, None, MUL)
            dve.wait_ge(s5_act, 5)
            then(tt(COS[:, w], COS[:, w], COS[:, w], MUL))
            then(ts(COS[:, w], COS[:, w], -2.0, 1.0, MUL, ADD))
            tt(SIN[:, w], SIN[:, w], MAG[:, w], MUL)
            then(tt(COS[:, w], COS[:, w], MAG[:, w], MUL))
            tt(U1[:, w], RE[:, w], RE[:, w], MUL)
            tt(U2[:, w], IM[:, w], IM[:, w], MUL)
            then(ts(COS[:, w], COS[:, w], -1.0, None, ADD))
            then(tt(U1[:, w], U1[:, w], U2[:, w], ADD))
            nc.vector.reciprocal(U1[:, w], U1[:, w])
            tt(FR[:, w], COS[:, w], RE[:, w], MUL)
            then(tt(U2[:, w], SIN[:, w], IM[:, w], MUL))
            then(tt(FR[:, w], FR[:, w], U2[:, w], ADD))
            tt(FI[:, w], SIN[:, w], RE[:, w], MUL)
            then(tt(U2[:, w], COS[:, w], IM[:, w], MUL))
            then(tt(FI[:, w], FI[:, w], U2[:, w], SUB))
            tt(FR[:, w], FR[:, w], U1[:, w], MUL)
            then(tt(FI[:, w], FI[:, w], U1[:, w], MUL))

            def by_unit(t):
                return t[:, w].rearrange("p (u n) -> p u n", n=P)

            tt(U1[:, w], FR[:, w], B_RE[:, w], MUL)
            then(tt(U2[:, w], FI[:, w], B_IM[:, w], MUL))
            tt(BB[:, :, 0, :], by_unit(U1), by_unit(U2), SUB)
            tt(U3[:, w], FR[:, w], B_IM[:, w], MUL)
            then(tt(MAG[:, w], FI[:, w], B_RE[:, w], MUL))
            tt(BB[:, :, 1, :], by_unit(U3), by_unit(MAG), ADD).then_inc(bb_ready, 1)
            dve.wait_ge(bb_ready, 1)
            dve.wait_ge(rstd_done, 1)

            def h_tmp(j):
                dve.wait_ge(h_lo_done, j + 1)
                dve.wait_ge(sel_done, 2 * j + 1 + 1)
                tt(MOD[:, 0], A0[2][:, 0:36].rearrange("p (b n) -> p b n", n=9), bias9(C_BADA + 4 * j), ADD)
                dve.wait_ge(h_hi_done, j + 1)
                for kk in range(BLK):
                    ins = stt(HT[:, kk, :], X[:, 4 * j + kk, :], col(C_G + 4 * j + kk), RSTD[:], MUL, MUL)
                then(ins)

            def h_rows(j):
                dve.wait_ge(sel_done, 2 * j + 2 + 1)
                then(stt(MOD[:, 1], A0[3][:, 0:36].rearrange("p (b n) -> p b n", n=9), 1.0,
                         bias9(C_BADA + 32 + 4 * j), ADD, ADD))
                for kk in range(BLK):
                    ts(HT[:, kk, 0:TP], HT[:, kk, 0:TP], MOD[:, 1, kk, 0:1], MOD[:, 0, kk, 0:1], MUL, ADD)
                then(tt(HTS[:], HTS[:], MOD[:, 1, :, 1:9].unsqueeze(3).to_broadcast([P, BLK, DB, DS]), MUL))
                tt(HTS[:], HTS[:], MOD[:, 0, :, 1:9].unsqueeze(3).to_broadcast([P, BLK, DB, DS]), ADD).then_inc(
                    ht_done, 1)
                dve.wait_ge(h_hi_done, j + 1 + 1)
                tt(H_LO[:, bass.ds(4 * j, BLK), :], HT[:], H_HI[:, bass.ds(4 * j, BLK), :].bitcast(F32),
                   SUB).then_inc(h_lo_done, 1)

            with dve.Fori(0, ADA_1 - 1) as j:
                st.enter(j, 3)
                h_tmp(j)
                h_rows(j)
            st.leave(ADA_1 - 1)
            h_tmp(ADA_1 - 1)
            for c in range(AHEAD):
                lo(0, c)
            h_rows(ADA_1 - 1)

            with dve.Fori(0, ADA_J - ADA_1) as jj:
                st.enter(jj, 3)
                for c in range(AHEAD, AHEAD + 2 * SPH):
                    lo(2 * jj * SPH, c)
                    if c == AHEAD + SPH + 1:
                        h_tmp(jj + ADA_1)
                h_rows(jj + ADA_1)
            st.leave(ADA_J - ADA_1)

            def bank_ready(q, b, nb_next):
                if b < BLK - 1:
                    dve.wait_ge(bank_done, 3 * q + b + 1)
                else:
                    dve.wait_ge(slab_done, nb_next + 1)

            for part, (strip, samples) in enumerate(((CST, CSTS), (SG, SGS))):
                with dve.Fori(0, 2) as g:
                    nb = SLAB_U + (2 * part + g) * SPH
                    for c in range(AHEAD, AHEAD + SPH):
                        lo(nb, c)
                    for b in range(BLK):
                        if b == 0 and part == 0:
                            dve.wait_ge(part_c_in, 16 * (g + 1))
                        bank_ready(Q_U + 2 * part + g, b, nb + SPH)
                        row, few = strip[:, 4 * g + b, 0:TP], samples[:, 4 * g + b, :, 1:]
                        tt(row, row, M[:, b, 0:TP], ADD)
                        tt(few, few, MS[:, b], ADD).then_inc(bank_free, 1)

            def freed(q, b):
                return 4 * q + b + 1 + BLK

            def turn(t, par):
                qr, qi = Q[par][:, 0, :], Q[par][:, 1, :]
                bu_re, bu_im = A0[0][:, 0:SW], A0[1][:, 0:SW]
                dve.wait_ge(bu_done, t + 1 + 1)
                dve.wait_ge(table_done, t + 1)
                tt(qr, bu_re, TCOS[par][:], MUL)
                tt(qi, bu_im, TCOS[par][:], MUL)
                then(tt(TMPD[:], bu_im, TSIN[par][:], MUL))
                then(tt(qr, qr, TMPD[:], ADD))
                tt(TMPD[:], bu_re, TSIN[par][:], MUL).then_inc(bu_used, 1)
                dve.wait_ge(bu_used, t + 1 + 1)
                then(tt(qi, qi, TMPD[:], SUB))
                then(nc.vector.tensor_copy(Q[par][:, :, TP:SW:DS + 1], S5H0[:, t, :, :]))
                dve.wait_ge(coef_done, t + 1)
                nc.vector.tensor_tensor_scan(qr, COEF[:], qr, 0.0, MUL, ADD)
                nc.vector.tensor_tensor_scan(qi, COEF[:], qi, 0.0, MUL, ADD).then_inc(q_done, 1)

            def conv_a(h, b):
                n = 4 * h + b
                dve.wait_ge(bank_free, freed(Q_A + 4 * h + 1, b))
                tt(PADA[:, b, 2:2 + TP], PADA[:, b, 2:2 + TP], AROW[:, n, 0:TP], MUL)
                then(tt(PADAS[:, b, :, 2:], PADAS[:, b, :, 2:], AROWS[:, n], MUL))
                ts(AROW[:, n, 0:TP], PADA[:, b, 0:TP], col(C_WCA + n), col(C_BCA + n), MUL, ADD)
                then(ts(AROWS[:, n], PADAS[:, b, :, 0:DS], col(C_WCA + n), col(C_BCA + n), MUL, ADD))
                for k in (1, 2):
                    stt(AROW[:, n, 0:TP], PADA[:, b, k:k + TP], col(C_WCA + 8 * k + n), AROW[:, n, 0:TP], MUL, ADD)
                    ins = stt(AROWS[:, n], PADAS[:, b, :, k:k + DS], col(C_WCA + 8 * k + n), AROWS[:, n], MUL, ADD)
                    if k == 1:
                        then(ins)
                if b == BLK - 1:
                    ins.then_inc(conva_done, 1)
                else:
                    then(ins)

            with dve.Fori(0, 2) as h:
                st.enter(h, 16 * 4 + 4 * 4 - 1)
                dve.wait_ge(pada_ready, h + 1)
                for m in range(4):
                    u = 4 * h + m
                    nb = SLAB_A + u * SPG
                    for c in range(AHEAD, AHEAD + SPG):
                        if c == 3:
                            dve.wait_ge(bbu_hi_done, u + 1)
                            tt(UU_LO[:], CST[:, u, :], UU_HI[:].bitcast(F32), SUB)
                            tt(BBU_LO[:], BB[:, u], BBU_HI[:].bitcast(F32), SUB).then_inc(bbu_ready, 1)
                        lo(nb, c)
                        if m == 2 and c in (4, 8, 11, 14):
                            conv_a(h, c // 3 - 1)
                        if c in (5, 7, 10, 13):
                            turn(4 * u + c // 3 - 1, (c // 3 - 1) % 2)
                        if m == 3 and c == 4:
                            dve.wait_ge(conva_done, h + 1)
                            dve.wait_ge(bank_free, freed(Q_A + 4 * h + 2, 3))
                            rows = AROW[:, bass.ds(4 * h, BLK), :]
                            tt(rows, rows, TMPA[:], MUL).then_inc(ab_done, 1)
                    dve.wait_ge(y_done, 2 * u + 2 + 1)
                    stt(CST[:, u, :], CST[:, u, :], col(C_S5D + u), A0[2][:, 0:SW], MUL, ADD).then_inc(y_sum, 1)
                    if m == 3:
                        dve.wait_ge(ab_done, h + 1)
                        dve.wait_ge(silu_a_done, h + 1)
                        rows = AROW[:, bass.ds(4 * h, BLK), :]
                        tt(rows, rows, TMPA[:], MUL).then_inc(ag_done, 1)
            st.leave(2)

            dve.wait_ge(staged_s, 8)
            dve.wait_ge(frac_done, 34)
            for i in range(4):
                dve.wait_ge(y_hi_done, i + 1)
                tt(Y_LO[:, 2 * i:2 * i + 2, :], CST[:, 2 * i:2 * i + 2, :], Y_HI[:, 2 * i:2 * i + 2, :].bitcast(F32),
                   SUB).then_inc(y_lo_done, 1)
            for c in range(AHEAD, AHEAD + 2 * SPGG):
                lo(SLAB_G, c)
                if c in (6, 10):
                    g = (c - 6) // 4
                    if g == 0:
                        dve.wait_ge(silu_done, 2)
                    dve.wait_ge(bank_free, freed(Q_G + g, 3))
                    tt(SG[:, 4 * g:4 * g + 4, :], SG[:, 4 * g:4 * g + 4, :], ZG[:], MUL).then_inc(z_used, 1)
            dve.wait_ge(z_used, 2)
            tt(CST[:], CST[:], SG[:], MUL).then_inc(c_done, 1)

            def conv_b(i, hd):
                n = 4 * i + hd
                ins = ts(XB[:, hd, :], PADB[:, hd, 0:XW], col(C_WCB + n), col(C_BCB + n), MUL, ADD)
                for k in (1, 2, 3):
                    then(ins)
                    ins = stt(XB[:, hd, :], PADB[:, hd, k:k + XW], col(C_WCB + 16 * k + n), XB[:, hd, :], MUL, ADD)
                return ins

            def lru(i, pr):
                dve.wait_ge(roots, 2 * i + pr + 1)
                nc.vector.memset(AA[:, :, TP + 2:XW - DS:DS + 3], 0.0)
                then(tt(TH[:], TH[:], IG[:], MUL))
                then(tt(TH[:], TH[:], XB[:, 2 * pr:2 * pr + 2, :], MUL))
                then(nc.vector.tensor_copy(TH[:, :, TP + 2:XW - DS:DS + 3],
                                           LRU0[:, bass.ds(4 * i + 2 * pr, 2), :]))
                for hd in range(2):
                    last = nc.vector.tensor_tensor_scan(R[:, hd, :], AA[:, hd, :], TH[:, hd, :], 0.0, MUL, ADD)
                last.then_inc(hs_done, 1)

            def mix_lo(i):
                dve.wait_ge(mix_hi_done, i + 1)
                dst, hi_ = H_LO[:, 4 * i:4 * i + 4, :], H_HI[:, 4 * i:4 * i + 4, :].bitcast(F32)
                if i < 2:
                    tt(dst[:, :, 0:TP], CST[:, 4 * i:4 * i + 4, 0:TP], hi_[:, :, 0:TP], SUB)
                    tt(dst[:, :, TP:T].rearrange("p n (s w) -> p n s w", w=DS), CSTS[:, 4 * i:4 * i + 4, :, 1:],
                       hi_[:, :, TP:T].rearrange("p n (s w) -> p n s w", w=DS), SUB).then_inc(mix_lo_done, 1)
                else:
                    src = AROW[:, 4 * i - 8:4 * i - 4, :] if i < 4 else BROW[:, 4 * i - 16:4 * i - 12, :]
                    tt(dst, src, hi_, SUB).then_inc(mix_lo_done, 1)

            def part_b(i, last_group):
                for g in range(2):
                    nb = SLAB_B + i * SPB + g * SPH
                    for c in range(AHEAD, AHEAD + (SPG if g else SPH)):
                        lo(nb, c)
                        if last_group and g == 1 and c - 1 in MIX_AT:
                            mix_lo(MIX_AT.index(c - 1))
                        if g == 1 and c in (4, 8):
                            pr = c // 8
                            if pr == 0:
                                dve.wait_ge(gates_done, 2 * i + 1)
                                dve.wait_ge(bank_free, freed(Q_B + 2 * i, 3))
                            then(conv_b(i, 2 * pr))
                            conv_b(i, 2 * pr + 1).then_inc(xb_ready, 1)
                        if g == 1 and c in (11, 17):
                            pr = c // 17
                            dve.wait_ge(lru_act, 4 * i + 2 * pr + 2)
                            stt(TH[:], R[:], 1.0, TH[:], ADD, MUL).then_inc(root_in, 1)
                        if g == 1 and c == 13:
                            lru(i, 0)
                    if g == 0:
                        dve.wait_ge(padb_ready, i + 1)
                        for b in range(BLK):
                            bank_ready(Q_B + 2 * i, b, nb + SPH)
                            row, few = PADB[:, b, 3:3 + TP], PADBS[:, b, :, 3:]
                            tt(row, row, M[:, b, 0:TP], ADD)
                            tt(few, few, MS[:, b], ADD).then_inc(bank_free, 1)
                lru(i, 1)
                dve.wait_ge(hs_out, 2 * i + 2 + 1)
                dve.wait_ge(silu_b_done, i + 1)
                rows = BROW[:, bass.ds(4 * i, BLK), :]
                tt(rows, rows, SGB[:], MUL).then_inc(bg_done, 1)
            with dve.Fori(0, 3) as i:
                st.enter(i, 3 * 4 + 2 + 2 * 3)
                part_b(i, False)
            st.leave(3)
            part_b(3, True)

            for i in range(4, 8):
                mix_lo(i)
            then(nc.vector.memset(SQS[:], 0.0))

            def group_o(j, last_group):
                for c in range(AHEAD, SPG + (2 if last_group else AHEAD)):
                    if c < SPG or not last_group:
                        lo(SLAB_O + j * SPG, c)
                    if c == 16:
                        dve.wait_ge(gsel_done, j + 1)
                        tt(MOD[:, 2], A0[1][:, 0:36].rearrange("p (b n) -> p b n", n=9),
                           bias9(C_BADA + 64 + 4 * j), ADD).then_inc(gmod_done, 1)
                dve.wait_ge(gmod_done, j + 1 + 1)
                dve.wait_ge(x_back, 16 * (j + 1))
                dve.wait_ge(bank_free, freed(Q_O + j, 3))
                for b in range(BLK):
                    row = X[:, 4 * j + b, 0:TP]
                    stt(row, OT[:, b, 0:TP], MOD[:, 2, b, 0:1], row, MUL, ADD)
                then(tt(OTS[:], OTS[:], MOD[:, 2, :, 1:9].unsqueeze(3).to_broadcast([P, BLK, DB, DS]), MUL))
                rows = XS[:, bass.ds(4 * j, BLK)]
                tt(rows, rows, OTS[:], ADD).then_inc(res_done, 1)
                for b in range(BLK):
                    dve.wait_ge(ysq_done, 4 * j + b + 1)
                    dve.wait_ge(ysq_used, 4 * j + b + 1)
                    tt(SQS[:], SQS[:], SQO[:, b % 2, :], ADD).then_inc(ysq_used, 1)

            with dve.Fori(0, N_O - 1) as j:
                st.enter(j, 1)
                group_o(j, False)
            st.leave(N_O - 1)
            group_o(N_O - 1, True)
            dve.wait_ge(yroot, 1)
            nc.vector.reciprocal(RST2[:], RST2[:]).then_inc(rstd2_done, 1)
            dve.wait_ge(rstd2_done, 1)
            for g in range(FIN_DVE):
                for b in range(BLK):
                    k = 4 * g + b
                    last = stt(X[:, k, :], X[:, k, :], col(C_GF + k), RST2[:], MUL, MUL)
                    if k == 1:
                        last.then_inc(fin_dve, 1)
                last.then_inc(fin_dve, 1)

        @block.gpsimd
        def _(pool):
            tt, ts, copy = nc.gpsimd.tensor_tensor, nc.gpsimd.tensor_scalar, nc.gpsimd.tensor_copy
            st = pool_step
            MUL, ADD, SUB = ALU.mult, ALU.add, ALU.subtract

            def wait(sem_, value):
                pool.wait_ge(sem_, value)
                if not isinstance(value, int):
                    pool.sem_inc(pool_passed, 1)

            def then(ins):
                st.up(ins)
                wait(st.sem, st.now())

            def pad_a(h):
                nc.gpsimd.memset(PADA[:, :, 0:2], 0.0)
                copy(PADAS[:, :, :, 0:2], CAST[:, bass.ds(4 * h, BLK)]).then_inc(pada_ready, 1)

            def frac(t, par):
                sin, cos = TSIN[par][:], TCOS[par][:]
                then(copy(TURN[:], MAGF[:, 1, bass.ds(t, 1)]))
                then(ts(sin, STEP[:], TURN[:], 1.0, MUL, MUL))
                then(ts(cos, sin, 1.0, ROUND, MUL, ADD))
                then(ts(cos, cos, 1.0, -ROUND, MUL, ADD))
                tt(sin, sin, cos, SUB).then_inc(frac_done, 1)

            for start, count, step, buf, dst in ((0, 4, 1, PART_B, part_b), (4, 2, 2, PART_C, part_c)):
                with pool.Fori(0, count) as n:
                    nc.gpsimd.memset(buf[:], 0.0).then_inc(part_free, 1)
                    wait(bank_free, 4 * step * n + 4 * start + 8)
                    pool.dma_start(dst[n], buf[:]).then_inc(part_out, 16)
                    wait(part_out, 16 * n + 16 * start + 16)
            wait(h_lo_done, ADA_J + 1)
            wait(ada_used, 2 * ADA_J * SPG)
            for g in range(2):
                pool.dma_start(CST[:, 4 * g:4 * g + 4], part_c[g]).then_inc(part_c_in, 16)
                wait(part_c_in, 16 * (g + 1))
            nc.gpsimd.memset(SG[:, :, TP:SW:DS + 1], 0.0).then_inc(sg_cleared, 1)
            wait(bb_ready, 1)
            frac(0, 0)
            frac(1, 1)
            with pool.Fori(0, 2) as h:
                st.enter(h, 4 * (4 * 8 - 1))
                wait(ag_done, h + 1)
                pad_a(h)
                for m in range(4):
                    u = 4 * h + m
                    wait(y_done, 2 * u + 1)
                    pool.dma_start(CC[:], a["s5c"][u]).then_inc(cc_in, 16)
                    for j in range(4):
                        t = 4 * u + j
                        par = j % 2
                        qr, qi, cos, sin = Q[par][:, 0, :], Q[par][:, 1, :], TCOS[par][:], TSIN[par][:]
                        if m == 2 and j == 3:
                            wait(conva_done, h + 1)
                            copy(STG_A[:, :, :, 0], PADA[:, :, TP:PA:DS + 2])
                            copy(STG_A[:, :, :, 1], PADA[:, :, TP + 1:PA:DS + 2]).then_inc(staged_a, 1)
                        wait(q_done, t + 1 + 1)
                        wait(y_done, 2 * u + j // 2 + 1)
                        hr, hi = HRI[par][:, 0, :], HRI[par][:, 1, :]
                        tt(hr, qr, cos, MUL)
                        then(tt(TMPP[:], qi, sin, MUL))
                        then(tt(hr, hr, TMPP[:], SUB))
                        tt(hi, qr, sin, MUL)
                        then(tt(TMPP[:], qi, cos, MUL))
                        tt(hi, hi, TMPP[:], ADD).then_inc(hs5_done, 1)
                        wait(hs5_done, t + 1)
                        ins = copy(STG_S[:, j], HRI[par][:, :, TP - 1:SW:DS + 1])
                        if j < 3:
                            then(ins)
                        else:
                            ins.then_inc(staged_s, 1)
                        frac(t + 2, par)
                    wait(staged_s, u + 1)
                    pool.dma_start(a["o_s5"][u], STG_S[:]).then_inc(out_s, 16)
                    wait(out_s, 16 * (u + 1))
                    if m == 2:
                        wait(staged_a, h + 1)
                        pool.dma_start(a["o_ca"][h], STG_A[:]).then_inc(out_a, 16)
                        wait(out_a, 16 * (h + 1))
            st.leave(2)

            wait(y_done, 16 + 1)
            pool.dma_start(CT[:], a["c"]).then_inc(c_back, 16)
            pool.dma_start(CBST[:], a["cb"]).then_inc(cb_in, 16)
            wait(cb_in, 16)
            wait(slab_done, SLAB_B + 1)
            with pool.Fori(0, 4) as i:
                wait(bg_done, i + 1)
                pool.dma_start(PADB[:, :, 3:PB], part_b[i]).then_inc(part_b_in, 16)
                wait(part_b_in, 16 * (i + 1))
                nc.gpsimd.memset(PADB[:, :, 0:3], 0.0)
                copy(PADBS[:, :, :, 0:3], CBST[:, bass.ds(4 * i, BLK)]).then_inc(padb_ready, 1)
                wait(gates_done, 2 * i + 1)
                pool.dma_start(WG[:], a["wg"][i]).then_inc(wg_in, 16)
                wait(bank_free, 4 * (Q_B + 2 * i) + 8)
                copy(STG_B[:, :, :, 0], PADB[:, :, TP:PB:DS + 3])
                copy(STG_B[:, :, :, 1], PADB[:, :, TP + 1:PB:DS + 3])
                copy(STG_B[:, :, :, 2], PADB[:, :, TP + 2:PB:DS + 3]).then_inc(convb_staged, 1)
                wait(convb_staged, i + 1)
                pool.dma_start(a["o_cb"][i], STG_B[:]).then_inc(out_b, 16)
                for pr in range(2):
                    wait(hs_done, 2 * i + pr + 1)
                    copy(STG_H[:, 2 * pr:2 * pr + 2, :], R[:, :, TP - 1:XW:DS + 3]).then_inc(lru_staged, 1)
                wait(lru_staged, 2 * i + 2 + 1)
                pool.dma_start(a["o_lru"][i], STG_H[:]).then_inc(out_b, 16)
                wait(out_b, 32 * (i + 1))

            wait(mix_lo_done, 8)
            for g in range(8):
                wait(slab_done, SLAB_O + 6 + 10 * g + 1)
                pool.dma_start(X[:, 4 * g:4 * g + 4, :], a["x"][:, 4 * g:4 * g + 4, :]).then_inc(x_back, 16)
                wait(x_back, 16 * (g + 1))
            wait(rstd2_done, 1)
            for k in range(4 * FIN_DVE, KT):
                tt(X[:, k, :], X[:, k, :], RST2[:], MUL).then_inc(fin_pool, 1)


def layouts():
    a0, b0, c0 = 0, 4 * W_A, 4 * W_A + 2 * W_B
    starts = [c0, c0 + COLS, c0 + W_C, c0 + W_C + COLS]
    for h in range(2):
        starts += [a0 + s * W_A + COLS * h for s in (1, 2, 0, 3)]
    for i in range(4):
        starts += [b0 + COLS * i, b0 + W_B + COLS * i]
    rows = [W_A + W_B + P * n for n in range(8)] + [P * n for n in range(8)] + [W_A + P * n for n in range(16)]
    return starts, rows


def slabs(w, starts, rows):
    out = []
    for s in starts:
        blk = np.stack([w[r:r + P, s:s + COLS] for r in rows])
        out.append(blk.reshape(len(rows) // 2, 2, P, COLS).transpose(0, 2, 1, 3).reshape(-1, P, SLAB))
    return np.concatenate(out)


def channel_major(v):
    v = np.asarray(v)
    v = v.reshape(*v.shape[:-1], v.shape[-1] // P, P)
    return np.moveaxis(v, -1, 0)


_OUTS = {"y": (8, P, 4, T), "o_ca": (2, P, BLK, 9, 2), "o_cb": (4, P, BLK, 9, 3), "o_lru": (4, P, BLK, 9),
         "o_s5": (8, P, BLK, 2, 9)}


def kernel(**inputs):
    import concourse.bacc as bacc
    from concourse.bass_utils import run_bass_kernel_spmd

    x = {k: np.asarray(v) for k, v in inputs.items()}
    f32 = np.float32
    l = {k: v[0] for k, v in x.items() if v.shape[0] == 1 and k not in ("x_prompt", "c_prompt")}
    starts, rows = layouts()
    kt = [P * k for k in range(KT)]
    lower, upper = kt[:KT // 2], kt[KT // 2:]
    b_x, b_g = starts[12::2], starts[13::2]
    w = np.concatenate([
        slabs(l["w_in"], b_x + [starts[g] for g in (0, 2, 1, 3)], lower), slabs(l["w_in"], starts[:4], upper),
        slabs(l["w_in"], starts[4:12], kt), slabs(l["w_glu"], [0, COLS], kt[:8]),
        *(part for i in range(4) for part in (slabs(l["w_in"], [b_x[i]], upper), slabs(l["w_in"], [b_g[i]], kt))),
        slabs(l["w_out"], [COLS * j for j in range(8)], rows)])
    assert len(w) == SLABS
    order = [c for j in range(8) for c in (COLS * j, D + COLS * j)] + [2 * D + COLS * j for j in range(8)]
    ada = slabs(l["w_ada"], order, kt)
    tok = np.concatenate([x["x_prompt"][0], x["x_sample"].reshape(DB * DS, D)])
    xT = channel_major(tok).transpose(0, 2, 1)
    cT = np.zeros((P, KT, 32), f32)
    cT[:, :, 0:9] = channel_major(np.concatenate([x["c_prompt"], x["c_sample"]])).transpose(0, 2, 1)
    par = np.concatenate([channel_major(l[k].reshape(-1)) for k in (
        "b_ada", "g_norm", "w_conv_a", "b_conv_a", "w_conv_b", "b_conv_b", "b_rg", "b_ig", "lru_lambda", "b_glu",
        "s5_d")] + [channel_major(x["g_final"])], axis=1)
    assert par.shape[1] == N_PAR
    sel_ones = np.zeros((P, 9 + P), f32)
    for b in range(9):
        sel_ones[b::32, b] = 1
    sel_ones[:, 9:] = 1
    mask, step = np.ones(SW, f32), np.zeros(SW, f32)
    mask[TP::DS + 1] = 0
    step[0:TP] = np.arange(1, TP + 1)
    for b in range(DB):
        step[TP + 9 * b + 1:TP + 9 * b + 9] = np.arange(1, DS + 1)
    mask, step = (np.ascontiguousarray(np.broadcast_to(v, (P, SW))) for v in (mask, step))
    log_dt = np.broadcast_to(l["s5_log_dt"][:, None], (64, S5_P))
    rep = np.zeros((P, 3, REP), f32)
    for n, v in enumerate((l["s5_lambda_re"], l["s5_lambda_im"], log_dt)):
        by = v.reshape(8, 4, P)
        rep[:, n, 0:8 * P] = np.repeat(by.transpose(1, 0, 2).reshape(4, 8 * P), 32, axis=0)
        rep[:, n, 8 * P:8 * P + NST] = v.reshape(NST, P).T
    s5b = np.zeros((4, 2, S5_I, 2, 8, 2, S5_P), f32)
    s5c = np.zeros((8, 2, S5_P, 2, 4, 2, S5_I), f32)
    for n, (b_, c_) in enumerate((("s5_b_re", "s5_c_re"), ("s5_b_im", "s5_c_im"))):
        bv = l[b_].reshape(8, 4, 2, S5_P, S5_I)
        cv = l[c_].reshape(8, 4, 2, S5_I, S5_P)
        for g in range(2):
            s5b[:, g, :, n, :, g, :] = bv[:, :, g].transpose(1, 3, 0, 2)
            s5c[:, g, :, n, :, g, :] = cv[:, :, g].transpose(0, 3, 1, 2)
    s5h0 = np.stack([l["state_s5_re"].reshape(DB, NST, P), l["state_s5_im"].reshape(DB, NST, P)])
    wg = np.stack([l["w_rg"], l["w_ig"]]).reshape(2, 4, BLK, P, P)
    arrays = {
        "w": w, "ada": ada, "x": xT, "c": cT, "par": par, "sel_ones": sel_ones, "mask": mask, "step": step,
        "rep": rep, "s5b": s5b.reshape(P, 2, 8 * P), "s5c": s5c.reshape(8, P, 2, BLK, 32),
        "s5h0": s5h0.transpose(3, 2, 0, 1), "wg": wg.transpose(1, 3, 2, 0, 4),
        "cb": channel_major(l["state_conv_b"]).transpose(0, 3, 1, 2),
        "lru": channel_major(l["state_lru_h"]).transpose(0, 2, 1),
        "ca": channel_major(l["state_conv_a"]).transpose(0, 3, 1, 2),
    }
    arrays = {f"in_{k}": np.ascontiguousarray(v) for k, v in arrays.items()}
    nc = bacc.Bacc("TRN2", target_bir_lowering=False, num_devices=1)
    aps = {k[3:]: nc.dram_tensor(k, v.shape, mybir.dt.from_np(v.dtype), kind="ExternalInput").ap()
           for k, v in arrays.items()}
    for k, shape in _OUTS.items():
        aps[k] = nc.dram_tensor(f"out_{k}", shape, F32, kind="ExternalOutput").ap()
    build(nc, aps)
    r = run_bass_kernel_spmd(nc, [arrays], core_ids=[0]).results[0]
    y, ca, cb, lru, s5 = (np.asarray(r[f"out_{k}"]) for k in _OUTS)
    y = y.transpose(3, 0, 2, 1).reshape(T, D)
    ca = ca.transpose(3, 4, 0, 2, 1).reshape(9, 2, W_A)
    cb = cb.transpose(3, 4, 0, 2, 1).reshape(9, 3, W_B)
    lru = lru.transpose(3, 0, 2, 1).reshape(9, W_B)
    s5 = s5.transpose(3, 4, 0, 2, 1).reshape(2, 9, 64, S5_P)
    both = [ca, cb, lru, s5[0], s5[1]]
    c = np.ascontiguousarray
    return (c(y[None, 0:TP]), c(y[TP:].reshape(DB, DS, D)), *(c(v[None, 0:1]) for v in both),
            *(c(v[None, 1:9]) for v in both))
```
